# Optimizing a Trainium2 kernel written in Bass

```python
import math
import jax, jax.numpy as jnp
from jax import lax
import numpy as np

D_MODEL = 1024
BATCH = 1
SEQ = 256
DEPTH = 2

N_MIXERS = 2
N_GLA_LAYERS = (DEPTH + 1) // 2
N_SB_LAYERS = DEPTH // 2
D_FF = 2816
EPS = 1e-6

GLA_HEADS = 4
GLA_DK = D_MODEL // 2
GLA_DV = D_MODEL
GLA_HK = GLA_DK // GLA_HEADS
GLA_HV = GLA_DV // GLA_HEADS
GLA_GATE_RANK = 16
GLA_GATE_TAU = 16.0
GLA_CHUNK = 64
GLA_IN_COLS = GLA_DK + GLA_DK + GLA_DV + GLA_DV + GLA_GATE_RANK

SB_HEADS = 16
SB_HD = D_MODEL // SB_HEADS
SB_QBLOCK = 128
SB_IN_COLS = 3 * D_MODEL


def rmsnorm(x, g):
    xf = x.astype(jnp.float32)
    y = xf * lax.rsqrt(jnp.mean(xf * xf, axis=-1, keepdims=True) + EPS)
    return (y * g.astype(jnp.float32)).astype(x.dtype)

def swiglu(h, w_gate, w_up, w_down):
    return (jax.nn.silu(h @ w_gate) * (h @ w_up)) @ w_down

def gla_mixer(h, w_in, w_gk2, b_gk, o_norm, w_out):
    B, S, _ = h.shape
    nc = S // GLA_CHUNK
    proj = h @ w_in
    q, k, v, g, gk_lr = jnp.split(
        proj, [GLA_DK, 2 * GLA_DK, 2 * GLA_DK + GLA_DV, 2 * GLA_DK + 2 * GLA_DV], axis=-1)
    log_a = jax.nn.log_sigmoid((gk_lr @ w_gk2 + b_gk).astype(jnp.float32)) / GLA_GATE_TAU

    def to_chunks(t, d):
        return t.astype(jnp.float32).reshape(B, nc, GLA_CHUNK, GLA_HEADS, d).transpose(1, 0, 3, 2, 4)

    qc = to_chunks(q, GLA_HK) * (GLA_HK ** -0.5)
    kc = to_chunks(k, GLA_HK)
    vc = to_chunks(v, GLA_HV)
    bc = jnp.cumsum(to_chunks(log_a, GLA_HK), axis=3)
    causal = jnp.tril(jnp.ones((GLA_CHUNK, GLA_CHUNK), dtype=bool))

    def step(state, inp):
        q_t, k_t, v_t, b_t = inp
        o_inter = jnp.einsum('bhtk,bhkv->bhtv', q_t * jnp.exp(b_t), state)
        diff = b_t[:, :, :, None, :] - b_t[:, :, None, :, :]
        decay = jnp.exp(jnp.where(causal[:, :, None], diff, -jnp.inf))
        scores = jnp.einsum('bhtk,bhtsk,bhsk->bhts', q_t, decay, k_t)
        o_intra = jnp.einsum('bhts,bhsv->bhtv', scores, v_t)
        b_last = b_t[:, :, -1, :]
        k_dec = k_t * jnp.exp(b_last[:, :, None, :] - b_t)
        state = jnp.exp(b_last)[..., None] * state + jnp.einsum('bhsk,bhsv->bhkv', k_dec, v_t)
        return state, o_inter + o_intra

    state0 = jnp.zeros((B, GLA_HEADS, GLA_HK, GLA_HV), jnp.float32)
    _, o = lax.scan(step, state0, (qc, kc, vc, bc))
    o = o.transpose(1, 0, 3, 2, 4).reshape(B, S, GLA_HEADS, GLA_HV)
    o = rmsnorm(o, o_norm).reshape(B, S, GLA_DV)
    o = o.astype(h.dtype) * jax.nn.silu(g)
    return o @ w_out

def sb_mixer(h, w_in, w_out):
    B, S, _ = h.shape
    nb = S // SB_QBLOCK
    q, k, v = jnp.split(h @ w_in, 3, axis=-1)

    def heads(t):
        return t.reshape(B, S, SB_HEADS, SB_HD).transpose(0, 2, 1, 3)

    q, k, v = heads(q), heads(k), heads(v)
    q_blocks = q.reshape(B, SB_HEADS, nb, SB_QBLOCK, SB_HD).transpose(2, 0, 1, 3, 4)
    s_pos = jnp.arange(S)
    scale = 1.0 / math.sqrt(SB_HD)

    def block(args):
        idx, q_blk = args
        z = jnp.einsum('bhtd,bhsd->bhts', q_blk, k).astype(jnp.float32) * scale
        t_pos = idx * SB_QBLOCK + jnp.arange(SB_QBLOCK)
        mask = s_pos[None, :] < t_pos[:, None]
        sp = jnp.where(mask, jax.nn.softplus(z), 0.0)
        rem = lax.cumsum(sp, axis=3, reverse=True) - sp
        weights = jnp.where(mask, jnp.exp(jax.nn.log_sigmoid(z) - rem), 0.0)
        return jnp.einsum('bhts,bhsd->bhtd', weights.astype(v.dtype), v)

    o = lax.map(block, (jnp.arange(nb), q_blocks))
    o = o.transpose(1, 0, 3, 2, 4).reshape(B, S, D_MODEL)
    return o @ w_out

def first_inputs(seed: int = 0) -> dict:
    key = jax.random.key(seed)
    ks = jax.random.split(key, 24)
    f32 = jnp.float32

    def nrm(k, shape, fan_in, gain=1.0):
        return jax.random.normal(k, shape, f32) * (gain * fan_in ** -0.5)

    def gain(k, shape):
        return 1.0 + 0.02 * jax.random.normal(k, shape, f32)

    return {
        "x": jax.random.normal(ks[0], (BATCH, SEQ, D_MODEL), f32),
        "ffn1_norm": gain(ks[1], (DEPTH, D_MODEL)),
        "ffn1_w_gate": nrm(ks[2], (DEPTH, D_MODEL, D_FF), D_MODEL),
        "ffn1_w_up": nrm(ks[3], (DEPTH, D_MODEL, D_FF), D_MODEL),
        "ffn1_w_down": nrm(ks[4], (DEPTH, D_FF, D_MODEL), D_FF),
        "mix_norm": gain(ks[5], (DEPTH, D_MODEL)),
        "ffn2_norm": gain(ks[6], (DEPTH, D_MODEL)),
        "ffn2_w_gate": nrm(ks[7], (DEPTH, D_MODEL, D_FF), D_MODEL),
        "ffn2_w_up": nrm(ks[8], (DEPTH, D_MODEL, D_FF), D_MODEL),
        "ffn2_w_down": nrm(ks[9], (DEPTH, D_FF, D_MODEL), D_FF),
        "gla_w_in": nrm(ks[10], (N_GLA_LAYERS, D_MODEL, GLA_IN_COLS), D_MODEL),
        "gla_w_gk2": nrm(ks[11], (N_GLA_LAYERS, GLA_GATE_RANK, GLA_DK), GLA_GATE_RANK),
        "gla_b_gk": 0.1 * jax.random.normal(ks[12], (N_GLA_LAYERS, GLA_DK), f32),
        "gla_o_norm": gain(ks[13], (N_GLA_LAYERS, GLA_HV)),
        "gla_w_out": nrm(ks[14], (N_GLA_LAYERS, GLA_DV, D_MODEL), GLA_DV),
        "sb_w_in": nrm(ks[15], (N_SB_LAYERS, D_MODEL, SB_IN_COLS), D_MODEL),
        "sb_w_out": nrm(ks[16], (N_SB_LAYERS, D_MODEL, D_MODEL), D_MODEL),
        "final_norm": gain(ks[17], (D_MODEL,)),
    }

def first_block(x, ffn1_norm, ffn1_w_gate, ffn1_w_up, ffn1_w_down, mix_norm,
              ffn2_norm, ffn2_w_gate, ffn2_w_up, ffn2_w_down,
              gla_w_in, gla_w_gk2, gla_b_gk, gla_o_norm, gla_w_out,
              sb_w_in, sb_w_out, final_norm):
    for i in range(DEPTH):
        x = x + 0.5 * swiglu(rmsnorm(x, ffn1_norm[i]), ffn1_w_gate[i], ffn1_w_up[i], ffn1_w_down[i])
        h = rmsnorm(x, mix_norm[i])
        j = i // N_MIXERS
        if i % N_MIXERS == 0:
            y = gla_mixer(h, gla_w_in[j], gla_w_gk2[j], gla_b_gk[j], gla_o_norm[j], gla_w_out[j])
        else:
            y = sb_mixer(h, sb_w_in[j], sb_w_out[j])
        x = x + y.astype(x.dtype)
        x = x + 0.5 * swiglu(rmsnorm(x, ffn2_norm[i]), ffn2_w_gate[i], ffn2_w_up[i], ffn2_w_down[i])
    return rmsnorm(x, final_norm)


DEPTH_2 = 1

N_META = 16
NORM_EPS = 1e-6
SSM_WIDTH = D_MODEL // 2
SSM_GROUP = 16
SSM_GROUPS = SSM_WIDTH // SSM_GROUP
SSM_STATE = 64
ML_WIDTH = D_MODEL
ML_HEADS = 4
ML_HEAD_DIM = ML_WIDTH // ML_HEADS
ML_CHUNK = 64
ML_CONV = 4
ML_QKV_BLOCK = 4
PEER_HEADS = 8
PEER_NKEYS = 128
PEER_EXPERTS = PEER_NKEYS * PEER_NKEYS
PEER_TOPK = 16
PEER_QDIM = 256
PEER_HALF = PEER_QDIM // 2
PEER_TOKEN_BLOCK = 256
IN_COLS = SSM_WIDTH + 2 * ML_WIDTH + 2 * D_MODEL


def rmsnorm_2(x, g):
    x32 = x.astype(jnp.float32)
    y = x32 * lax.rsqrt(jnp.mean(x32 * x32, axis=-1, keepdims=True) + NORM_EPS)
    return (y * g.astype(jnp.float32)).astype(x.dtype)

def s5_branch(u, a_re, a_im, log_dt, b_re, b_im, c_re, c_im, d, w_glu, b_glu):
    f32 = jnp.float32
    bn, L, _ = u.shape
    u32 = u.astype(f32).reshape(bn, L, SSM_GROUPS, SSM_GROUP)
    lam = lax.complex(a_re.astype(f32), a_im.astype(f32))
    dt = jnp.exp(log_dt.astype(f32))[:, None]
    a_bar = jnp.exp(lam * dt)
    b_bar = ((a_bar - 1.0) / lam)[..., None] * lax.complex(b_re.astype(f32), b_im.astype(f32))
    bu = jnp.einsum('blgc,gpc->blgp', u32.astype(jnp.complex64), b_bar)
    a_seq = jnp.broadcast_to(a_bar, (1, L) + a_bar.shape)

    def combine(e1, e2):
        a1, b1 = e1
        a2, b2 = e2
        return a1 * a2, a2 * b1 + b2

    _, states = lax.associative_scan(combine, (a_seq, bu), axis=1)
    c = lax.complex(c_re.astype(f32), c_im.astype(f32))
    y = jnp.real(jnp.einsum('blgp,gcp->blgc', states, c)) + d.astype(f32).reshape(SSM_GROUPS, SSM_GROUP) * u32
    y = jax.nn.gelu(y.reshape(bn, L, SSM_WIDTH))
    y = y * jax.nn.sigmoid(y @ w_glu.astype(f32) + b_glu.astype(f32))
    return y.astype(u.dtype)

def causal_depthwise_conv(x, w, b):
    K = w.shape[0]
    L = x.shape[1]
    xp = jnp.pad(x, ((0, 0), (K - 1, 0), (0, 0)))
    return sum(xp[:, j:j + L] * w[j] for j in range(K)) + b

def blockdiag(x, w):
    sh = x.shape
    xb = x.reshape(sh[:-1] + (w.shape[0], w.shape[1]))
    return jnp.einsum('blnc,ncd->blnd', xb, w).reshape(sh)

def mlstm_chunk_step(carry, xs):
    c_mat, n_vec, m_st = carry
    q, k, v, log_i, log_f = xs
    b = jnp.cumsum(log_f, axis=-1)
    g = b[..., -1]
    causal = jnp.tril(jnp.ones((ML_CHUNK, ML_CHUNK), dtype=bool))
    d_log = jnp.where(causal, b[..., :, None] - b[..., None, :] + log_i[..., None, :], -jnp.inf)
    inter_log = b + m_st[..., None]
    m_t = jnp.maximum(inter_log, jnp.max(d_log, axis=-1))
    w_intra = jnp.exp(d_log - m_t[..., None])
    s = jnp.einsum('bhtd,bhsd->bhts', q, k) * w_intra
    w_inter = jnp.exp(inter_log - m_t)
    num = jnp.einsum('bhts,bhsd->bhtd', s, v) + w_inter[..., None] * jnp.einsum('bhed,bhtd->bhte', c_mat, q)
    den = jnp.sum(s, axis=-1) + w_inter * jnp.einsum('bhd,bhtd->bht', n_vec, q)
    h = num / jnp.maximum(jnp.abs(den), jnp.exp(-m_t))[..., None]
    a = g[..., None] - b + log_i
    m_new = jnp.maximum(g + m_st, jnp.max(a, axis=-1))
    w_state = jnp.exp(a - m_new[..., None])
    decay = jnp.exp(g + m_st - m_new)
    c_new = decay[..., None, None] * c_mat + jnp.einsum('bhs,bhse,bhsd->bhed', w_state, v, k)
    n_new = decay[..., None] * n_vec + jnp.einsum('bhs,bhsd->bhd', w_state, k)
    return (c_new, n_new, m_new), h

def mlstm_branch(xm, z, conv_w, conv_b, wq, wk, wv, w_if, b_if, norm_g, skip):
    f32 = jnp.float32
    bn, L, _ = xm.shape
    H, dh = ML_HEADS, ML_HEAD_DIM
    xc = jax.nn.silu(causal_depthwise_conv(xm, conv_w, conv_b))
    q = blockdiag(xc, wq)
    k = blockdiag(xc, wk)
    v = blockdiag(xm, wv)
    gates = (jnp.concatenate([q, k, v], axis=-1) @ w_if + b_if).astype(f32)
    log_i = gates[..., :H]
    log_f = jax.nn.log_sigmoid(gates[..., H:])
    k = k * (dh ** -0.5)
    pad_f = (-N_META) % ML_CHUNK
    pad_b = (-(L + pad_f)) % ML_CHUNK
    n_chunks = (L + pad_f + pad_b) // ML_CHUNK

    def heads_to_chunks(t):
        t = jnp.pad(t.astype(f32).reshape(bn, L, H, dh), ((0, 0), (pad_f, pad_b), (0, 0), (0, 0)))
        return t.reshape(bn, n_chunks, ML_CHUNK, H, dh).transpose(1, 0, 3, 2, 4)

    def gate_to_chunks(t):
        t = jnp.pad(t, ((0, 0), (pad_f, pad_b), (0, 0)))
        return t.reshape(bn, n_chunks, ML_CHUNK, H).transpose(1, 0, 3, 2)

    init = (jnp.zeros((bn, H, dh, dh), f32), jnp.zeros((bn, H, dh), f32), jnp.zeros((bn, H), f32))
    _, hc = lax.scan(mlstm_chunk_step, init,
                     (heads_to_chunks(q), heads_to_chunks(k), heads_to_chunks(v),
                      gate_to_chunks(log_i), gate_to_chunks(log_f)))
    h = hc.transpose(1, 0, 3, 2, 4).reshape(bn, n_chunks * ML_CHUNK, H, dh)[:, pad_f:pad_f + L]
    h = jax.nn.sigmoid(z.astype(f32)).reshape(bn, L, H, dh) * h
    h = h * lax.rsqrt(jnp.mean(h * h, axis=-1, keepdims=True) + NORM_EPS)
    h = h.reshape(bn, L, ML_WIDTH) * norm_g.astype(f32) + skip.astype(f32) * xc.astype(f32)
    return h.astype(xm.dtype)

def peer_ffn(xn, w_q, sub_keys, u_tab, v_tab):
    f32 = jnp.float32
    bn, L, D = xn.shape
    T = bn * L
    n_blk = -(-T // PEER_TOKEN_BLOCK)
    xt = jnp.pad(xn.reshape(T, D), ((0, n_blk * PEER_TOKEN_BLOCK - T), (0, 0)))
    xt = xt.reshape(n_blk, PEER_TOKEN_BLOCK, D)
    keys32 = sub_keys.astype(f32)

    def block(xb):
        q = (xb @ w_q).astype(f32).reshape(PEER_TOKEN_BLOCK, PEER_HEADS, 2, PEER_HALF)
        s = jnp.einsum('thid,hikd->thik', q, keys32)
        sv, si = lax.top_k(s, PEER_TOPK)
        cand = sv[..., 0, :, None] + sv[..., 1, None, :]
        cidx = si[..., 0, :, None] * PEER_NKEYS + si[..., 1, None, :]
        cand = cand.reshape(PEER_TOKEN_BLOCK, PEER_HEADS, PEER_TOPK * PEER_TOPK)
        cidx = cidx.reshape(PEER_TOKEN_BLOCK, PEER_HEADS, PEER_TOPK * PEER_TOPK)
        cs, ci = lax.top_k(cand, PEER_TOPK)
        eidx = jnp.take_along_axis(cidx, ci, axis=-1)
        gate = jax.nn.softmax(cs, axis=-1)
        ug = u_tab[eidx]
        act = jax.nn.gelu(jnp.einsum('td,thkd->thk', xb, ug).astype(f32))
        vg = v_tab[eidx]
        return jnp.einsum('thk,thkd->td', (gate * act).astype(vg.dtype), vg)

    out = lax.map(block, xt).reshape(n_blk * PEER_TOKEN_BLOCK, D)[:T]
    return out.reshape(bn, L, D).astype(xn.dtype)

def second_inputs(seed: int = 0) -> dict:
    key = jax.random.key(seed)
    ks = list(jax.random.split(key, 40))
    f32 = jnp.float32
    it = iter(ks)

    def nrm(shape, scale):
        return jax.random.normal(next(it), shape, f32) * scale

    def gain(shape):
        return 1.0 + nrm(shape, 0.02)

    Dp = DEPTH_2
    x = nrm((BATCH, SEQ, D_MODEL), 1.0)
    meta_tokens = nrm((N_META, D_MODEL), 1.0)
    norm1_g = gain((Dp, D_MODEL))
    w_in = nrm((Dp, D_MODEL, IN_COLS), D_MODEL ** -0.5)
    ssm_a_re = -0.5 * jnp.exp(nrm((Dp, SSM_GROUPS, SSM_STATE), 0.05))
    ssm_a_im = jnp.pi * jnp.arange(SSM_STATE, dtype=f32) + nrm((Dp, SSM_GROUPS, SSM_STATE), 0.01)
    ssm_log_dt = jax.random.uniform(next(it), (Dp, SSM_GROUPS), f32, math.log(1e-3), math.log(1e-1))
    ssm_b_re = nrm((Dp, SSM_GROUPS, SSM_STATE, SSM_GROUP), (2 * SSM_GROUP) ** -0.5)
    ssm_b_im = nrm((Dp, SSM_GROUPS, SSM_STATE, SSM_GROUP), (2 * SSM_GROUP) ** -0.5)
    ssm_c_re = nrm((Dp, SSM_GROUPS, SSM_GROUP, SSM_STATE), (2 * SSM_STATE) ** -0.5)
    ssm_c_im = nrm((Dp, SSM_GROUPS, SSM_GROUP, SSM_STATE), (2 * SSM_STATE) ** -0.5)
    ssm_d = nrm((Dp, SSM_WIDTH), 0.5)
    ssm_w_glu = nrm((Dp, SSM_WIDTH, SSM_WIDTH), SSM_WIDTH ** -0.5)
    ssm_b_glu = nrm((Dp, SSM_WIDTH), 0.02)
    w_ssm_out = nrm((Dp, SSM_WIDTH, D_MODEL), SSM_WIDTH ** -0.5)
    ml_conv_w = nrm((Dp, ML_CONV, ML_WIDTH), 0.5)
    ml_conv_b = nrm((Dp, ML_WIDTH), 0.02)
    nb = ML_WIDTH // ML_QKV_BLOCK
    ml_wq = nrm((Dp, nb, ML_QKV_BLOCK, ML_QKV_BLOCK), ML_QKV_BLOCK ** -0.5)
    ml_wk = nrm((Dp, nb, ML_QKV_BLOCK, ML_QKV_BLOCK), ML_QKV_BLOCK ** -0.5)
    ml_wv = nrm((Dp, nb, ML_QKV_BLOCK, ML_QKV_BLOCK), ML_QKV_BLOCK ** -0.5)
    ml_w_if = nrm((Dp, 3 * ML_WIDTH, 2 * ML_HEADS), (3 * ML_WIDTH) ** -0.5)
    ml_b_if = jnp.concatenate([nrm((Dp, ML_HEADS), 0.1),
                               3.0 + 3.0 * jax.random.uniform(next(it), (Dp, ML_HEADS), f32)], axis=-1)
    ml_norm_g = gain((Dp, ML_WIDTH))
    ml_skip = 1.0 + nrm((Dp, ML_WIDTH), 0.1)
    w_ml_out = nrm((Dp, ML_WIDTH, D_MODEL), ML_WIDTH ** -0.5)
    w_out = nrm((Dp, D_MODEL, D_MODEL), D_MODEL ** -0.5)
    norm2_g = gain((Dp, D_MODEL))
    peer_w_q = nrm((Dp, D_MODEL, PEER_HEADS * PEER_QDIM), D_MODEL ** -0.5)
    peer_sub_keys = nrm((Dp, PEER_HEADS, 2, PEER_NKEYS, PEER_HALF), PEER_HALF ** -0.5)
    peer_u = nrm((Dp, PEER_EXPERTS, D_MODEL), D_MODEL ** -0.5)
    peer_v = nrm((Dp, PEER_EXPERTS, D_MODEL), 0.5 * PEER_HEADS ** -0.5)
    final_norm_g = gain((D_MODEL,))
    return {"x": x, "meta_tokens": meta_tokens, "norm1_g": norm1_g, "w_in": w_in,
            "ssm_a_re": ssm_a_re, "ssm_a_im": ssm_a_im, "ssm_log_dt": ssm_log_dt,
            "ssm_b_re": ssm_b_re, "ssm_b_im": ssm_b_im, "ssm_c_re": ssm_c_re, "ssm_c_im": ssm_c_im,
            "ssm_d": ssm_d, "ssm_w_glu": ssm_w_glu, "ssm_b_glu": ssm_b_glu, "w_ssm_out": w_ssm_out,
            "ml_conv_w": ml_conv_w, "ml_conv_b": ml_conv_b, "ml_wq": ml_wq, "ml_wk": ml_wk, "ml_wv": ml_wv,
            "ml_w_if": ml_w_if, "ml_b_if": ml_b_if, "ml_norm_g": ml_norm_g, "ml_skip": ml_skip,
            "w_ml_out": w_ml_out, "w_out": w_out, "norm2_g": norm2_g, "peer_w_q": peer_w_q,
            "peer_sub_keys": peer_sub_keys, "peer_u": peer_u, "peer_v": peer_v,
            "final_norm_g": final_norm_g}

def second_block(x, meta_tokens, norm1_g, w_in, ssm_a_re, ssm_a_im, ssm_log_dt, ssm_b_re, ssm_b_im,
              ssm_c_re, ssm_c_im, ssm_d, ssm_w_glu, ssm_b_glu, w_ssm_out, ml_conv_w, ml_conv_b,
              ml_wq, ml_wk, ml_wv, ml_w_if, ml_b_if, ml_norm_g, ml_skip, w_ml_out, w_out, norm2_g,
              peer_w_q, peer_sub_keys, peer_u, peer_v, final_norm_g):
    bn = x.shape[0]
    meta = jnp.broadcast_to(meta_tokens.astype(x.dtype)[None], (bn, N_META, D_MODEL))
    h = jnp.concatenate([meta, x], axis=1)
    splits = [SSM_WIDTH, SSM_WIDTH + ML_WIDTH, SSM_WIDTH + 2 * ML_WIDTH,
              SSM_WIDTH + 2 * ML_WIDTH + D_MODEL]
    for l in range(DEPTH_2):
        xn = rmsnorm_2(h, norm1_g[l])
        proj = xn @ w_in[l]
        u_s, x_m, z_m, g_s, g_m = jnp.split(proj, splits, axis=-1)
        y_s = s5_branch(u_s, ssm_a_re[l], ssm_a_im[l], ssm_log_dt[l], ssm_b_re[l], ssm_b_im[l],
                        ssm_c_re[l], ssm_c_im[l], ssm_d[l], ssm_w_glu[l], ssm_b_glu[l]) @ w_ssm_out[l]
        y_m = mlstm_branch(x_m, z_m, ml_conv_w[l], ml_conv_b[l], ml_wq[l], ml_wk[l], ml_wv[l],
                           ml_w_if[l], ml_b_if[l], ml_norm_g[l], ml_skip[l]) @ w_ml_out[l]
        mixed = jax.nn.sigmoid(g_s) * y_s + jax.nn.sigmoid(g_m) * y_m
        h = h + mixed @ w_out[l]
        h = h + peer_ffn(rmsnorm_2(h, norm2_g[l]), peer_w_q[l], peer_sub_keys[l], peer_u[l], peer_v[l])
    return rmsnorm_2(h, final_norm_g)[:, N_META:]


def setup_inputs(seed=0):
    out = dict(first_inputs(seed))
    for name, value in second_inputs(seed + 1).items():
        if name != "x":
            out[name + "_2"] = value
    return out


def reference(
    x, ffn1_norm, ffn1_w_gate, ffn1_w_up, ffn1_w_down, mix_norm, ffn2_norm, ffn2_w_gate,
    ffn2_w_up, ffn2_w_down, gla_w_in, gla_w_gk2, gla_b_gk, gla_o_norm, gla_w_out, sb_w_in,
    sb_w_out, final_norm, meta_tokens_2, norm1_g_2, w_in_2, ssm_a_re_2, ssm_a_im_2,
    ssm_log_dt_2, ssm_b_re_2, ssm_b_im_2, ssm_c_re_2, ssm_c_im_2, ssm_d_2, ssm_w_glu_2,
    ssm_b_glu_2, w_ssm_out_2, ml_conv_w_2, ml_conv_b_2, ml_wq_2, ml_wk_2, ml_wv_2, ml_w_if_2,
    ml_b_if_2, ml_norm_g_2, ml_skip_2, w_ml_out_2, w_out_2, norm2_g_2, peer_w_q_2,
    peer_sub_keys_2, peer_u_2, peer_v_2, final_norm_g_2,
):
    x = first_block(
        x, ffn1_norm, ffn1_w_gate, ffn1_w_up, ffn1_w_down, mix_norm, ffn2_norm, ffn2_w_gate,
        ffn2_w_up, ffn2_w_down, gla_w_in, gla_w_gk2, gla_b_gk, gla_o_norm, gla_w_out, sb_w_in,
        sb_w_out, final_norm,
    )
    return second_block(
        x, meta_tokens_2, norm1_g_2, w_in_2, ssm_a_re_2, ssm_a_im_2, ssm_log_dt_2, ssm_b_re_2,
        ssm_b_im_2, ssm_c_re_2, ssm_c_im_2, ssm_d_2, ssm_w_glu_2, ssm_b_glu_2, w_ssm_out_2,
        ml_conv_w_2, ml_conv_b_2, ml_wq_2, ml_wk_2, ml_wv_2, ml_w_if_2, ml_b_if_2, ml_norm_g_2,
        ml_skip_2, w_ml_out_2, w_out_2, norm2_g_2, peer_w_q_2, peer_sub_keys_2, peer_u_2,
        peer_v_2, final_norm_g_2,
    )


_drawn_inputs = setup_inputs


def setup_inputs(seed=0):
    import zlib

    import numpy as np

    out = dict(_drawn_inputs(seed))
    spreads = {}
    factors = {'ffn2_norm': 3.636,
     'gla_o_norm': 3.187,
     'ssm_a_re_2': 64.0,
     'ssm_a_im_2': 40.656,
     'ssm_log_dt_2': 42.64,
     'ssm_b_re_2': 51.456,
     'ssm_b_im_2': 51.44,
     'ssm_c_re_2': 53.32,
     'ssm_c_im_2': 53.64,
     'ssm_w_glu_2': 10.582,
     'ssm_b_glu_2': 178.587,
     'ml_conv_b_2': 3.092,
     'ml_norm_g_2': 4.697,
     'norm2_g_2': 5.113,
     'final_norm_g_2': 21.953,
     'ml_skip_2': 3.249}
    for name, (base, spread) in spreads.items():
        noise = np.random.default_rng([zlib.crc32(name.encode()), seed]).standard_normal(out[name].shape)
        drawn = base * np.exp(spread * noise) if base else spread * noise
        out[name] = __import__('jax').numpy.asarray(drawn.astype(out[name].dtype))
    for name, factor in factors.items():
        out[name] = (out[name] * factor).astype(out[name].dtype)
    return out
```

```python
from contextlib import ExitStack

import numpy as np
import concourse.bass as bass
from concourse import mybir

F32 = mybir.dt.float32
BF16 = mybir.dt.bfloat16
U32 = mybir.dt.uint32
ACT = mybir.ActivationFunctionType
ALU = mybir.AluOpType
AX_X = mybir.AxisListType.X

P = 128
D = 1024
DC = D // P
SEQ = 256
META = 16
TOK = SEQ + META
DFF = 2816
FT = DFF // P
GLA_H, GLA_K, GLA_V, GLA_RANK, GLA_C = 4, 128, 256, 16, 64
GLA_B = SEQ // GLA_C
SB_H, SB_D = 16, 64
S5_C = 16
S5_W = 512
ML_H, ML_D = 4, 256
PE_H, PE_K, PE_N = 8, 16, 128
HK = PE_H * PE_K
PE_SLOTS = 8
EPS = 1e-6
TWO_PI = 2 * np.pi
ROUND = 12582912.0

RING = 12


def packet_plan():
    at, n = {}, 0
    for name, count in (
        ("ffn0", 3 * FT), ("gla_in", 24), ("gla_out", 8), ("ffn1", 3 * FT),
        ("ffn2", 3 * FT), ("sb_in", 24), ("sb_out", 8), ("ffn3", 3 * FT),
        ("w_in", 36), ("s5_glu", 2), ("s5_out", 4), ("ml_out", 8), ("w_out", 8),
        ("peer_q", 16), ("peer_keys", 2),
    ):
        at[name] = n
        n += count
    return at, n


AT, PACKETS = packet_plan()

SMALL = {}
_n = 0
for _name, _width in (
    ("gains", 10 * DC), ("b_gk", 4), ("o_norm", 2), ("w_lr", DC * GLA_RANK),
    ("a_re", S5_C), ("a_im", S5_C), ("log_dt", S5_C), ("s5_d", 4), ("b_glu", 4),
    ("c_re", S5_C * 32), ("c_im", S5_C * 32), ("b_re", 4 * P), ("b_im", 4 * P),
    ("conv_w", DC * 4), ("conv_b", DC), ("wq", DC * 4), ("wk", DC * 4), ("wv", DC * 4),
    ("w_if", 24 * 8), ("ml_g", DC), ("ml_skip", DC),
):
    SMALL[_name] = (_n, _width)
    _n += _width
SMALL_W = _n
GAIN = {n: i for i, n in enumerate(
    ("ffn1_0", "mix_0", "ffn2_0", "ffn1_1", "mix_1", "ffn2_1", "final", "norm1", "norm2", "last"))}


class Counted:

    def __init__(self, sem):
        self.sem, self.n = sem, 0

    def __call__(self, ins):
        self.n += 1
        return ins.then_inc(self.sem, 1)

    def settle(self, eng):
        eng.wait_ge(self.sem, self.n)


class Arena:

    def __init__(self, tensor, width):
        self.t, self.at, self.width = tensor, 0, width

    def take(self, *dims):
        n = int(np.prod(dims))
        a = self.t[:, self.at:self.at + n]
        self.at += n
        assert self.at <= self.width, self.at
        if len(dims) == 2:
            a = a.rearrange("p (a b) -> p a b", b=dims[1])
        elif len(dims) == 3:
            a = a.rearrange("p (a b c) -> p a b c", b=dims[1], c=dims[2])
        elif len(dims) == 4:
            a = a.rearrange("p (a b c d) -> p a b c d", b=dims[1], c=dims[2], d=dims[3])
        return a


def spread(ap, n):
    return ap.unsqueeze(2).to_broadcast([ap.shape[0], ap.shape[1], n])


def bcast(ap, n):
    return ap.unsqueeze(1).to_broadcast([ap.shape[0], n, ap.shape[1]])




def slot_of(k, n):
    return k.ring[:, n % RING, :]


def wait_packet(k, pe, n):
    pe.wait_ge(k.landed[n % RING], 16 * (n // RING + 1))


def mm_packet(k, pe, n, x, out, kc=DC, col=0, width=128):
    w = slot_of(k, n).rearrange("p (c m) -> p c m", c=kc)
    for c in range(kc):
        last = pe.matmul(out, w[:, c, col:col + 128], x[:, c, :], start=(c == 0), stop=(c == kc - 1))
    return last


def stage_end(k, eng, who):
    k.stage[who] += 1
    eng.drain().then_inc(k.stage_sem[who], 1)
    for other, sem in k.stage_sem.items():
        if other != who:
            eng.wait_ge(sem, k.stage[who])


def norm_act(k, act, r, x, T):
    for h in range(2):
        act.activation(k.sq[:, 4 * h:4 * h + 4, 0:T], x[:, 4 * h:4 * h + 4, :], ACT.Square).then_inc(k.sq_ready, 1)
    act.wait_ge(k.ss_ready, r + 1)
    act.activation(k.rms[:, 0:T], k.ps[:, 7, 0:T], ACT.Sqrt, bias=k.eps, scale=1.0 / D).then_inc(k.rms_ready, 1)


def norm_pe(k, pe, r, T):
    for c in range(DC):
        if c % 4 == 0:
            pe.wait_ge(k.sq_ready, 2 * r + c // 4 + 1)
        last = pe.matmul(k.ps[:, 7, 0:T], k.ones, k.sq[:, c, 0:T], start=(c == 0), stop=(c == DC - 1))
    last.then_inc(k.ss_ready, 1)


def norm_dve(k, dve, r, x, xn, gain, T):
    dve.wait_ge(k.rms_ready, r + 1)
    k.dve(dve.reciprocal(k.rstd[:, 0:T], k.rms[:, 0:T]))
    k.dve.settle(dve)
    for c in range(DC):
        g = k.small["gains"][:, gain * DC + c:gain * DC + c + 1]
        dve.scalar_tensor_tensor(out=xn[:, c, :], in0=x[:, c, :], scalar=g, in1=k.rstd[:, 0:T],
                                 op0=ALU.mult, op1=ALU.mult).then_inc(k.xn_ready, 1)


class Tiles:

    def __init__(self, k, engs):
        self.k, self.engs, self.base = k, engs, (k.dve_tiles, k.act_tiles)
        k.dve_tiles += engs.count("D")
        k.act_tiles += engs.count("A")

    def wait_free(self, pe, n):
        if n >= 4:
            self.wait_emptied(pe, n - 4)

    def wait_emptied(self, pe, n):
        if self.engs[n] == "D":
            pe.wait_ge(self.k.dve_emptied, self.base[0] + self.engs[:n + 1].count("D"))
        else:
            pe.wait_ge(self.k.act_emptied, self.base[1] + self.engs[:n + 1].count("A"))




def setup(k, block):

    @block.scalar
    def _(act):
        for dst, src in k.small_loads:
            act.dma_start(dst, src).then_inc(k.small_in, 16)
        act.wait_ge(k.small_in, 16 * len(k.small_loads))

    @block.vector
    def _(dve):
        k.dve(dve.memset(k.eps, EPS))
        k.dve(dve.memset(k.ones, 1.0))
        k.dve(dve.memset(k.one_col, 1.0))
        k.dve(dve.memset(k.neg_ones, -1.0))
        k.dve(dve.memset(k.zero_bf, 0.0))
        k.dve(dve.memset(k.ones_row, 1.0))

    @block.gpsimd
    def _(pool):
        k.pool(pool.memset(k.ident, 1.0))
        k.pool(pool.memset(k.keep_ge, 1.0))
        k.pool(pool.memset(k.keep_gt, 1.0))
        k.pool(pool.memset(k.neg_tri, -1.0))
        k.pool(pool.memset(k.head_row, 1.0))
        k.pool(pool.memset(k.block4, 1.0))
        k.pool(pool.iota(k.iota16, pattern=[[0, 16], [1, 16]], base=0, channel_multiplier=0,
                         allow_small_or_imprecise_dtypes=True))
        k.pool.settle(pool)
        k.pool(pool.affine_select(out=k.ident, in_=k.ident, compare_op=ALU.is_equal, fill=0.0, base=0,
                                  pattern=[[1, P]], channel_multiplier=-1))
        k.pool(pool.affine_select(out=k.keep_ge, in_=k.keep_ge, compare_op=ALU.is_ge, fill=0.0, base=0,
                                  pattern=[[1, P]], channel_multiplier=-1))
        k.pool(pool.affine_select(out=k.keep_gt, in_=k.keep_gt, compare_op=ALU.is_gt, fill=0.0, base=0,
                                  pattern=[[1, P]], channel_multiplier=-1))
        k.pool(pool.affine_select(out=k.neg_tri, in_=k.neg_tri, compare_op=ALU.is_ge, fill=0.0, base=0,
                                  pattern=[[-1, P]], channel_multiplier=1))
        k.pool(pool.affine_select(out=k.head_row, in_=k.head_row, compare_op=ALU.is_equal, fill=0.0, base=0,
                                  pattern=[[1, ML_H], [0, P]], channel_multiplier=-1))
        k.pool(pool.affine_select(out=k.block4, in_=k.block4, compare_op=ALU.is_ge, fill=0.0, base=0,
                                  pattern=[[-4, 32]], channel_multiplier=1))
        k.pool.settle(pool)
        k.pool(pool.affine_select(out=k.block4, in_=k.block4, compare_op=ALU.is_ge, fill=0.0, base=3,
                                  pattern=[[4, 32]], channel_multiplier=-1))

    block.scalar(lambda e: stage_end(k, e, "act"))
    block.vector(lambda e: stage_end(k, e, "dve"))
    block.gpsimd(lambda e: stage_end(k, e, "pool"))
    block.tensor(lambda e: stage_end(k, e, "pe"))


def all_end(k, block):
    block.scalar(lambda e: stage_end(k, e, "act"))
    block.vector(lambda e: stage_end(k, e, "dve"))
    block.gpsimd(lambda e: stage_end(k, e, "pool"))
    block.tensor(lambda e: stage_end(k, e, "pe"))


def weights_in(k, block, wstream):

    @block.sync
    def _(sp):
        for n in range(RING):
            sp.dma_start(k.ring[:, n, :], wstream[n]).then_inc(k.landed[n], 16)
        full = PACKETS // RING
        with sp.Fori(1, full) as i:
            for s in range(RING):
                sp.wait_ge(k.tile_done, (i - 1) * RING + (s + 1))
                sp.dma_start(k.ring[:, s, :], wstream[bass.ds(i * RING + s, 1)].rearrange("a p m -> p (a m)")
                             ).then_inc(k.landed[s], 16)
        for n in range(full * RING, PACKETS):
            sp.wait_ge(k.tile_done, n - RING + 1)
            sp.dma_start(k.ring[:, n % RING, :], wstream[n]).then_inc(k.landed[n % RING], 16)


def s5_tables(k, block):
    sm = k.small

    @block.scalar
    def _(act):
        act.activation(k.s5_dt, sm["log_dt"], ACT.Exp).then_inc(k.s5_act, 1)
        act.wait_ge(k.s5_er, 1)
        act.activation(k.s5_r, k.s5_ere, ACT.Exp).then_inc(k.s5_act, 1)
        act.wait_ge(k.s5_th, 1)
        act.activation(k.s5_sin, k.s5_theta, ACT.Sin).then_inc(k.s5_act, 1)
        act.activation(k.s5_half, k.s5_theta, ACT.Sin, scale=0.5).then_inc(k.s5_act, 1)

    @block.gpsimd
    def _(pool):
        t = k.s5_tmp

        def tt(out, a, b, op):
            k.pool(pool.tensor_tensor(out, a, b, op))
            k.pool.settle(pool)

        def ts(out, a, s1, s2, op0, op1):
            k.pool(pool.tensor_scalar(out, a, s1, s2, op0, op1))
            k.pool.settle(pool)

        pool.wait_ge(k.s5_act, 1)
        pool.tensor_tensor(k.s5_ere, sm["a_re"], k.s5_dt, ALU.mult).then_inc(k.s5_er, 1)
        tt(k.s5_theta, sm["a_im"], k.s5_dt, ALU.mult)
        ts(t[0], k.s5_theta, 1.0 / TWO_PI, ROUND, ALU.mult, ALU.add)
        ts(t[0], t[0], -ROUND, -6.28125, ALU.add, ALU.mult)
        tt(k.s5_theta, k.s5_theta, t[0], ALU.add)
        c2 = float(np.float32(0.0019353071795864769))
        c2 = float(np.float32(round(c2 * 2 ** 23) / 2 ** 23))
        ts(t[1], t[0], c2 / 6.28125, None, ALU.mult, ALU.bypass)
        tt(k.s5_theta, k.s5_theta, t[1], ALU.add)
        c3 = TWO_PI - 6.28125 - c2
        ts(t[1], t[0], c3 / 6.28125, None, ALU.mult, ALU.bypass)
        tt(k.s5_theta, k.s5_theta, t[1], ALU.add)
        pool.tensor_scalar(k.s5_theta, k.s5_theta, 3.1415925, -3.1415925, ALU.min, ALU.max).then_inc(k.s5_th, 1)
        pool.wait_ge(k.s5_act, 4)
        tt(t[0], k.s5_half, k.s5_half, ALU.mult)
        ts(k.s5_cos, t[0], -2.0, 1.0, ALU.mult, ALU.add)
        tt(t[0], k.s5_r, k.s5_cos, ALU.mult)
        ts(t[0], t[0], -1.0, None, ALU.add, ALU.bypass)
        tt(t[1], k.s5_r, k.s5_sin, ALU.mult)
        tt(t[2], sm["a_re"], sm["a_re"], ALU.mult)
        tt(t[3], sm["a_im"], sm["a_im"], ALU.mult)
        k.pool(pool.tensor_tensor(k.s5_mod, t[2], t[3], ALU.add))
        k.pool.settle(pool)
        pool.tensor_copy(k.s5_mod2, k.s5_mod).then_inc(k.s5_mod_ready, 1)
        pool.wait_ge(k.s5_inv_ready, 1)
        tt(t[2], t[0], sm["a_re"], ALU.mult)
        tt(t[3], t[1], sm["a_im"], ALU.mult)
        tt(t[2], t[2], t[3], ALU.add)
        tt(k.s5_cre, t[2], k.s5_inv, ALU.mult)
        tt(t[2], t[1], sm["a_re"], ALU.mult)
        tt(t[3], t[0], sm["a_im"], ALU.mult)
        tt(t[2], t[2], t[3], ALU.subtract)
        tt(k.s5_cim, t[2], k.s5_inv, ALU.mult)
        cre = sm["c_re"].rearrange("p (c m) -> p c m", c=S5_C)
        cim = sm["c_im"].rearrange("p (c m) -> p c m", c=S5_C)
        ar, ai = spread(k.s5_cre, 32), spread(k.s5_cim, 32)
        w = [k.s5_big[i][:, :, 0:32] for i in range(4)]
        tt(w[0], cre, ar, ALU.mult)
        tt(w[1], cim, ai, ALU.mult)
        tt(w[2], cre, ai, ALU.mult)
        tt(w[3], cim, ar, ALU.mult)
        tt(cre, w[0], w[1], ALU.subtract)
        tt(cim, w[2], w[3], ALU.add)
        ec, es = k.s5_ec, k.s5_es
        k.pool(pool.memset(ec[:, :, 0:1], 1.0))
        k.pool(pool.memset(es[:, :, 0:1], 0.0))
        k.pool.settle(pool)
        pc, pn = t[4], t[5]
        k.pool(pool.tensor_copy(pc, k.s5_cos))
        k.pool(pool.tensor_copy(pn, k.s5_sin))
        k.pool.settle(pool)
        n = 1
        while n < TOK:
            m = min(n, TOK - n)
            bc, bs = spread(pc, m), spread(pn, m)
            a, b = k.s5_big[0][:, :, 0:m], k.s5_big[1][:, :, 0:m]
            tt(a, ec[:, :, 0:m], bc, ALU.mult)
            tt(b, es[:, :, 0:m], bs, ALU.mult)
            tt(ec[:, :, n:n + m], a, b, ALU.subtract)
            tt(a, ec[:, :, 0:m], bs, ALU.mult)
            tt(b, es[:, :, 0:m], bc, ALU.mult)
            tt(es[:, :, n:n + m], a, b, ALU.add)
            tt(t[0], pc, pc, ALU.mult)
            tt(t[1], pn, pn, ALU.mult)
            tt(t[2], pc, pn, ALU.mult)
            tt(pc, t[0], t[1], ALU.subtract)
            ts(pn, t[2], 2.0, None, ALU.mult, ALU.bypass)
            n *= 2

    @block.vector
    def _(dve):
        dve.wait_ge(k.s5_mod_ready, 1)
        dve.reciprocal(k.s5_inv, k.s5_mod2).then_inc(k.s5_inv_ready, 1)


def feed_forward(k, block, q, gain, packet):
    x = k.x[:, :, META:TOK]
    xn = k.xn[:, :, 0:SEQ]
    r = k.norms
    k.norms += 1
    gate_ps, up_ps = [k.ps[:, 4 + b, 0:SEQ] for b in range(2)], [k.ps[:, 6 + b, 0:SEQ] for b in range(2)]
    y = k.ps[:, 0:4, :]
    base = FT * q

    @block.scalar
    def _(act):
        norm_act(k, act, r, x, SEQ)

        def one(f, b, n):
            act.wait_ge(k.tile_done, n)
            if not (isinstance(f, int) and f < 2):
                act.wait_ge(k.h_ready, base + f - 1)
            act.activation(k.gate_s[:, b, :], gate_ps[b], ACT.Silu).then_inc(k.silu_ready, 1)

        one(0, 0, packet + 1)
        one(1, 1, packet + 3)
        with act.Fori(0, (FT - 2) // 4) as i:
            for j in range(4):
                one(i * 4 + (2 + j), j % 2, i * RING + (packet + 5 + 3 * j + 1))

    @block.vector
    def _(dve):
        norm_dve(k, dve, r, x, xn, gain, SEQ)

        def one(f, b, n):
            dve.wait_ge(k.tile_done, n)
            dve.wait_ge(k.silu_ready, base + 1 + f)
            dve.tensor_tensor(k.h[:, b, :], k.gate_s[:, b, :], up_ps[b], ALU.mult).then_inc(k.h_ready, 1)

        one(0, 0, packet + 2)
        one(1, 1, packet + 4)
        with dve.Fori(0, (FT - 2) // 4) as i:
            for j in range(4):
                one(i * 4 + (2 + j), j % 2, i * RING + (packet + 5 + 3 * j + 2))
        dve.wait_ge(k.tile_done, packet + 3 * FT)
        for b in range(4):
            xb = x[:, 2 * b:2 * b + 2, :]
            dve.scalar_tensor_tensor(out=xb, in0=y[:, b, :].rearrange("p (a t) -> p a t", a=2), scalar=0.5,
                                     in1=xb, op0=ALU.mult, op1=ALU.add)

    @block.tensor
    def _(pe):
        norm_pe(k, pe, r, SEQ)
        for b in range(4):
            pe.matmul(y[:, b, :], k.zero_bf[:, 0:P], k.zero_bf, start=True, stop=False, skip_group_check=True)

        def gate_up(f, b, n, waits, first):
            if f is not None:
                pe.wait_ge(k.h_ready, base - 1 + f)
            for w in range(2):
                if first:
                    wait_packet(k, pe, n + w)
                else:
                    pe.wait_ge(k.landed[(n + w) % RING], waits[w])
                wt = slot_of(k, n + w).rearrange("p (c m) -> p c m", c=DC)
                for c in range(DC):
                    if first and w == 0:
                        pe.wait_ge(k.xn_ready, DC * r + c + 1)
                    last = pe.matmul((gate_ps, up_ps)[w][b], wt[:, c, :], xn[:, c, :],
                                     start=(c == 0), stop=(c == DC - 1))
                last.then_inc(k.tile_done, 1)

        def down(f, b, n, wait, stop=False):
            pe.wait_ge(k.h_ready, base + 1 + f)
            pe.wait_ge(k.landed[n % RING], wait)
            for c in range(DC):
                last = pe.matmul(y[:, c // 2, (c % 2) * SEQ:(c % 2 + 1) * SEQ], slot_of(k, n)[:, c * P:(c + 1) * P],
                                 k.h[:, b, :], start=False, stop=stop, skip_group_check=True)
            last.then_inc(k.tile_done, 1)

        turn = lambda n: 16 * (n // RING + 1)
        gate_up(None, 0, packet, None, True)
        gate_up(None, 1, packet + 2, None, True)
        down(0, 0, packet + 4, turn(packet + 4))
        with pe.Fori(0, (FT - 2) // 4) as i:
            for j in range(4):
                n = packet + 5 + 3 * j
                gate_up(i * 4 + (2 + j), j % 2, n, [i * 16 + turn(n), i * 16 + turn(n + 1)], False)
                down(i * 4 + (1 + j), (1 + j) % 2, n + 2, i * 16 + turn(n + 2))
        n = packet + 3 * FT - 1
        down(FT - 1, (FT - 1) % 2, n, turn(n), stop=True)

    all_end(k, block)


def add_projection(k, block, packet, src, ready, count, tok0=META):
    tiles = Tiles(k, ["D"] * 8)

    @block.tensor
    def _(pe):
        for n in range(8):
            if n == 0:
                pe.wait_ge(ready, count)
            tiles.wait_free(pe, n)
            wait_packet(k, pe, packet + n)
            mm_packet(k, pe, packet + n, src, k.ps[:, n % 4, 0:SEQ]).then_inc(k.tile_done, 1)

    @block.vector
    def _(dve):
        for n in range(8):
            dve.wait_ge(k.tile_done, packet + n + 1)
            xb = k.x[:, n, META:TOK]
            dve.tensor_tensor(xb, k.ps[:, n % 4, 0:SEQ], xb, ALU.add).then_inc(k.dve_emptied, 1)

    all_end(k, block)


def gated_linear_attention(k, block, gain):
    x, xn = k.x[:, :, META:TOK], k.xn[:, :, 0:SEQ]
    sm, ps = k.small, k.ps
    r = k.norms
    k.norms += 1
    mark = k.arena.at
    take = k.arena.take
    H, B, C = GLA_H, GLA_B, GLA_C
    qs, ks = take(H, SEQ), take(H, SEQ)
    vt = take(2, D)
    sg = take(DC, SEQ)
    lr = take(SEQ)
    zb_at = k.arena.at
    zb, az, cum = take(H, SEQ), take(H, SEQ), take(H, SEQ)
    la = zb
    up, down_ = take(H, B), take(H, B)
    off = [0]
    for i in range(B):
        off.append(off[-1] + C * (i + 1))
    eq, ek = take(H, SEQ), take(H, off[B])
    st = take(2, 3 * P)
    o = take(H, 2 * SEQ)
    osq = k.arena.t[:, zb_at:zb_at + 2 * H * SEQ].rearrange("p (h t) -> p h t", h=H)
    rms = take(H, SEQ)
    wlr = sm["w_lr"].rearrange("p (c m) -> p c m", c=DC)
    tiles = Tiles(k, ["D"] * 16 + ["A"] * 8)
    p0 = AT["gla_in"]

    @block.scalar
    def _(act):
        norm_act(k, act, r, x, SEQ)
        act.wait_ge(k.gla_pe, 1)
        act.activation(lr[0:GLA_RANK, :], ps[0:GLA_RANK, 7, 0:SEQ], ACT.Copy).then_inc(k.gla_act, 1)
        act.wait_ge(k.gla_dve, 1)
        k.act(act.activation(az, az, ACT.Exp, scale=-1.0))
        k.act.settle(act)
        act.activation(az, az, ACT.Ln, bias=k.one_col).then_inc(k.gla_act, 1)
        act.wait_ge(k.gla_dve, 2)
        for h in range(H):
            for i in range(B):
                act.activation(eq[:, h, C * i:C * (i + 1)], cum[:, h, C * i:C * (i + 1)], ACT.Exp,
                               bias=down_[:, h, i:i + 1], scale=1.0 / 16)
                last = act.activation(ek[:, h, off[i]:off[i + 1]], cum[:, h, 0:C * (i + 1)], ACT.Exp,
                                      bias=up[:, h, i:i + 1], scale=-1.0 / 16)
            last.then_inc(k.gla_act, 1)
        for n in range(16, 24):
            act.wait_ge(k.tile_done, p0 + n + 1)
            act.activation(sg[:, n - 16, :], ps[:, n % 4, 0:SEQ], ACT.Silu).then_inc(k.act_emptied, 1)
        for h in range(H):
            act.wait_ge(k.gla_o, h + 1)
            act.activation(osq[:, h, :], ps[:, 6 + h % 2, :], ACT.Square).then_inc(k.gla_sq, 1)
        for h in range(H):
            act.wait_ge(k.gla_ss, h + 1)
            act.activation(rms[:, h, :], ps[:, h, 0:SEQ], ACT.Sqrt, bias=k.eps, scale=1.0 / GLA_V
                           ).then_inc(k.gla_rms, 1)

    @block.vector
    def _(dve):
        norm_dve(k, dve, r, x, xn, gain, SEQ)
        k.dve(dve.memset(st, 0.0))
        dve.wait_ge(k.gla_pe, 2)
        for h in range(H):
            k.dve(dve.tensor_scalar(zb[:, h, :], ps[:, 4 + h // 2, (h % 2) * SEQ:(h % 2 + 1) * SEQ],
                                    sm["b_gk"][:, h:h + 1], None, ALU.add))
        k.dve.settle(dve)
        dve.scalar_tensor_tensor(out=az, in0=zb, scalar=-1.0, in1=zb, op0=ALU.mult, op1=ALU.max
                                 ).then_inc(k.gla_dve, 1)
        for n in range(4):
            dve.wait_ge(k.tile_done, p0 + n + 1)
            dve.tensor_scalar(qs[:, n, :], ps[:, n % 4, 0:SEQ], GLA_K ** -0.5, None, ALU.mult
                              ).then_inc(k.dve_emptied, 1)
        dve.wait_ge(k.gla_act, 2)
        k.dve(dve.scalar_tensor_tensor(out=la, in0=zb, scalar=0.0, in1=az, op0=ALU.min, op1=ALU.subtract))
        k.dve.settle(dve)
        for h in range(H):
            k.dve(dve.tensor_tensor_scan(cum[:, h, :], k.ones_row[:, 0:SEQ], la[:, h, :], 0.0, ALU.mult, ALU.add))
        k.dve.settle(dve)
        mid = cum.rearrange("p h (i c) -> p h i c", c=C)[:, :, :, C // 2 - 1]
        k.dve(dve.tensor_scalar(up, mid, 1.0 / 16, None, ALU.mult))
        dve.tensor_scalar(down_, mid, -1.0 / 16, None, ALU.mult).then_inc(k.gla_dve, 1)
        for n in range(4, 8):
            dve.wait_ge(k.tile_done, p0 + n + 1)
            dve.tensor_copy(ks[:, n - 4, :], ps[:, n % 4, 0:SEQ]).then_inc(k.dve_emptied, 1)
        for n in range(8, 16):
            dve.wait_ge(k.tile_done, p0 + n + 1)
            dve.tensor_copy(vt[:, :, (n - 8) * P:(n - 7) * P],
                            ps[:, n % 4, 0:2 * P].rearrange("p (a m) -> p a m", a=2)).then_inc(k.dve_emptied, 1)
        dve.wait_ge(k.dve_emptied, tiles.base[0] + 16)
        k.dve.settle(dve)
        for h in range(H):
            dve.wait_ge(k.gla_act, 3 + h)
            dve.tensor_tensor(eq[:, h, :], eq[:, h, :], qs[:, h, :], ALU.mult).then_inc(k.gla_qk, 1)
            for i in range(B):
                e = ek[:, h, off[i]:off[i + 1]]
                dve.tensor_tensor(e, e, ks[:, h, 0:C * (i + 1)], ALU.mult).then_inc(k.gla_qk, 1)
        for h in range(H):
            b, s = ps[:, 4 + h % 2, :], st[:, h % 2, :]
            dve.wait_ge(k.gla_s, h + 1)
            if h >= 2:
                dve.wait_ge(k.gla_o, h - 1)
            m = k.keep_ge
            dve.tensor_tensor(s[0:C, 0:C], b[0:C, 0:C], m[0:C, 0:C], ALU.mult)
            dve.tensor_tensor(s[:, C:2 * C], b[:, C:2 * C], m[:, C:2 * C], ALU.mult)
            dve.tensor_copy(s[:, 2 * C:4 * C], b[:, 2 * C:4 * C])
            dve.tensor_tensor(s[0:C, 4 * C:5 * C], b[0:C, 4 * C:5 * C], m[0:C, 0:C], ALU.mult)
            dve.tensor_tensor(s[:, 5 * C:6 * C], b[:, 5 * C:6 * C], m[:, C:2 * C], ALU.mult).then_inc(k.gla_st, 1)
            dve.wait_ge(k.gla_sq, h + 1)
            dve.tensor_copy(o[:, h, :], ps[:, 6 + h % 2, :]).then_inc(k.gla_copied, 1)
        dve.wait_ge(k.gla_copied, H)
        dve.wait_ge(k.act_emptied, tiles.base[1] + 8)
        for h in range(H):
            dve.wait_ge(k.gla_rms, h + 1)
            k.dve(dve.reciprocal(rms[:, h, :], rms[:, h, :]))
            k.dve.settle(dve)
            for e in range(2):
                oe = o[:, h, e * SEQ:(e + 1) * SEQ]
                k.dve(dve.scalar_tensor_tensor(out=oe, in0=oe, scalar=sm["o_norm"][:, e:e + 1], in1=rms[:, h, :],
                                               op0=ALU.mult, op1=ALU.mult))
            k.dve.settle(dve)
            g = sg[:, 2 * h:2 * h + 2, :]
            oh = o[:, h, :].rearrange("p (e t) -> p e t", e=2)
            dve.tensor_tensor(g, g, oh, ALU.mult).then_inc(k.mix_ready, 1)

    @block.tensor
    def _(pe):
        norm_pe(k, pe, r, SEQ)
        pe.wait_ge(k.rms_ready, r + 1)
        pe.wait_ge(k.xn_ready, DC * (r + 1))
        for c in range(DC):
            last = pe.matmul(ps[0:GLA_RANK, 7, 0:SEQ], wlr[:, c, :], xn[:, c, :], start=(c == 0), stop=(c == DC - 1))
        last.then_inc(k.gla_pe, 1)

        def tile(n):
            tiles.wait_free(pe, n)
            wait_packet(k, pe, p0 + n)
            if n < 8 or n >= 16:
                mm_packet(k, pe, p0 + n, xn, ps[:, n % 4, 0:SEQ]).then_inc(k.tile_done, 1)
            else:
                w = slot_of(k, p0 + n).rearrange("p (c m) -> p c m", c=DC)
                for t in range(2):
                    for c in range(DC):
                        last = pe.matmul(ps[:, n % 4, t * P:(t + 1) * P], xn[:, c, t * P:(t + 1) * P], w[:, c, :],
                                         start=(c == 0), stop=(c == DC - 1))
                last.then_inc(k.tile_done, 1)

        tile(0)
        pe.wait_ge(k.gla_act, 1)
        for h in range(H):
            last = pe.matmul(ps[:, 4 + h // 2, (h % 2) * SEQ:(h % 2 + 1) * SEQ],
                             k.w_gk2[:, h * P:(h + 1) * P], lr[0:GLA_RANK, :], start=True, stop=True)
        last.then_inc(k.gla_pe, 1)
        for n in range(1, 24):
            tile(n)

        def scores(h):
            b = ps[:, 4 + h % 2, :]
            pe.wait_ge(k.gla_qk, 5 * (h + 1))
            if h >= 2:
                pe.wait_ge(k.gla_st, h - 1)
            q = lambda i: eq[:, h, C * i:C * (i + 1)]
            kk = lambda i, lo, n: ek[:, h, off[i] + lo:off[i] + lo + n]
            pe.matmul(b[0:C, 0:C], kk(0, 0, C), q(0), start=True, stop=True)
            pe.matmul(b[:, C:2 * C], kk(1, 0, P), q(1), start=True, stop=True)
            pe.matmul(b[:, 2 * C:3 * C], kk(2, 0, P), q(2), start=True, stop=True)
            pe.matmul(b[:, 3 * C:4 * C], kk(3, 0, P), q(3), start=True, stop=True)
            pe.matmul(b[0:C, 4 * C:5 * C], kk(2, P, C), q(2), start=True, stop=True)
            pe.matmul(b[:, 5 * C:6 * C], kk(3, P, P), q(3), start=True, stop=True).then_inc(k.gla_s, 1)

        def outputs(h):
            pe.wait_ge(k.gla_st, h + 1)
            if h >= 2:
                pe.wait_ge(k.gla_copied, h - 1)
                pe.wait_ge(k.gla_sq, h - 1)
            s = st[:, h % 2, :]
            for e in range(2):
                b = ps[:, 6 + h % 2, e * SEQ:(e + 1) * SEQ]
                v = lambda t: vt[:, t, h * GLA_V + e * P:h * GLA_V + (e + 1) * P]
                pe.matmul(b, v(0), s[:, 0:SEQ], start=True, stop=False, skip_group_check=True)
                last = pe.matmul(b[:, P:SEQ], v(1), s[:, SEQ:SEQ + P], start=False, stop=True, skip_group_check=True)
            last.then_inc(k.gla_o, 1)

        for h in range(H):
            scores(h)
            outputs(h)
        for h in range(H):
            pe.wait_ge(k.gla_sq, h + 1)
            if h == 0:
                for n in range(20, 24):
                    tiles.wait_emptied(pe, n)
            for e in range(2):
                last = pe.matmul(ps[:, h, 0:SEQ], k.ones, osq[:, h, e * SEQ:(e + 1) * SEQ], start=(e == 0), stop=(e == 1))
            last.then_inc(k.gla_ss, 1)
        pe.wait_ge(k.gla_rms, H)

    k.mixes += H
    add_projection(k, block, AT["gla_out"], sg, k.mix_ready, k.mixes)
    k.arena.at = mark


def stick_breaking(k, block, gain):
    x, xn = k.x[:, :, META:TOK], k.xn[:, :, 0:SEQ]
    ps = k.ps
    r = k.norms
    k.norms += 1
    mark = k.arena.at
    take = k.arena.take
    qs, ks = take(DC, SEQ), take(DC, SEQ)
    vt = take(2, D)
    ot = take(DC, SEQ)
    ab, spl, w = take(2, 3 * P), take(2, 3 * P), take(2, 3 * P)
    tiles = Tiles(k, ["A"] * 8 + ["D"] * 16)
    p0 = AT["sb_in"]
    N3 = 3 * P
    diag = lambda a: a.rearrange("p (j t) -> p j t", j=3)[:, 0:3:2, :]
    mask = bcast(k.keep_gt, 2)

    @block.scalar
    def _(act):
        norm_act(k, act, r, x, SEQ)
        for n in range(8):
            act.wait_ge(k.tile_done, p0 + n + 1)
            act.activation(qs[:, n, :], ps[:, n % 4, 0:SEQ], ACT.Copy, scale=SB_D ** -0.5).then_inc(k.act_emptied, 1)
        for h in range(SB_H + 1):
            if h < SB_H:
                b = ps[:, 4 + h % 2, 0:N3]
                a = ab[:, h % 2, :]
                act.wait_ge(k.sb_z, h + 1)
                if h >= 2:
                    act.wait_ge(k.sb_sp, h - 1)
                k.act(act.activation(a, b, ACT.Abs))
                k.act.settle(act)
                k.act(act.activation(a, a, ACT.Exp, scale=-1.0))
                k.act.settle(act)
                act.activation(a, a, ACT.Ln, bias=k.one_col).then_inc(k.sb_ln, 1)
            if h >= 1:
                g = h - 1
                act.wait_ge(k.sb_log, g + 1)
                if g >= 2:
                    act.wait_ge(k.sb_av, g - 1)
                act.activation(w[:, g % 2, :], ps[:, 4 + g % 2, 0:N3], ACT.Exp).then_inc(k.sb_exp, 1)

    @block.vector
    def _(dve):
        norm_dve(k, dve, r, x, xn, gain, SEQ)
        for n in range(8, 24):
            dve.wait_ge(k.tile_done, p0 + n + 1)
            if n < 16:
                c = dve.tensor_copy(ks[:, n - 8, :], ps[:, n % 4, 0:SEQ])
            else:
                c = dve.tensor_copy(vt[:, :, (n - 16) * P:(n - 15) * P],
                                    ps[:, n % 4, 0:2 * P].rearrange("p (a m) -> p a m", a=2))
            c.then_inc(k.dve_emptied, 1)
        for h in range(SB_H + 2):
            if h < SB_H:
                dve.wait_ge(k.sb_ln, h + 1)
                if h >= 2:
                    dve.wait_ge(k.sb_log, h - 1)
                s = spl[:, h % 2, :]
                k.dve(dve.scalar_tensor_tensor(out=s, in0=ps[:, 4 + h % 2, 0:N3], scalar=0.0, in1=ab[:, h % 2, :],
                                               op0=ALU.max, op1=ALU.add))
                k.dve.settle(dve)
                dve.tensor_tensor(diag(s), diag(s), mask, ALU.mult).then_inc(k.sb_sp, 1)
            if 1 <= h <= SB_H:
                g = h - 1
                dve.wait_ge(k.sb_exp, g + 1)
                s = diag(w[:, g % 2, :])
                dve.scalar_tensor_tensor(out=s, in0=s, scalar=1.0, in1=mask, op0=ALU.min, op1=ALU.mult
                                         ).then_inc(k.sb_w, 1)
            if h >= 2 and (h - 2) % 2 == 1:
                g = h - 2
                dve.wait_ge(k.sb_av, g + 1)
                dve.tensor_copy(ot[:, g // 2, :], ps[:, 6 + (g // 2) % 2, 0:SEQ]).then_inc(k.mix_ready, 1)

    @block.tensor
    def _(pe):
        norm_pe(k, pe, r, SEQ)
        pe.wait_ge(k.xn_ready, DC * (r + 1))
        for n in range(24):
            tiles.wait_free(pe, n)
            wait_packet(k, pe, p0 + n)
            if n < 16:
                mm_packet(k, pe, p0 + n, xn, ps[:, n % 4, 0:SEQ]).then_inc(k.tile_done, 1)
            else:
                wt = slot_of(k, p0 + n).rearrange("p (c m) -> p c m", c=DC)
                for t in range(2):
                    for c in range(DC):
                        last = pe.matmul(ps[:, n % 4, t * P:(t + 1) * P], xn[:, c, t * P:(t + 1) * P], wt[:, c, :],
                                         start=(c == 0), stop=(c == DC - 1))
                last.then_inc(k.tile_done, 1)
        tiles.wait_emptied(pe, 7)
        tiles.wait_emptied(pe, 23)
        for h in range(SB_H + 2):
            if h < SB_H:
                b = ps[:, 4 + h % 2, :]
                lo = SB_D * (h % 2)
                kt, qt = ks[lo:lo + SB_D, h // 2, :], qs[lo:lo + SB_D, h // 2, :]
                if h >= 2:
                    pe.wait_ge(k.sb_exp, h - 1)
                pe.matmul(b[:, 0:SEQ], kt[:, 0:P], qt, start=True, stop=False, skip_group_check=True)
                pe.matmul(b[:, SEQ:N3], kt[:, P:SEQ], qt[:, P:SEQ], start=False, stop=False, skip_group_check=True
                          ).then_inc(k.sb_z, 1)
            if 1 <= h <= SB_H:
                g = h - 1
                b, s = ps[:, 4 + g % 2, :], spl[:, g % 2, :]
                pe.wait_ge(k.sb_sp, g + 1)
                pe.matmul(b[:, 0:SEQ], k.neg_tri, s[:, 0:SEQ], start=False, stop=False, skip_group_check=True)
                pe.matmul(b[:, P:SEQ], k.neg_ones, s[:, SEQ:N3], start=False, stop=False, skip_group_check=True)
                pe.matmul(b[:, SEQ:N3], k.neg_tri, s[:, SEQ:N3], start=False, stop=True, skip_group_check=True
                          ).then_inc(k.sb_log, 1)
            if h >= 2:
                g = h - 2
                pe.wait_ge(k.sb_w, g + 1)
                if g >= 4 and g % 2 == 0:
                    pe.wait_ge(k.mix_ready, k.mixes + g // 2 - 1)
                lo = SB_D * (g % 2)
                b = ps[lo:lo + SB_D, 6 + (g // 2) % 2, :]
                v = lambda t: vt[:, t, g * SB_D:(g + 1) * SB_D]
                pe.matmul(b[:, 0:SEQ], v(0), w[:, g % 2, 0:SEQ], start=True, stop=False, skip_group_check=True)
                pe.matmul(b[:, P:SEQ], v(1), w[:, g % 2, SEQ:N3], start=False, stop=True, skip_group_check=True
                          ).then_inc(k.sb_av, 1)

    k.mixes += 8
    add_projection(k, block, AT["sb_out"], ot, k.mix_ready, k.mixes)
    k.arena.at = mark


def final_of_first(k, block, gain):
    x = k.x[:, :, META:TOK]
    r = k.norms
    k.norms += 1
    block.scalar(lambda act: norm_act(k, act, r, x, SEQ))
    block.tensor(lambda pe: norm_pe(k, pe, r, SEQ))

    @block.vector
    def _(dve):
        norm_dve(k, dve, r, x, x, gain, SEQ)

    all_end(k, block)


def input_projection(k, block, gain):
    ps = k.ps
    r = k.norms
    k.norms += 1
    p0 = AT["w_in"]
    tiles = Tiles(k, ["D"] * 12 + ["A"] * 24)

    @block.scalar
    def _(act):
        norm_act(k, act, r, k.x, TOK)
        for n in range(12, 36):
            act.wait_ge(k.tile_done, p0 + n + 1)
            act.activation(k.sig[:, n - 12, :], ps[:, n % 4, 0:SEQ], ACT.Sigmoid).then_inc(k.act_emptied, 1)

    @block.vector
    def _(dve):
        k.dve(dve.memset(k.xm[:, :, 0:3], 0.0))
        norm_dve(k, dve, r, k.x, k.xn, gain, TOK)
        for n in range(12):
            dve.wait_ge(k.tile_done, p0 + n + 1)
            dst = k.u[:, n, :] if n < 4 else k.xm[:, n - 4, 3:3 + TOK]
            dve.tensor_copy(dst, ps[:, n % 4, 0:TOK]).then_inc(k.dve_emptied, 1)

    @block.tensor
    def _(pe):
        norm_pe(k, pe, r, TOK)
        pe.wait_ge(k.xn_ready, DC * (r + 1))
        for n in range(36):
            tiles.wait_free(pe, n)
            wait_packet(k, pe, p0 + n)
            if n < 12:
                mm_packet(k, pe, p0 + n, k.xn, ps[:, n % 4, 0:TOK]).then_inc(k.tile_done, 1)
            else:
                mm_packet(k, pe, p0 + n, k.xn[:, :, META:TOK], ps[:, n % 4, 0:SEQ]).then_inc(k.tile_done, 1)

    all_end(k, block)


def state_space(k, block):
    ps, sm = k.ps, k.small
    mark = k.arena.at
    take = k.arena.take
    v, g, hh = take(2, 2, TOK), take(2, 2, TOK), take(2, 2, TOK)
    t4 = take(4, TOK)
    t5 = take(4, TOK)
    y, yg = take(4, SEQ), take(4, SEQ)
    bre = sm["b_re"].rearrange("p (j m) -> p j m", j=4)
    bim = sm["b_im"].rearrange("p (j m) -> p j m", j=4)
    cre = sm["c_re"].rearrange("p (c m) -> p c m", c=S5_C)
    cim = sm["c_im"].rearrange("p (c m) -> p c m", c=S5_C)
    ec, es = k.s5_ec, k.s5_es
    pg, po = AT["s5_glu"], AT["s5_out"]

    @block.scalar
    def _(act):
        for j in range(4):
            act.wait_ge(k.s5_y, j + 1)
            act.activation(y[:, j, :], y[:, j, :], ACT.Gelu_apprx_tanh).then_inc(k.s5_gelu, 1)
        for j in range(4):
            act.wait_ge(k.tile_done, pg + j // 2 + 1)
            act.activation(yg[:, j, :], ps[:, j, 0:SEQ], ACT.Sigmoid, bias=sm["b_glu"][:, j:j + 1]
                           ).then_inc(k.s5_sig, 1)

    @block.vector
    def _(dve):
        for c in range(S5_C):
            b = c % 2
            br, bi = ps[:, 2 * b, 0:TOK], ps[:, 2 * b + 1, 0:TOK]
            dve.wait_ge(k.s5_bu, c + 1)
            k.dve(dve.tensor_tensor(t4[:, 0, :], br, ec[:, c, :], ALU.mult))
            k.dve(dve.tensor_tensor(t4[:, 1, :], bi, es[:, c, :], ALU.mult))
            k.dve(dve.tensor_tensor(t4[:, 2, :], bi, ec[:, c, :], ALU.mult))
            dve.tensor_tensor(t4[:, 3, :], br, es[:, c, :], ALU.mult).then_inc(k.s5_bu_used, 1)
            k.dve.settle(dve)
            dve.wait_ge(k.s5_bu_used, c + 1)
            k.dve(dve.tensor_tensor(v[:, b, 0, :], t4[:, 0, :], t4[:, 1, :], ALU.add))
            k.dve(dve.tensor_tensor(v[:, b, 1, :], t4[:, 2, :], t4[:, 3, :], ALU.subtract))
            k.dve.settle(dve)
            rr = k.s5_r[:, c:c + 1].to_broadcast([P, TOK])
            for i in range(2):
                k.dve(dve.tensor_tensor_scan(g[:, b, i, :], rr, v[:, b, i, :], 0.0, ALU.mult, ALU.add))
            k.dve.settle(dve)
            k.dve(dve.tensor_tensor(t5[:, 0, :], g[:, b, 0, :], ec[:, c, :], ALU.mult))
            k.dve(dve.tensor_tensor(t5[:, 1, :], g[:, b, 1, :], es[:, c, :], ALU.mult))
            k.dve(dve.tensor_tensor(t5[:, 2, :], g[:, b, 0, :], es[:, c, :], ALU.mult))
            k.dve(dve.tensor_tensor(t5[:, 3, :], g[:, b, 1, :], ec[:, c, :], ALU.mult))
            k.dve.settle(dve)
            if c >= 2:
                dve.wait_ge(k.s5_cu, c - 1)
            k.dve(dve.tensor_tensor(hh[:, b, 0, :], t5[:, 0, :], t5[:, 1, :], ALU.subtract))
            dve.scalar_tensor_tensor(out=hh[:, b, 1, :], in0=t5[:, 2, :], scalar=-1.0, in1=t5[:, 3, :],
                                     op0=ALU.mult, op1=ALU.subtract).then_inc(k.s5_h, 1)
            if c % 4 == 3:
                j = c // 4
                dve.wait_ge(k.s5_cu, c + 1)
                dve.scalar_tensor_tensor(out=y[:, j, :], in0=k.u[:, j, META:TOK], scalar=sm["s5_d"][:, j:j + 1],
                                         in1=ps[:, 4 + j, 0:SEQ], op0=ALU.mult, op1=ALU.add).then_inc(k.s5_y, 1)
        for j in range(4):
            dve.wait_ge(k.s5_sig, j + 1)
            dve.tensor_tensor(yg[:, j, :], yg[:, j, :], y[:, j, :], ALU.mult).then_inc(k.s5_yg, 1)
        for n in range(8):
            dve.wait_ge(k.tile_done, po + n // 2 + 1)
            s = k.sig[:, 8 + n, :]
            dve.tensor_tensor(s, s, ps[:, n, 0:SEQ], ALU.mult)

    @block.tensor
    def _(pe):
        def bu(c):
            b, j, lo = c % 2, c // 4, 32 * (c % 4)
            if c >= 2:
                pe.wait_ge(k.s5_bu_used, c - 1)
            pe.matmul(ps[:, 2 * b, 0:TOK], bre[lo:lo + 32, j, :], k.u[lo:lo + 32, j, :], start=True, stop=True,
                      tile_position=(lo, 0))
            pe.matmul(ps[:, 2 * b + 1, 0:TOK], bim[lo:lo + 32, j, :], k.u[lo:lo + 32, j, :], start=True, stop=True,
                      tile_position=(lo, 0)).then_inc(k.s5_bu, 1)

        bu(0)
        for c in range(S5_C):
            if c + 1 < S5_C:
                bu(c + 1)
            j, lo = c // 4, 32 * (c % 4)
            pe.wait_ge(k.s5_h, c + 1)
            for i, w in enumerate((cre, cim)):
                last = pe.matmul(ps[lo:lo + 32, 4 + j, 0:SEQ], w[:, c, :], hh[:, c % 2, i, META:TOK],
                                 start=(i == 0), stop=(i == 1), tile_position=(0, lo))
            last.then_inc(k.s5_cu, 1)
        pe.wait_ge(k.s5_gelu, 4)
        pe.wait_ge(k.s5_bu_used, S5_C)
        for n in range(2):
            wait_packet(k, pe, pg + n)
            for i in range(2):
                last = mm_packet(k, pe, pg + n, y, ps[:, 2 * n + i, 0:SEQ], kc=4, col=P * i)
            last.then_inc(k.tile_done, 1)
        pe.wait_ge(k.s5_yg, 4)
        pe.wait_ge(k.s5_y, 4)
        for n in range(4):
            wait_packet(k, pe, po + n)
            for i in range(2):
                last = mm_packet(k, pe, po + n, yg, ps[:, 2 * n + i, 0:SEQ], kc=4, col=P * i)
            last.then_inc(k.tile_done, 1)

    all_end(k, block)
    k.arena.at = mark


def mlstm(k, block):
    ps, sm = k.ps, k.small
    mark = k.arena.at
    take = k.arena.take
    xc = take(DC, TOK)
    qkv = take(3, DC, TOK)
    bd = take(3, DC, P)
    vt = take(3, D)
    gi, gf = take(TOK), take(TOK)
    az, cs, mx, bb = take(TOK), take(TOK), take(TOK), take(TOK)
    ccol = take(3, ML_H)
    em = take(2, SEQ)
    dm = take(2, 3, SEQ)
    sT = dm
    hz, hsq = take(2, 2 * SEQ), take(2, 2 * SEQ)
    den = take(2, SEQ)
    rms = take(2, SEQ)
    w_if = sm["w_if"].rearrange("p (c m) -> p c m", c=24)
    cw = sm["conv_w"].rearrange("p (c m) -> p c m", c=DC)
    spans = ((0, META), (META, P), (META + P, P))
    R = slice(0, ML_H)

    @block.scalar
    def _(act):
        for c in range(DC):
            act.wait_ge(k.ml_conv, c + 1)
            act.activation(xc[:, c, :], xc[:, c, :], ACT.Silu).then_inc(k.ml_xc, 1)
        for n in range(2 * DC):
            act.wait_ge(k.ml_qkv, n + 1)
            act.activation(qkv[:, n // DC, n % DC, :], ps[:, n % 4, 0:TOK], ACT.Copy).then_inc(k.act_emptied, 1)
        act.wait_ge(k.ml_gate, 1)
        act.activation(gi[R, :], ps[R, 4, 0:TOK], ACT.Identity, bias=k.b_if[:, 0:1]).then_inc(k.ml_act, 1)
        act.activation(gf[R, :], ps[R, 5, 0:TOK], ACT.Identity, bias=k.b_if[:, 1:2]).then_inc(k.ml_act, 1)
        act.wait_ge(k.ml_dve, 1)
        k.act(act.activation(az[R, :], az[R, :], ACT.Exp, scale=-1.0))
        k.act.settle(act)
        act.activation(az[R, :], az[R, :], ACT.Ln, bias=k.one_col[R, :]).then_inc(k.ml_act, 1)

        def decays(h):
            b = h % 2
            act.wait_ge(k.ml_mb, h + 1)
            if h >= 2:
                act.wait_ge(k.ml_den, h - 1)
            for s, (lo, n) in enumerate(spans):
                act.activation(dm[0:n, b, s, :], ps[0:n, b, 0:SEQ], ACT.Exp, bias=ccol[0:n, s, h:h + 1], scale=-1.0)
            act.activation(em[:, b, :], ps[:, b, SEQ:2 * SEQ], ACT.Exp, scale=-1.0).then_inc(k.ml_exp, 1)

        decays(0)
        decays(1)
        for h in range(ML_H):
            act.wait_ge(k.ml_hz, h + 1)
            if h >= 2:
                act.wait_ge(k.ml_ss, h - 1)
            act.activation(hsq[:, h % 2, :], hz[:, h % 2, :], ACT.Square).then_inc(k.ml_sq, 1)
            act.wait_ge(k.ml_ss, h + 1)
            act.activation(rms[:, h % 2, :], ps[:, 7, 0:SEQ], ACT.Sqrt, bias=k.eps, scale=1.0 / ML_D
                           ).then_inc(k.ml_rms, 1)
            if h + 2 < ML_H:
                decays(h + 2)

    @block.vector
    def _(dve):
        for c in range(DC):
            k.dve(dve.tensor_scalar(xc[:, c, :], k.xm[:, c, 0:TOK], cw[:, c, 0:1], sm["conv_b"][:, c:c + 1],
                                    ALU.mult, ALU.add))
            for j in range(1, 4):
                k.dve.settle(dve)
                i = dve.scalar_tensor_tensor(out=xc[:, c, :], in0=k.xm[:, c, j:j + TOK], scalar=cw[:, c, j:j + 1],
                                             in1=xc[:, c, :], op0=ALU.mult, op1=ALU.add)
                if j < 3:
                    k.dve(i)
            i.then_inc(k.ml_conv, 1)
        for m, name in enumerate(("wq", "wk", "wv")):
            for c in range(DC):
                w4 = sm[name][:, 4 * c:4 * c + 4]
                last = dve.tensor_tensor(bd[:, m, c, :].rearrange("p (n j) -> p n j", j=4), bcast(w4, 32),
                                         spread(k.block4, 4), ALU.mult)
            last.then_inc(k.ml_bd, 1)
        for c in range(DC):
            dve.wait_ge(k.ml_qkv, 2 * DC + c + 1)
            dve.tensor_copy(qkv[:, 2, c, :], ps[:, c % 4, 0:TOK]).then_inc(k.ml_vcopied, 1)
        for s, (lo, n) in enumerate(spans):
            for half in range(2):
                dve.wait_ge(k.ml_vt, 2 * s + half + 1)
                dve.tensor_copy(vt[0:n, s, half * 512:(half + 1) * 512], ps[0:n, 6 + half, :]).then_inc(k.ml_vtc, 1)
        dve.wait_ge(k.ml_act, 2)
        dve.scalar_tensor_tensor(out=az[R, :], in0=gf[R, :], scalar=-1.0, in1=gf[R, :], op0=ALU.mult, op1=ALU.max
                                 ).then_inc(k.ml_dve, 1)
        dve.wait_ge(k.ml_act, 3)
        k.dve(dve.scalar_tensor_tensor(out=gf[R, :], in0=gf[R, :], scalar=0.0, in1=az[R, :],
                                       op0=ALU.min, op1=ALU.subtract))
        k.dve.settle(dve)
        k.dve(dve.tensor_tensor_scan(bb[R, :], k.ones_row[R, 0:TOK], gf[R, :], 0.0, ALU.mult, ALU.add))
        k.dve.settle(dve)
        k.dve(dve.tensor_tensor(cs[R, :], gi[R, :], bb[R, :], ALU.subtract))
        k.dve.settle(dve)
        k.dve(dve.tensor_tensor_scan(mx[R, :], k.ones_row[R, 0:TOK], cs[R, :], 0.0, ALU.mult, ALU.max))
        k.dve.settle(dve)
        dve.tensor_tensor(bb[R, :], bb[R, :], mx[R, :], ALU.add).then_inc(k.ml_dve, 1)
        dve.wait_ge(k.ml_cc, 1)
        for s, (lo, n) in enumerate(spans):
            last = dve.tensor_copy(ccol[0:n, s, :], ps[0:n, 6, 16 * s:16 * s + ML_H])
        last.then_inc(k.ml_dve, 1)
        for h in range(ML_H):
            b = h % 2
            dve.wait_ge(k.ml_exp, h + 1)
            k.dve(dve.tensor_scalar(dm[0:META, b, 0, :], dm[0:META, b, 0, :], 1.0, None, ALU.min))
            dd = dm[:, b, 1, 0:P]
            k.dve(dve.scalar_tensor_tensor(out=dd, in0=dd, scalar=1.0, in1=k.keep_ge, op0=ALU.min, op1=ALU.mult))
            dd = dm[:, b, 1, P:SEQ]
            k.dve(dve.tensor_scalar(dd, dd, 1.0, None, ALU.min))
            dd = dm[:, b, 2, P:SEQ]
            k.dve(dve.scalar_tensor_tensor(out=dd, in0=dd, scalar=1.0, in1=k.keep_ge, op0=ALU.min, op1=ALU.mult))
            dve.wait_ge(k.ml_s, h + 1)
            if h >= 2:
                dve.wait_ge(k.ml_num, h - 1)
            k.dve.settle(dve)
            sc = ML_D ** -0.5
            dve.scalar_tensor_tensor(out=sT[0:META, b, 0, :], in0=ps[0:META, 2, SEQ:2 * SEQ], scalar=sc,
                                     in1=dm[0:META, b, 0, :], op0=ALU.mult, op1=ALU.mult)
            dve.scalar_tensor_tensor(out=sT[:, b, 1, :], in0=ps[:, 2, 0:SEQ], scalar=sc,
                                     in1=dm[:, b, 1, :], op0=ALU.mult, op1=ALU.mult)
            dve.scalar_tensor_tensor(out=sT[:, b, 2, P:SEQ], in0=ps[:, 3, 0:P], scalar=sc,
                                     in1=dm[:, b, 2, P:SEQ], op0=ALU.mult, op1=ALU.mult).then_inc(k.ml_sT, 1)
            dve.wait_ge(k.ml_num, h + 1)
            k.dve(dve.scalar_tensor_tensor(out=den[:, b, :], in0=ps[:, 6, 0:SEQ], scalar=-1.0, in1=em[:, b, :],
                                           op0=ALU.mult, op1=ALU.max))
            k.dve.settle(dve)
            dve.tensor_tensor(den[:, b, :], ps[:, 6, 0:SEQ], den[:, b, :], ALU.max).then_inc(k.ml_den, 1)
            dve.wait_ge(k.ml_den, h + 1)
            k.dve(dve.reciprocal(den[:, b, :], den[:, b, :]))
            k.dve.settle(dve)
            hv = hz[:, b, :].rearrange("p (e t) -> p e t", e=2)
            k.dve(dve.tensor_tensor(hv, k.sig[:, 2 * h:2 * h + 2, :], bcast(den[:, b, :], 2), ALU.mult))
            k.dve.settle(dve)
            dve.tensor_tensor(hz[:, b, :], ps[:, 4 + b, :], hz[:, b, :], ALU.mult).then_inc(k.ml_hz, 1)
            dve.wait_ge(k.ml_hz, h + 1)
            dve.wait_ge(k.ml_rms, h + 1)
            k.dve(dve.reciprocal(rms[:, b, :], rms[:, b, :]))
            k.dve.settle(dve)
            for e in range(2):
                c = 2 * h + e
                he = hz[:, b, e * SEQ:(e + 1) * SEQ]
                k.dve(dve.scalar_tensor_tensor(out=he, in0=he, scalar=sm["ml_g"][:, c:c + 1], in1=rms[:, b, :],
                                               op0=ALU.mult, op1=ALU.mult))
                k.dve.settle(dve)
                dve.scalar_tensor_tensor(out=k.sig[:, c, :], in0=xc[:, c, META:TOK],
                                         scalar=sm["ml_skip"][:, c:c + 1], in1=he,
                                         op0=ALU.mult, op1=ALU.add).then_inc(k.mix_ready, 1)

    @block.tensor
    def _(pe):
        for n in range(3 * DC):
            m, c = n // DC, n % DC
            if c == 0:
                pe.wait_ge(k.ml_bd, m + 1)
            if m < 2:
                pe.wait_ge(k.ml_xc, c + 1)
            if 4 <= n < 2 * DC + 4:
                pe.wait_ge(k.act_emptied, k.act_tiles + n - 3)
            elif n >= 4:
                pe.wait_ge(k.ml_vcopied, n - 3 - 2 * DC)
            src = xc[:, c, :] if m < 2 else k.xm[:, c, 3:3 + TOK]
            pe.matmul(ps[:, n % 4, 0:TOK], bd[:, m, c, :], src, start=True, stop=True).then_inc(k.ml_qkv, 1)
        for s, (lo, n) in enumerate(spans):
            for half in range(2):
                if s:
                    pe.wait_ge(k.ml_vtc, 2 * s + half - 1)
                for c in range(4 * half, 4 * half + 4):
                    last = pe.matmul(ps[0:n, 6 + half, (c % 4) * P:(c % 4 + 1) * P], k.xm[:, c, 3 + lo:3 + lo + n],
                                     bd[:, 2, c, :], start=True, stop=True)
                last.then_inc(k.ml_vt, 1)
        pe.wait_ge(k.ml_vcopied, DC)
        pe.wait_ge(k.act_emptied, k.act_tiles + 2 * DC)
        for g in range(2):
            for c in range(24):
                last = pe.matmul(ps[R, 4 + g, 0:TOK], w_if[:, c, 4 * g:4 * g + 4], qkv[:, c // DC, c % DC, :],
                                 start=(c == 0), stop=(c == 23))
        last.then_inc(k.ml_gate, 1)
        pe.wait_ge(k.ml_dve, 2)
        pe.wait_ge(k.ml_vtc, 6)
        for s, (lo, n) in enumerate(spans):
            last = pe.matmul(ps[0:n, 6, 16 * s:16 * s + ML_H], cs[R, lo:lo + n], k.ident[R, R], start=True, stop=True)
        last.then_inc(k.ml_cc, 1)
        pe.wait_ge(k.ml_dve, 3)
        pe.wait_ge(k.ml_act, 3)

        def stab(h):
            if h >= 2:
                pe.wait_ge(k.ml_exp, h - 1)
            hr = k.head_row[R, h, :]
            pe.matmul(ps[:, h % 2, 0:SEQ], hr, mx[R, META:TOK], start=True, stop=True)
            pe.matmul(ps[:, h % 2, SEQ:2 * SEQ], hr, bb[R, META:TOK], start=True, stop=True).then_inc(k.ml_mb, 1)

        stab(0)
        stab(1)
        for h in range(ML_H):
            b = h % 2
            q = lambda e, lo, hi: qkv[:, 0, 2 * h + e, lo:hi]
            kk = lambda e, s: qkv[:, 1, 2 * h + e, spans[s][0]:spans[s][0] + spans[s][1]]
            if h >= 1:
                pe.wait_ge(k.ml_sT, h)
            for e in range(2):
                pe.matmul(ps[:, 2, 0:SEQ], kk(e, 1), q(e, META, TOK), start=(e == 0), stop=(e == 1))
            for e in range(2):
                pe.matmul(ps[0:META, 2, SEQ:2 * SEQ], kk(e, 0), q(e, META, TOK), start=(e == 0), stop=(e == 1))
            for e in range(2):
                last = pe.matmul(ps[:, 3, 0:P], kk(e, 2), q(e, META + P, TOK), start=(e == 0), stop=(e == 1))
            last.then_inc(k.ml_s, 1)
            pe.wait_ge(k.ml_sT, h + 1)
            if h >= 1:
                pe.wait_ge(k.ml_hz, h)
            for e in range(2):
                o = ps[:, 4 + b, e * SEQ:(e + 1) * SEQ]
                v = lambda s: vt[0:spans[s][1], s, h * ML_D + e * P:h * ML_D + (e + 1) * P]
                pe.matmul(o, v(1), sT[:, b, 1, :], start=True, stop=False, skip_group_check=True)
                pe.matmul(o, v(0), sT[0:META, b, 0, :], start=False, stop=False, skip_group_check=True)
                pe.matmul(o[:, P:SEQ], v(2), sT[:, b, 2, P:SEQ], start=False, stop=True, skip_group_check=True)
            o = ps[:, 6, 0:SEQ]
            pe.matmul(o, k.ones, sT[:, b, 1, :], start=True, stop=False, skip_group_check=True)
            pe.matmul(o, k.ones[0:META, :], sT[0:META, b, 0, :], start=False, stop=False, skip_group_check=True)
            pe.matmul(o[:, P:SEQ], k.ones, sT[:, b, 2, P:SEQ], start=False, stop=True, skip_group_check=True
                      ).then_inc(k.ml_num, 1)
            if h + 2 < ML_H:
                stab(h + 2)
            pe.wait_ge(k.ml_sq, h + 1)
            if h >= 1:
                pe.wait_ge(k.ml_rms, h)
            for e in range(2):
                last = pe.matmul(ps[:, 7, 0:SEQ], k.ones, hsq[:, b, e * SEQ:(e + 1) * SEQ], start=(e == 0), stop=(e == 1))
            last.then_inc(k.ml_ss, 1)

    k.act_tiles += 2 * DC
    k.mixes += 2 * ML_H
    all_end(k, block)
    k.arena.at = mark


def mix_out(k, block):
    tiles = Tiles(k, ["D"] * 8)
    packet = AT["ml_out"]
    ps = k.ps

    @block.tensor
    def _(pe):
        for n in range(8):
            tiles.wait_free(pe, n)
            wait_packet(k, pe, packet + n)
            mm_packet(k, pe, packet + n, k.sig[:, 0:8, :], ps[:, n % 4, 0:SEQ]).then_inc(k.tile_done, 1)

    @block.vector
    def _(dve):
        for n in range(8):
            dve.wait_ge(k.tile_done, packet + n + 1)
            g, s = k.sig[:, 16 + n, :], k.sig[:, 8 + n, :]
            dve.tensor_tensor(g, g, ps[:, n % 4, 0:SEQ], ALU.mult).then_inc(k.dve_emptied, 1)
        dve.wait_ge(k.dve_emptied, tiles.base[0] + 8)
        dve.tensor_tensor(k.sig[:, 8:16, :], k.sig[:, 8:16, :], k.sig[:, 16:24, :], ALU.add).then_inc(k.mix_ready, 1)

    k.mixes += 1
    add_projection(k, block, AT["w_out"], k.sig[:, 8:16, :], k.mix_ready, k.mixes)


def peer_route(k, block, gain, glast):
    ps, sm = k.ps, k.small
    x, xn = k.x[:, :, META:TOK], k.xn[:, :, 0:SEQ]
    r = k.norms
    k.norms += 1
    mark = k.arena.at
    take = k.arena.take
    qT = take(16, SEQ)
    sc = take(2, 16, P)
    wk = take(256)
    val = take(16, PE_K)
    idx = take(16, PE_K).bitcast(U32)
    idf = take(16, PE_K)
    cand = take(PE_H, 256)
    cv = take(PE_H, PE_K)
    ci = take(PE_H, PE_K).bitcast(U32)
    ab = take(2, HK).bitcast(U32)
    abf = take(2, HK)
    one = take(HK, PE_K)
    sel = take(2, HK)
    nm = take(PE_H)
    p0, pk = AT["peer_q"], AT["peer_keys"]
    tiles = Tiles(k, ["A"] * 16)

    @block.scalar
    def _(act):
        act.dma_start(k.glast_row[0:1, :], glast).then_inc(k.glast_in, 16)
        norm_act(k, act, r, x, SEQ)
        for n in range(16):
            act.wait_ge(k.tile_done, p0 + n + 1)
            act.activation(qT[:, n, :], ps[:, n % 4, 0:SEQ], ACT.Copy).then_inc(k.act_emptied, 1)
        for n in range(8):
            act.wait_ge(k.pr_s, n + 1)
            act.activation(sc[:, n % 2, 4 * (n // 2):4 * (n // 2) + 4, :], ps[:, n % 4, :].rearrange("p (a b) -> p a b", a=4),
                           ACT.Copy).then_inc(k.pr_sc, 1)
        for n in range(8):
            act.wait_ge(k.pr_t, n + 1)
            dst = (k.xt, k.ht)[n // 4]
            act.activation(dst[:, (n % 4) // 2, (n % 2) * 512:(n % 2 + 1) * 512], ps[:, 4 + n % 4, :], ACT.Copy
                           ).then_inc(k.pr_tc, 1)
        for n in range(2):
            act.wait_ge(k.pr_g, n + 1)
            act.activation(k.gate[:, n, :], k.gate[:, n, :], ACT.Exp).then_inc(k.pr_e, 1)
        act.wait_ge(k.pr_gl, 1)
        act.activation(k.glast, ps[:, 0:2, :], ACT.Copy)

    @block.vector
    def _(dve):
        norm_dve(k, dve, r, x, xn, gain, SEQ)
        k.dve(dve.memset(k.expert[:, 4 * HK:], 0))
        dve.wait_ge(k.pr_sc, 8)

        def run(i):
            k.dve(i)
            k.dve.settle(dve)

        def top16(values, scratch, v, ix):
            run(dve.max(v[:, 0:8], values))
            run(dve.max_index(ix[:, 0:8], v[:, 0:8], values))
            run(dve.match_replace(scratch, v[:, 0:8], values, -3e38))
            run(dve.max(v[:, 8:16], scratch))
            run(dve.max_index(ix[:, 8:16], v[:, 8:16], scratch))

        for t in range(2):
            for n in range(16):
                top16(sc[:, t, n, :], wk[:, 0:P], val[:, n, :], idx[:, n, :])
            run(dve.tensor_copy(idf, idx))
            v2 = val.rearrange("p (h i) k -> p h i k", i=2)
            for h in range(PE_H):
                k.dve(dve.tensor_tensor(cand[:, h, :].rearrange("p (a b) -> p a b", a=16), spread(v2[:, h, 0, :], 16),
                                        bcast(v2[:, h, 1, :], 16), ALU.add))
            k.dve.settle(dve)
            for h in range(PE_H):
                top16(cand[:, h, :], wk, cv[:, h, :], ci[:, h, :])
            cif = ci.rearrange("p h k -> p (h k)")
            run(dve.tensor_scalar(ab[:, 0, :], cif, 4, None, ALU.logical_shift_right))
            run(dve.tensor_scalar(ab[:, 1, :], cif, 15, None, ALU.bitwise_and))
            run(dve.tensor_copy(abf, ab))
            f2 = idf.rearrange("p (h i) k -> p h i k", i=2)
            for i in range(2):
                for h in range(PE_H):
                    o = one[:, h * 16:(h + 1) * 16, :]
                    k.dve(dve.tensor_tensor(o, spread(abf[:, i, h * 16:(h + 1) * 16], 16), k.iota16, ALU.is_equal))
                    k.dve.settle(dve)
                    k.dve(dve.tensor_tensor(o, o, bcast(f2[:, h, i, :], 16), ALU.mult))
                k.dve.settle(dve)
                run(dve.tensor_reduce(sel[:, i, :], one, AX_X, ALU.add))
            run(dve.scalar_tensor_tensor(out=sel[:, 0, :], in0=sel[:, 0, :], scalar=float(PE_N), in1=sel[:, 1, :],
                                         op0=ALU.mult, op1=ALU.add))
            for ph in (t, t + 2):
                k.dve(dve.tensor_copy(k.expert[:, ph * HK:(ph + 1) * HK], sel[:, 0, :]))
            g = k.gate[:, t, :].rearrange("p (h k) -> p h k", h=PE_H)
            dve.tensor_tensor(g, cv, cv[:, :, 0:1].to_broadcast([P, PE_H, PE_K]), ALU.subtract).then_inc(k.pr_g, 1)
            dve.wait_ge(k.pr_e, t + 1)
            run(dve.tensor_reduce(nm, g, AX_X, ALU.add))
            run(dve.reciprocal(nm, nm))
            run(dve.tensor_tensor(g, g, spread(nm, PE_K), ALU.mult))

    @block.tensor
    def _(pe):
        norm_pe(k, pe, r, SEQ)
        pe.wait_ge(k.xn_ready, DC * (r + 1))
        for n in range(16):
            tiles.wait_free(pe, n)
            wait_packet(k, pe, p0 + n)
            mm_packet(k, pe, p0 + n, xn, ps[:, n % 4, 0:SEQ]).then_inc(k.tile_done, 1)
        tiles.wait_emptied(pe, 15)
        for n in range(8):
            j, t = n // 2, n % 2
            if n >= 4:
                pe.wait_ge(k.pr_sc, n - 3)
            if j % 2 == 0 and t == 0:
                wait_packet(k, pe, pk + j // 2)
            for i in range(4):
                hi = 4 * j + i
                last = pe.matmul(ps[:, n % 4, i * P:(i + 1) * P], qT[:, hi, t * P:(t + 1) * P],
                                 slot_of(k, pk + j // 2)[:, (hi % 8) * P:(hi % 8 + 1) * P], start=True, stop=True)
            last.then_inc(k.pr_s, 1)
        pe.wait_ge(k.rms_ready, r + 1)
        for n in range(8):
            if n >= 4:
                pe.wait_ge(k.pr_tc, n - 3)
            src = (x, xn)[n // 4]
            t, half = (n % 4) // 2, n % 2
            for i in range(4):
                last = pe.transpose(ps[:, 4 + n % 4, i * P:(i + 1) * P], src[:, 4 * half + i, t * P:(t + 1) * P], k.ident)
            last.then_inc(k.pr_t, 1)
        pe.wait_ge(k.pr_sc, 8)
        pe.wait_ge(k.glast_in, 16)
        for i in range(2):
            last = pe.matmul(ps[:, i, :], k.ones[0:1, :], k.glast_row[0:1, i * 512:(i + 1) * 512], start=True, stop=True)
        last.then_inc(k.pr_gl, 1)

    all_end(k, block)
    k.arena.at = mark


def peer_experts(k, block, u_tab, v_tab, out):
    mark = k.arena.at
    take = k.arena.take
    NS = PE_SLOTS
    rows = take(NS, D)
    ids = take(2, NS).bitcast(U32)
    dots, w8 = take(2, NS), take(NS)
    acts = take(2, HK)
    acc = take(2, D)
    ssq, rms = take(2), take(2)
    turns = HK // NS

    @block.gpsimd
    def _(pool):
        for ph in range(4):
            tab = (u_tab, v_tab)[ph // 2]
            with pool.Fori(0, turns // 2) as i:
                for half in range(2):
                    pool.wait_ge(k.px_ids, i * 2 + (turns * ph + half + 1))
                    for s in range(NS):
                        pool.wait_ge(k.px_free, i * (2 * NS) + (NS * (turns * ph + half) + s + 1))
                        pool.sem_inc(k.px_go, 1)
                        pool.indirect_dma_start(rows[:, s, :], None, tab,
                                                bass.IndirectOffsetOnAxis(ap=ids[:, half, s:s + 1], axis=0)
                                                ).then_inc(k.px_in[s], 16)

    @block.vector
    def _(dve):
        for s in range(NS):
            dve.memset(dots[:, 0, s:s + 1], 0.0).then_inc(k.px_free, 1)
        dve.tensor_copy(ids[:, 0, :], k.expert[:, 0:NS]).then_inc(k.px_ids, 1)
        for ph in range(4):
            t = ph % 2
            for_v = ph >= 2
            if for_v:
                dve.wait_ge(k.px_gelu, t + 1)
                k.dve(dve.tensor_tensor(acts[:, t, :], acts[:, t, :], k.gate[:, t, :], ALU.mult))
                k.dve(dve.memset(acc[:, t, :], 0.0))
                k.dve.settle(dve)
            with dve.Fori(0, turns // 2) as i:
                for half in range(2):
                    used = lambda n: i * (2 * NS) + (NS * (turns * ph + half + 1) + n)
                    dve.tensor_copy(ids[:, 1 - half, :],
                                    k.expert[:, bass.ds(i * (2 * NS) + (ph * HK + (half + 1) * NS), NS)]
                                    ).then_inc(k.px_ids, 1)
                    if for_v:
                        dve.tensor_copy(w8, acts[:, t, bass.ds(i * (2 * NS) + half * NS, NS)]).then_inc(k.px_w, 1)
                        dve.wait_ge(k.px_w, i * 2 + ((ph - 2) * turns + half + 1))
                    for s in range(NS):
                        dve.wait_ge(k.px_in[s], i * 32 + 16 * (ph * turns + half + 1))
                        if for_v:
                            if s:
                                dve.wait_ge(k.px_free, used(s))
                            dve.scalar_tensor_tensor(out=acc[:, t, :], in0=rows[:, s, :], scalar=w8[:, s:s + 1],
                                                     in1=acc[:, t, :], op0=ALU.mult, op1=ALU.add
                                                     ).then_inc(k.px_free, 1)
                        else:
                            dve.tensor_tensor_reduce(rows[:, s, :], rows[:, s, :], k.ht[:, t, :], 1.0, 0.0, ALU.mult, ALU.add,
                                                     dots[:, half, s:s + 1]).then_inc(k.px_free, 1)
                    dve.wait_ge(k.px_free, used(NS))
                    if not for_v:
                        dve.tensor_copy(acts[:, t, bass.ds(i * (2 * NS) + half * NS, NS)], dots[:, half, :]).then_inc(k.px_dots, 1)
        dve.tensor_tensor(acc, acc, k.xt, ALU.add).then_inc(k.px_acc, 1)
        dve.wait_ge(k.px_rms, 2)
        k.dve(dve.reciprocal(rms, rms))
        k.dve.settle(dve)
        for t in range(2):
            dve.scalar_tensor_tensor(out=acc[:, t, :], in0=acc[:, t, :], scalar=rms[:, t:t + 1],
                                     in1=k.glast.rearrange("p a b -> p (a b)"), op0=ALU.mult, op1=ALU.mult
                                     ).then_inc(k.px_out, 1)

    @block.scalar
    def _(act):
        for t in range(2):
            act.wait_ge(k.px_dots, turns * (t + 1))
            act.activation(acts[:, t, :], acts[:, t, :], ACT.Gelu_apprx_tanh).then_inc(k.px_gelu, 1)
        act.wait_ge(k.px_acc, 1)
        for t in range(2):
            k.act(act.activation(rows[:, t, :], acc[:, t, :], ACT.Square, accum_out=ssq[:, t:t + 1]))
        k.act.settle(act)
        for t in range(2):
            act.activation(rms[:, t:t + 1], ssq[:, t:t + 1], ACT.Sqrt, bias=k.eps, scale=1.0 / D).then_inc(k.px_rms, 1)
        for t in range(2):
            act.wait_ge(k.px_out, t + 1)
            act.dma_start(out[t * P:(t + 1) * P, :], acc[:, t, :]).then_inc(k.stored, 16)
        act.wait_ge(k.stored, 32)

    k.arena.at = mark


class Shared:
    pass


def name_semaphores(k, sem):
    (k.sq_ready, k.ss_ready, k.rms_ready, k.xn_ready, k.silu_ready, k.h_ready, k.tile_done,
     k.dve_emptied, k.act_emptied, k.small_in, k.mix_ready, k.stored, k.glast_in) = (
        sem(n) for n in """sq_ready ss_ready rms_ready xn_ready silu_ready h_ready
        tile_done dve_emptied act_emptied small_in mix_ready stored glast_in""".split())
    (k.gla_pe, k.gla_act, k.gla_dve, k.gla_qk, k.gla_s, k.gla_st, k.gla_o, k.gla_copied, k.gla_sq,
     k.gla_ss, k.gla_rms) = (
        sem(n) for n in """gla_pe gla_act gla_dve gla_qk gla_s gla_st gla_o
        gla_copied gla_sq gla_ss gla_rms""".split())
    (k.sb_z, k.sb_ln, k.sb_sp, k.sb_log, k.sb_exp, k.sb_w, k.sb_av) = (
        sem(n) for n in """sb_z sb_ln sb_sp sb_log sb_exp sb_w sb_av""".split())
    (k.s5_act, k.s5_er, k.s5_th, k.s5_mod_ready, k.s5_inv_ready, k.s5_bu, k.s5_bu_used, k.s5_h,
     k.s5_cu, k.s5_y, k.s5_gelu, k.s5_sig, k.s5_yg) = (
        sem(n) for n in """s5_act s5_er s5_th s5_mod_ready s5_inv_ready s5_bu
        s5_bu_used s5_h s5_cu s5_y s5_gelu s5_sig s5_yg""".split())
    (k.ml_conv, k.ml_xc, k.ml_bd, k.ml_qkv, k.ml_vcopied, k.ml_vt, k.ml_vtc, k.ml_gate, k.ml_act,
     k.ml_dve, k.ml_cc, k.ml_mb, k.ml_exp, k.ml_s, k.ml_sT, k.ml_num, k.ml_den, k.ml_hz, k.ml_sq,
     k.ml_ss, k.ml_rms) = (
        sem(n) for n in """ml_conv ml_xc ml_bd ml_qkv ml_vcopied ml_vt ml_vtc
        ml_gate ml_act ml_dve ml_cc ml_mb ml_exp ml_s ml_sT ml_num ml_den ml_hz
        ml_sq ml_ss ml_rms""".split())
    (k.pr_s, k.pr_sc, k.pr_t, k.pr_tc, k.pr_g, k.pr_e, k.pr_gl) = (
        sem(n) for n in """pr_s pr_sc pr_t pr_tc pr_g pr_e pr_gl""".split())
    (k.px_ids, k.px_free, k.px_go, k.px_w, k.px_dots, k.px_gelu, k.px_acc, k.px_rms, k.px_out) = (
        sem(n) for n in """px_ids px_free px_go px_w px_dots px_gelu px_acc px_rms
        px_out""".split())


def build_program(nc, ins, out, upto=99, probe=None):
    with ExitStack() as ctx:
        k = Shared()
        name_semaphores(k, lambda n: ctx.enter_context(nc.semaphore(n)))
        width = 40000
        k.arena = Arena(ctx.enter_context(nc.sbuf_tensor("arena", [P, width], F32)), width)
        k.ring = ctx.enter_context(nc.sbuf_tensor("ring", [P, RING, D], F32))
        k.ps = ctx.enter_context(nc.psum_tensor("ps", [P, 8, 512], F32))
        k.zero_bf = ctx.enter_context(nc.sbuf_tensor("zero_bf", [P, 512], BF16))[:, :]
        k.w_gk2 = ctx.enter_context(nc.sbuf_tensor("w_gk2_sb", [GLA_RANK, GLA_H * P], F32))
        k.b_if = ctx.enter_context(nc.sbuf_tensor("b_if_sb", [ML_H, 2], F32))
        k.landed = [ctx.enter_context(nc.semaphore(f"landed{s}")) for s in range(RING)]
        k.px_in = [ctx.enter_context(nc.semaphore(f"px_in{s}")) for s in range(8)]
        k.stage_sem = {e: ctx.enter_context(nc.semaphore(f"stage_{e}")) for e in ("pe", "act", "dve", "pool")}
        k.stage = {e: 0 for e in k.stage_sem}
        k.dve = Counted(ctx.enter_context(nc.semaphore("dve_steps")))
        k.act = Counted(ctx.enter_context(nc.semaphore("act_steps")))
        k.pool = Counted(ctx.enter_context(nc.semaphore("pool_steps")))
        k.norms = k.mixes = k.dve_tiles = k.act_tiles = 0

        take = k.arena.take
        k.x, k.xn = take(DC, TOK), take(DC, TOK)
        k.small_all = take(SMALL_W)
        k.small = {n: k.small_all[:, a:a + w] for n, (a, w) in SMALL.items()}
        k.rms, k.rstd = take(TOK), take(TOK)
        k.ones, k.neg_ones, k.ident = take(P), take(P), take(P)
        k.keep_ge, k.keep_gt, k.neg_tri = take(P), take(P), take(P)
        k.head_row, k.block4 = take(ML_H, P)[0:ML_H], take(32)
        k.iota16 = take(16, 16)
        k.eps, k.one_col = take(1), take(1)
        k.s5_r = take(S5_C)
        k.ones_row = take(TOK)
        k.small_loads = [
            (k.x[:, :, META:TOK], ins["xT"]),
            (k.x[:, :, 0:META], ins["metaT"]),
            (k.small_all, ins["small"]),
            (k.w_gk2[:, :], ins["w_gk2"]),
            (k.b_if[:, :], ins["b_if"]),
        ]
        low = k.arena.at
        k.s5_ec, k.s5_es = take(S5_C, TOK), take(S5_C, TOK)
        tables = k.arena.at
        k.sq = take(DC, TOK)
        k.gate_s, k.h = take(2, SEQ), take(2, SEQ)
        shared = k.arena.at
        k.s5_dt, k.s5_ere, k.s5_theta, k.s5_sin, k.s5_half, k.s5_cos = (take(S5_C) for _ in range(6))
        k.s5_mod, k.s5_mod2, k.s5_inv, k.s5_cre, k.s5_cim = (take(S5_C) for _ in range(5))
        k.s5_tmp = [take(S5_C) for _ in range(6)]
        k.s5_big = [take(S5_C, P) for _ in range(4)]

        block = ctx.enter_context(nc.Block())
        weights_in(k, block, ins["wstream"])
        setup(k, block)
        s5_tables(k, block)
        feed_forward(k, block, 0, GAIN["ffn1_0"], AT["ffn0"])
        k.arena.at = shared
        if upto >= 2:
            gated_linear_attention(k, block, GAIN["mix_0"])
        if upto >= 3:
            feed_forward(k, block, 1, GAIN["ffn2_0"], AT["ffn1"])
        if upto >= 4:
            feed_forward(k, block, 2, GAIN["ffn1_1"], AT["ffn2"])
            stick_breaking(k, block, GAIN["mix_1"])
        if upto >= 5:
            feed_forward(k, block, 3, GAIN["ffn2_1"], AT["ffn3"])
            final_of_first(k, block, GAIN["final"])
        top = width - 4 * TOK - DC * (TOK + 3) - 24 * SEQ
        k.arena.at = top
        if upto >= 6:
            k.u, k.xm = take(4, TOK), take(DC, TOK + 3)
            k.sig = take(24, SEQ)
            k.arena.at, k.arena.width = tables + DC * TOK, top
            input_projection(k, block, GAIN["norm1"])
            state_space(k, block)
        if upto >= 7:
            k.arena.at, k.arena.width = low, top + 4 * TOK
            mlstm(k, block)
            k.arena.width = width
        if upto >= 8:
            mix_out(k, block)
        if upto >= 9:
            k.arena.at = low
            k.xt, k.ht = take(2, D), take(2, D)
            k.expert = take(4 * HK + PE_SLOTS).bitcast(U32)
            k.gate = take(2, HK)
            k.glast, k.glast_row = take(2, 512), take(D)
            k.sq = take(DC, TOK)
            peer_route(k, block, GAIN["norm2"], ins["glast"])
            peer_experts(k, block, ins["u_tab"], ins["v_tab"], out)
        else:
            probe(k, block)




def lay_out(a):
    a = {n: np.asarray(v) for n, v in a.items()}

    def columns(w, width=P):
        kc = w.shape[0] // P
        w = w.reshape(kc, P, w.shape[1] // width, width).transpose(2, 1, 0, 3)
        return w.reshape(-1, P, kc * width)

    def feed(gate, up, down):
        g, u, d = columns(gate), columns(up), down.reshape(FT, P, D)
        order = [g[0], u[0], g[1], u[1], d[0]]
        for f in range(2, FT):
            order += [g[f], u[f], d[f - 1]]
        return order + [d[FT - 1]]

    gla_in = a["gla_w_in"][0]
    sb_in = a["sb_w_in"][0]
    ffn = lambda n, i: feed(a[f"{n}_w_gate"][i], a[f"{n}_w_up"][i], a[f"{n}_w_down"][i])
    cols = 2 * GLA_H * GLA_K + 2 * D
    keys = a["peer_sub_keys_2"][0].reshape(16, PE_N, P).transpose(2, 0, 1).reshape(P, 2, D).transpose(1, 0, 2)
    parts = [
        ffn("ffn1", 0), columns(gla_in[:, :cols]), columns(a["gla_w_out"][0]), ffn("ffn2", 0),
        ffn("ffn1", 1), columns(sb_in), columns(a["sb_w_out"][0]), ffn("ffn2", 1),
        columns(a["w_in_2"][0]), columns(a["ssm_w_glu_2"][0], 256), columns(a["w_ssm_out_2"][0], 256),
        columns(a["w_ml_out_2"][0]), columns(a["w_out_2"][0]), columns(a["peer_w_q_2"][0]), keys,
    ]
    wstream = np.concatenate([np.stack(p) if isinstance(p, list) else p for p in parts])
    assert wstream.shape == (PACKETS, P, D)

    feat = lambda v: v.reshape(-1, P).T
    gains = np.concatenate([feat(v) for v in (
        a["ffn1_norm"][0], a["mix_norm"][0], a["ffn2_norm"][0], a["ffn1_norm"][1], a["mix_norm"][1],
        a["ffn2_norm"][1], a["final_norm"], a["norm1_g_2"][0], a["norm2_g_2"][0], a["final_norm_g_2"])], 1)

    def c_blocks(c):
        o = np.zeros((2, 64, S5_C, 2, 16), c.dtype)
        c = c.reshape(S5_C, 2, 16, 64)
        for g in range(2):
            o[g, :, :, g, :] = c[:, g].transpose(2, 0, 1)
        return o.reshape(P, -1)

    def b_blocks(b):
        o = np.zeros((4, 2, 16, 4, 2, 64), b.dtype)
        b = b.reshape(4, 4, 2, 64, 16)
        for g in range(2):
            o[:, g, :, :, g, :] = b[:, :, g].transpose(1, 3, 0, 2)
        return o.reshape(P, -1)

    chunks = lambda w: w.reshape(-1, P, w.shape[-1]).transpose(1, 0, 2).reshape(P, -1)
    small = {
        "gains": gains, "b_gk": feat(a["gla_b_gk"][0]), "o_norm": feat(a["gla_o_norm"][0]),
        "w_lr": chunks(gla_in[:, cols:]),
        "a_re": feat(a["ssm_a_re_2"][0].ravel()), "a_im": feat(a["ssm_a_im_2"][0].ravel()),
        "log_dt": feat(np.repeat(a["ssm_log_dt_2"][0], 64)), "s5_d": feat(a["ssm_d_2"][0]),
        "b_glu": feat(a["ssm_b_glu_2"][0]),
        "c_re": c_blocks(a["ssm_c_re_2"][0]), "c_im": c_blocks(a["ssm_c_im_2"][0]),
        "b_re": b_blocks(a["ssm_b_re_2"][0]), "b_im": b_blocks(a["ssm_b_im_2"][0]),
        "conv_w": chunks(a["ml_conv_w_2"][0].T), "conv_b": feat(a["ml_conv_b_2"][0]),
        "wq": chunks(a["ml_wq_2"][0].reshape(D, 4)), "wk": chunks(a["ml_wk_2"][0].reshape(D, 4)),
        "wv": chunks(a["ml_wv_2"][0].reshape(D, 4)),
        "w_if": chunks(a["ml_w_if_2"][0]),
        "ml_g": feat(a["ml_norm_g_2"][0]), "ml_skip": feat(a["ml_skip_2"][0]),
    }
    for n, (_, w) in SMALL.items():
        assert small[n].shape == (P, w), (n, small[n].shape, w)
    tokens = lambda v: v.T.reshape(DC, P, -1).transpose(1, 0, 2)
    return {
        "wstream": wstream,
        "small": np.concatenate([small[n] for n in SMALL], 1),
        "xT": tokens(a["x"][0]), "metaT": tokens(a["meta_tokens_2"]),
        "w_gk2": a["gla_w_gk2"][0], "b_if": a["ml_b_if_2"][0].reshape(2, ML_H).T,
        "glast": a["final_norm_g_2"].reshape(1, D),
        "u_tab": a["peer_u_2"][0], "v_tab": a["peer_v_2"][0],
    }


def kernel(**inputs):
    import concourse.bacc as bacc
    from concourse.bass_utils import run_bass_kernel_spmd

    arrays = {n: np.ascontiguousarray(v) for n, v in lay_out(inputs).items()}
    nc = bacc.Bacc("TRN2", target_bir_lowering=False, num_devices=1)
    ins = {n: nc.dram_tensor(n, v.shape, mybir.dt.from_np(v.dtype), kind="ExternalInput").ap()
           for n, v in arrays.items()}
    out = nc.dram_tensor("out", (SEQ, D), F32, kind="ExternalOutput").ap()
    build_program(nc, ins, out)
    r = run_bass_kernel_spmd(nc, [arrays], core_ids=[0])
    return r.results[0]["out"].reshape(1, SEQ, D)
```

```python
from contextlib import ExitStack

import numpy as np
import concourse.bass as bass
from concourse import mybir

F32 = mybir.dt.float32
BF16 = mybir.dt.bfloat16
F32R = mybir.dt.float32r
U32 = mybir.dt.uint32
ACT = mybir.ActivationFunctionType
ALU = mybir.AluOpType
AX_X = mybir.AxisListType.X

P = 128
D = 1024
DC = D // P
SEQ = 256
META = 16
TOK = SEQ + META
DFF = 2816
FT = DFF // P
GLA_H, GLA_K, GLA_V, GLA_RANK, GLA_C = 4, 128, 256, 16, 64
GLA_B = SEQ // GLA_C
SB_H, SB_D = 16, 64
S5_C = 16
S5_W = 512
ML_H, ML_D = 4, 256
PE_H, PE_K, PE_N = 8, 16, 128
HK = PE_H * PE_K
PE_SLOTS = 8
EPS = 1e-6
TWO_PI = 2 * np.pi
ROUND = 12582912.0

RAW = 6
SPLIT = 4
BODY = 12


def packet_plan():
    at, n = {}, 0
    for name, count in (
        ("ffn0", 3 * FT), ("gla_in", 24), ("gla_out", 8), ("ffn1", 3 * FT),
        ("ffn2", 3 * FT), ("sb_in", 24), ("sb_out", 8), ("ffn3", 3 * FT),
        ("w_in", 36), ("s5_glu", 2), ("s5_out", 4), ("ml_out", 8), ("w_out", 8),
        ("peer_q", 16), ("peer_keys", 2),
    ):
        at[name] = n
        n += count
    return at, n


AT, PACKETS = packet_plan()
SPLIT_PACKETS = AT["peer_keys"]


SMALL = {}
_n = 0
for _name, _width in (
    ("gains", 10 * DC), ("b_gk", 4), ("o_norm", 2), ("w_lr", DC * GLA_RANK),
    ("a_re", S5_C), ("a_im", S5_C), ("log_dt", S5_C), ("s5_d", 4), ("b_glu", 4),
    ("c_re", S5_C * 32), ("c_im", S5_C * 32), ("b_re", 4 * P), ("b_im", 4 * P),
    ("conv_w", DC * 4), ("conv_b", DC), ("wq", DC * 4), ("wk", DC * 4), ("wv", DC * 4),
    ("w_if", 24 * 8), ("ml_g", DC), ("ml_skip", DC),
):
    SMALL[_name] = (_n, _width)
    _n += _width
SMALL_W = _n
GAIN = {n: i for i, n in enumerate(
    ("ffn1_0", "mix_0", "ffn2_0", "ffn1_1", "mix_1", "ffn2_1", "final", "norm1", "norm2", "last"))}


class Counted:

    def __init__(self, sem):
        self.sem, self.n = sem, 0

    def __call__(self, ins):
        self.n += 1
        return ins.then_inc(self.sem, 1)

    def settle(self, eng):
        eng.wait_ge(self.sem, self.n)


class Arena:

    def __init__(self, tensor, width):
        self.t, self.at, self.width = tensor, 0, width

    def take(self, *dims):
        n = int(np.prod(dims))
        a = self.t[:, self.at:self.at + n]
        self.at += n
        assert self.at <= self.width, self.at
        if len(dims) == 2:
            a = a.rearrange("p (a b) -> p a b", b=dims[1])
        elif len(dims) == 3:
            a = a.rearrange("p (a b c) -> p a b c", b=dims[1], c=dims[2])
        elif len(dims) == 4:
            a = a.rearrange("p (a b c d) -> p a b c d", b=dims[1], c=dims[2], d=dims[3])
        return a


def spread(ap, n):
    return ap.unsqueeze(2).to_broadcast([ap.shape[0], ap.shape[1], n])


def bcast(ap, n):
    return ap.unsqueeze(1).to_broadcast([ap.shape[0], n, ap.shape[1]])




def raw_slot(k, n):
    return k.raw[:, n % RAW, :]


def parts_of(k, n):
    return k.split[:, n % SPLIT, 0, :], k.split[:, n % SPLIT, 1, :]


def wait_packet(k, pe, n):
    pe.wait_ge(k.lo_done, n + 1)


def matmul3(pe, out, w_hi, w_lo, x_hi, x_lo, start, stop, **kw):
    pe.matmul(out, w_hi, x_hi, start=start, stop=False, **kw)
    pe.matmul(out, w_hi, x_lo, start=False, stop=False, **kw)
    return pe.matmul(out, w_lo, x_hi, start=False, stop=stop, **kw)


def mm_packet(k, pe, n, out, t0=0, T=SEQ, kc=DC, col=0, width=128):
    hi, lo = (p.rearrange("p (c m) -> p c m", c=kc) for p in parts_of(k, n))
    for c in range(kc):
        last = matmul3(pe, out, hi[:, c, col:col + 128], lo[:, c, col:col + 128],
                       k.xs[:, 0, c, t0:t0 + T], k.xs[:, 1, c, t0:t0 + T], c == 0, c == kc - 1)
    return last


def refill(k, act, n, i=None):
    m = n + SPLIT
    if i is None:
        if m >= SPLIT_PACKETS:
            return
        act.wait_ge(k.tile_done, n + 1)
        act.wait_ge(k.landed[m % RAW], 16 * (m // RAW + 1))
    else:
        act.wait_ge(k.tile_done, i * BODY + (n + 1))
        act.wait_ge(k.landed[m % RAW], i * (16 * BODY // RAW) + 16 * (m // RAW + 1))
    act.activation(parts_of(k, m)[0], raw_slot(k, m), ACT.Copy).then_inc(k.hi_done, 1)


def split(k, dve, c, src, t0=0, T=SEQ):
    k.dve(dve.tensor_copy(k.xs[:, 0, c, t0:t0 + T], src))
    k.dve.settle(dve)
    return dve.tensor_tensor(k.xs[:, 1, c, t0:t0 + T], src, k.xs[:, 0, c, t0:t0 + T].bitcast(F32), ALU.subtract)


def stage_end(k, eng, who):
    k.stage[who] += 1
    eng.drain().then_inc(k.stage_sem[who], 1)
    for other, sem in k.stage_sem.items():
        if other != who:
            eng.wait_ge(sem, k.stage[who])




def norm_act(k, act, r, x, gain, T=SEQ, t0=0):
    for c in range(DC if gain is not None else 0):
        g = k.small["gains"][:, gain * DC + c:gain * DC + c + 1]
        act.activation(k.xs[:, 0, c, t0:t0 + T], x[:, c, :], ACT.Copy, scale=g).then_inc(k.xh_ready, 1)
    for h in range(2):
        act.activation(k.sq[:, 4 * h:4 * h + 4, 0:T], x[:, 4 * h:4 * h + 4, :], ACT.Square).then_inc(k.sq_ready, 1)
    act.wait_ge(k.ss_ready, r + 1)
    act.activation(k.rms[:, 0:T], k.ps[:, 7, 0:T], ACT.Sqrt, bias=k.eps, scale=1.0 / D).then_inc(k.rms_ready, 1)


def norm_pe(k, pe, r, T=SEQ):
    for c in range(DC):
        if c % 4 == 0:
            pe.wait_ge(k.sq_ready, 2 * r + c // 4 + 1)
        last = pe.matmul(k.ps[:, 7, 0:T], k.ones, k.sq[:, c, 0:T], start=(c == 0), stop=(c == DC - 1))
    last.then_inc(k.ss_ready, 1)


def norm_low(k, dve, q, x, gain, T=SEQ, t0=0):
    for c in range(DC):
        g = k.small["gains"][:, gain * DC + c:gain * DC + c + 1]
        dve.wait_ge(k.xh_ready, DC * q + c + 1)
        dve.scalar_tensor_tensor(out=k.xs[:, 1, c, t0:t0 + T], in0=x[:, c, :], scalar=g,
                                 in1=k.xs[:, 0, c, t0:t0 + T].bitcast(F32), op0=ALU.mult, op1=ALU.subtract
                                 ).then_inc(k.xl_ready, 1)


def norm_rstd(k, dve, r, T=SEQ):
    dve.wait_ge(k.rms_ready, r + 1)
    k.dve(dve.reciprocal(k.rstd[:, 0:T], k.rms[:, 0:T]))
    k.dve.settle(dve)




def columns_pe(k, pe, q):
    for t in range(2):
        for c in range(DC):
            last = pe.matmul(k.ps[:, 5 + t, 0:1], k.sq[:, c, t * P:(t + 1) * P], k.ones[:, 0:1],
                             start=(c == 0), stop=(c == DC - 1))
    last.then_inc(k.col_ss, 1)


def columns_act(k, act, q):
    act.wait_ge(k.col_ss, q + 1)
    act.activation(k.rcol, k.ps[:, 5:7, 0], ACT.Sqrt, bias=k.eps, scale=1.0 / D).then_inc(k.col_rms, 1)


def columns_dve(k, dve, q):
    dve.wait_ge(k.col_rms, q + 1)
    k.dve(dve.reciprocal(k.rcol, k.rcol))
    k.dve.settle(dve)


class Tiles:

    def __init__(self, k, engs):
        self.k, self.engs, self.base = k, engs, (k.dve_tiles, k.act_tiles)
        k.dve_tiles += engs.count("D")
        k.act_tiles += engs.count("A")

    def wait_free(self, pe, n):
        if n >= 4:
            self.wait_emptied(pe, n - 4)

    def wait_emptied(self, pe, n):
        if self.engs[n] == "D":
            pe.wait_ge(self.k.dve_emptied, self.base[0] + self.engs[:n + 1].count("D"))
        else:
            pe.wait_ge(self.k.act_emptied, self.base[1] + self.engs[:n + 1].count("A"))




def setup(k, block):

    @block.scalar
    def _(act):
        for dst, src in k.small_loads:
            act.dma_start(dst, src).then_inc(k.small_in, 16)
        act.wait_ge(k.small_in, 16 * len(k.small_loads))
        for n in range(SPLIT):
            act.wait_ge(k.landed[n], 16)
            act.activation(parts_of(k, n)[0], raw_slot(k, n), ACT.Copy).then_inc(k.hi_done, 1)

    @block.vector
    def _(dve):
        k.dve(dve.memset(k.eps, EPS))
        k.dve(dve.memset(k.ones, 1.0))
        k.dve(dve.memset(k.one_col, 1.0))
        k.dve(dve.memset(k.neg_ones, -1.0))
        k.dve(dve.memset(k.zero_bf, 0.0))
        k.dve(dve.memset(k.ones_row, 1.0))

    @block.gpsimd
    def _(pool):
        k.pool(pool.memset(k.ident, 1.0))
        k.pool(pool.memset(k.keep_ge, 1.0))
        k.pool(pool.memset(k.keep_gt, 1.0))
        k.pool(pool.memset(k.neg_tri, -1.0))
        k.pool(pool.memset(k.head_row, 1.0))
        k.pool(pool.memset(k.block4, 1.0))
        k.pool(pool.iota(k.iota16, pattern=[[0, 16], [1, 16]], base=0, channel_multiplier=0,
                         allow_small_or_imprecise_dtypes=True))
        k.pool.settle(pool)
        k.pool(pool.affine_select(out=k.ident, in_=k.ident, compare_op=ALU.is_equal, fill=0.0, base=0,
                                  pattern=[[1, P]], channel_multiplier=-1))
        k.pool(pool.affine_select(out=k.keep_ge, in_=k.keep_ge, compare_op=ALU.is_ge, fill=0.0, base=0,
                                  pattern=[[1, P]], channel_multiplier=-1))
        k.pool(pool.affine_select(out=k.keep_gt, in_=k.keep_gt, compare_op=ALU.is_gt, fill=0.0, base=0,
                                  pattern=[[1, P]], channel_multiplier=-1))
        k.pool(pool.affine_select(out=k.neg_tri, in_=k.neg_tri, compare_op=ALU.is_ge, fill=0.0, base=0,
                                  pattern=[[-1, P]], channel_multiplier=1))
        k.pool(pool.affine_select(out=k.head_row, in_=k.head_row, compare_op=ALU.is_equal, fill=0.0, base=0,
                                  pattern=[[1, ML_H], [0, P]], channel_multiplier=-1))
        k.pool(pool.affine_select(out=k.block4, in_=k.block4, compare_op=ALU.is_ge, fill=0.0, base=0,
                                  pattern=[[-4, 32]], channel_multiplier=1))
        k.pool.settle(pool)
        k.pool(pool.affine_select(out=k.block4, in_=k.block4, compare_op=ALU.is_ge, fill=0.0, base=3,
                                  pattern=[[4, 32]], channel_multiplier=-1))


    @block.gpsimd
    def _(pool):
        pool.engine_nop().then_inc(k.consts_made, 1)

    for engine in (block.scalar, block.vector, block.tensor):
        engine(lambda e: e.wait_ge(k.consts_made, 1))
    all_end(k, block)


def all_end(k, block):
    block.scalar(lambda e: stage_end(k, e, "act"))
    block.vector(lambda e: stage_end(k, e, "dve"))
    block.tensor(lambda e: stage_end(k, e, "pe"))


def weights_in(k, block, wstream):

    @block.sync
    def _(sp):
        for n in range(RAW):
            sp.dma_start(k.raw[:, n, :], wstream[n]).then_inc(k.landed[n], 16)
        full = PACKETS // RAW
        with sp.Fori(1, full) as i:
            for s in range(RAW):
                sp.wait_ge(k.lo_done, (i - 1) * RAW + (s + 1))
                sp.dma_start(k.raw[:, s, :], wstream[bass.ds(i * RAW + s, 1)].rearrange("a p m -> p (a m)")
                             ).then_inc(k.landed[s], 16)
        for n in range(full * RAW, PACKETS):
            sp.wait_ge(k.lo_done, n - RAW + 1)
            sp.dma_start(k.raw[:, n % RAW, :], wstream[n]).then_inc(k.landed[n % RAW], 16)


def low_parts(k, block, first, last):

    @block.gpsimd
    def _(pool):
        def one(n, i=None):
            pool.wait_ge(k.hi_done, n + 1 if i is None else i * BODY + (n + 1))
            hi, lo = parts_of(k, n)
            pool.tensor_tensor(lo, raw_slot(k, n), hi.bitcast(F32), ALU.subtract).then_inc(k.lo_done, 1)

        turns = (last - first) // BODY
        if turns > 1:
            with pool.Fori(0, turns) as i:
                for j in range(BODY):
                    one(first + j, i)
        for n in range(first + BODY * turns if turns > 1 else first, last):
            one(n)


def s5_parameters(k, block):
    sm = k.small
    t = k.s5_tmp

    @block.scalar
    def _(act):
        act.activation(k.s5_dt, sm["log_dt"], ACT.Exp).then_inc(k.s5_act, 1)
        act.wait_ge(k.s5_er, 1)
        act.activation(k.s5_r, k.s5_ere, ACT.Exp).then_inc(k.s5_act, 1)
        act.wait_ge(k.s5_th, 1)
        act.activation(k.s5_sin, k.s5_theta, ACT.Sin).then_inc(k.s5_act, 1)
        act.activation(k.s5_half, k.s5_theta, ACT.Sin, scale=0.5).then_inc(k.s5_act, 1)

    @block.vector
    def _(dve):
        def tt(out, a, b, op):
            k.dve(dve.tensor_tensor(out, a, b, op))
            k.dve.settle(dve)

        def ts(out, a, s1, s2, op0, op1):
            k.dve(dve.tensor_scalar(out, a, s1, s2, op0, op1))
            k.dve.settle(dve)

        dve.wait_ge(k.s5_act, 1)
        dve.tensor_tensor(k.s5_ere, sm["a_re"], k.s5_dt, ALU.mult).then_inc(k.s5_er, 1)
        tt(k.s5_theta, sm["a_im"], k.s5_dt, ALU.mult)
        ts(t[0], k.s5_theta, 1.0 / TWO_PI, ROUND, ALU.mult, ALU.add)
        ts(t[0], t[0], -ROUND, -6.28125, ALU.add, ALU.mult)
        tt(k.s5_theta, k.s5_theta, t[0], ALU.add)
        c2 = round((TWO_PI - 6.28125) * 2 ** 23) / 2 ** 23
        for part in (c2, TWO_PI - 6.28125 - c2):
            ts(t[1], t[0], part / 6.28125, None, ALU.mult, ALU.bypass)
            tt(k.s5_theta, k.s5_theta, t[1], ALU.add)
        dve.tensor_scalar(k.s5_theta, k.s5_theta, 3.1415925, -3.1415925, ALU.min, ALU.max).then_inc(k.s5_th, 1)
        dve.wait_ge(k.s5_act, 4)
        tt(t[0], k.s5_half, k.s5_half, ALU.mult)
        ts(k.s5_cos, t[0], -2.0, 1.0, ALU.mult, ALU.add)
        tt(t[0], k.s5_r, k.s5_cos, ALU.mult)
        ts(t[0], t[0], -1.0, None, ALU.add, ALU.bypass)
        tt(t[1], k.s5_r, k.s5_sin, ALU.mult)
        tt(t[2], sm["a_re"], sm["a_re"], ALU.mult)
        tt(t[3], sm["a_im"], sm["a_im"], ALU.mult)
        tt(t[4], t[2], t[3], ALU.add)
        k.dve(dve.reciprocal(t[5], t[4]))
        k.dve.settle(dve)
        tt(t[2], t[0], sm["a_re"], ALU.mult)
        tt(t[3], t[1], sm["a_im"], ALU.mult)
        tt(t[2], t[2], t[3], ALU.add)
        tt(k.s5_cre, t[2], t[5], ALU.mult)
        tt(t[2], t[1], sm["a_re"], ALU.mult)
        tt(t[3], t[0], sm["a_im"], ALU.mult)
        tt(t[2], t[2], t[3], ALU.subtract)
        dve.tensor_tensor(k.s5_cim, t[2], t[5], ALU.mult).then_inc(k.s5_coef, 1)


def s5_tables(k, block):
    sm = k.small

    @block.gpsimd
    def _(pool):
        t = k.s5_tmp

        def tt(out, a, b, op):
            k.pool(pool.tensor_tensor(out, a, b, op))
            k.pool.settle(pool)

        pool.wait_ge(k.s5_coef, 1)
        cre = sm["c_re"].rearrange("p (c m) -> p c m", c=S5_C)
        cim = sm["c_im"].rearrange("p (c m) -> p c m", c=S5_C)
        ar, ai = spread(k.s5_cre, 32), spread(k.s5_cim, 32)
        w = [k.s5_big[i // 2][:, :, 32 * (i % 2):32 * (i % 2) + 32] for i in range(4)]
        tt(w[0], cre, ar, ALU.mult)
        tt(w[1], cim, ai, ALU.mult)
        tt(w[2], cre, ai, ALU.mult)
        tt(w[3], cim, ar, ALU.mult)
        tt(cre, w[0], w[1], ALU.subtract)
        tt(cim, w[2], w[3], ALU.add)
        ec, es = k.s5_ec, k.s5_es
        k.pool(pool.memset(ec[:, :, 0:1], 1.0))
        k.pool(pool.memset(es[:, :, 0:1], 0.0))
        k.pool.settle(pool)
        pc, pn = k.s5_cos, k.s5_sin
        n = 1
        while n < TOK:
            m = min(n, TOK - n)
            bc, bs = spread(pc, m), spread(pn, m)
            a, b = k.s5_big[0][:, :, 0:m], k.s5_big[1][:, :, 0:m]
            tt(a, ec[:, :, 0:m], bc, ALU.mult)
            tt(b, es[:, :, 0:m], bs, ALU.mult)
            tt(ec[:, :, n:n + m], a, b, ALU.subtract)
            tt(a, ec[:, :, 0:m], bs, ALU.mult)
            tt(b, es[:, :, 0:m], bc, ALU.mult)
            tt(es[:, :, n:n + m], a, b, ALU.add)
            tt(t[0], pc, pc, ALU.mult)
            tt(t[1], pn, pn, ALU.mult)
            tt(t[2], pc, pn, ALU.mult)
            tt(pc, t[0], t[1], ALU.subtract)
            k.pool(pool.tensor_tensor(pn, t[2], t[2], ALU.add))
            k.pool.settle(pool)
            n *= 2
        pool.engine_nop().then_inc(k.s5_made, 1)


def feed_forward(k, block, q, gain, packet):
    x = k.x[:, :, META:TOK]
    r, e = k.norms, k.early
    k.norms += 1
    k.early += 1
    gate_ps, up_ps = [k.ps[:, 4 + b, 0:SEQ] for b in range(2)], [k.ps[:, 6 + b, 0:SEQ] for b in range(2)]
    y = k.ps[:, 0:4, :]
    base = FT * q

    @block.scalar
    def _(act):
        norm_act(k, act, r, x, gain)

        def one(b, f):
            act.wait_ge(k.gate_ready, f)
            act.activation(k.gate_s[:, b, :], k.gate_t[:, b, :], ACT.Silu).then_inc(k.silu_ready, 1)

        refill(k, act, packet)
        one(0, base + 1)
        refill(k, act, packet + 1)
        refill(k, act, packet + 2)
        one(1, base + 2)
        refill(k, act, packet + 3)
        refill(k, act, packet + 4)
        with act.Fori(0, (FT - 2) // 4) as i:
            for j in range(4):
                n = packet + 5 + 3 * j
                refill(k, act, n, i)
                one(j % 2, i * 4 + (base + 3 + j))
                refill(k, act, n + 1, i)
                refill(k, act, n + 2, i)
        refill(k, act, packet + 3 * FT - 1)

    @block.vector
    def _(dve):
        norm_low(k, dve, e, x, gain)
        norm_rstd(k, dve, r)

        def one(b, f, n_gate, n_up, first=False):
            dve.wait_ge(k.tile_done, n_gate)
            if not first:
                dve.wait_ge(k.silu_ready, f - 2)
            dve.tensor_tensor(k.gate_t[:, b, :], gate_ps[b], k.rstd[:, 0:SEQ], ALU.mult).then_inc(k.gate_ready, 1)
            dve.wait_ge(k.tile_done, n_up)
            dve.wait_ge(k.silu_ready, f)
            h, hh, hl = k.gate_s[:, b, :], k.h[:, b, 0, :], k.h[:, b, 1, :]
            dve.tensor_tensor(h, h, up_ps[b], ALU.mult).then_inc(k.h_made, 1)
            dve.wait_ge(k.h_made, f)
            dve.tensor_copy(hh, h).then_inc(k.h_high, 1)
            dve.wait_ge(k.h_high, f)
            dve.tensor_tensor(hl, h, hh.bitcast(F32), ALU.subtract).then_inc(k.h_ready, 1)

        one(0, base + 1, packet + 1, packet + 2, first=True)
        one(1, base + 2, packet + 3, packet + 4, first=True)
        with dve.Fori(0, (FT - 2) // 4) as i:
            for j in range(4):
                n = packet + 5 + 3 * j
                one(j % 2, i * 4 + (base + 3 + j), i * BODY + (n + 1), i * BODY + (n + 2))
        dve.wait_ge(k.h_ready, base + FT)
        k.dve(dve.tensor_scalar(k.rstd[:, 0:SEQ], k.rstd[:, 0:SEQ], 0.5, None, ALU.mult))
        k.dve.settle(dve)
        dve.wait_ge(k.tile_done, packet + 3 * FT)
        for b in range(4):
            k.dve(dve.tensor_tensor(k.sq[:, 2 * b:2 * b + 2, 0:SEQ], y[:, b, :].rearrange("p (a t) -> p a t", a=2),
                                    bcast(k.rstd[:, 0:SEQ], 2), ALU.mult))
        k.dve.settle(dve)
        for b in range(4):
            xb = x[:, 2 * b:2 * b + 2, :]
            dve.tensor_tensor(xb, xb, k.sq[:, 2 * b:2 * b + 2, 0:SEQ], ALU.add)

    @block.tensor
    def _(pe):
        for b in range(4):
            pe.matmul(y[:, b, :], k.zero_bf[:, 0:P], k.zero_bf, start=True, stop=False, skip_group_check=True)

        def half(w, b, n, wait, first=False):
            pe.wait_ge(k.lo_done, wait)
            hi, lo = (p.rearrange("p (c m) -> p c m", c=DC) for p in parts_of(k, n))
            for c in range(DC):
                if first:
                    pe.wait_ge(k.xl_ready, DC * e + c + 1)
                last = matmul3(pe, (gate_ps, up_ps)[w][b], hi[:, c, :], lo[:, c, :],
                               k.xs[:, 0, c, 0:SEQ], k.xs[:, 1, c, 0:SEQ], c == 0, c == DC - 1)
            last.then_inc(k.tile_done, 1)

        def down(b, n, wait, f, stop=False):
            pe.wait_ge(k.h_ready, f)
            pe.wait_ge(k.lo_done, wait)
            hi, lo = parts_of(k, n)
            for c in range(DC):
                last = matmul3(pe, y[:, c // 2, (c % 2) * SEQ:(c % 2 + 1) * SEQ], hi[:, c * P:(c + 1) * P],
                               lo[:, c * P:(c + 1) * P], k.h[:, b, 0, :], k.h[:, b, 1, :], False, stop,
                               skip_group_check=True)
            last.then_inc(k.tile_done, 1)

        half(0, 0, packet, packet + 1, first=True)
        norm_pe(k, pe, r)
        half(1, 0, packet + 1, packet + 2)
        half(0, 1, packet + 2, packet + 3)
        pe.wait_ge(k.rms_ready, r + 1)
        half(1, 1, packet + 3, packet + 4)
        down(0, packet + 4, packet + 5, base + 1)
        with pe.Fori(0, (FT - 2) // 4) as i:
            for j in range(4):
                n = packet + 5 + 3 * j
                pe.wait_ge(k.h_ready, i * 4 + (base + 1 + j))
                half(0, j % 2, n, i * BODY + (n + 1))
                half(1, j % 2, n + 1, i * BODY + (n + 2))
                down((1 + j) % 2, n + 2, i * BODY + (n + 3), i * 4 + (base + 2 + j))
        n = packet + 3 * FT - 1
        down((FT - 1) % 2, n, n + 1, base + FT, stop=True)

    all_end(k, block)


def add_projection(k, block, packet, ready, count):
    tiles = Tiles(k, ["D"] * 8)

    @block.tensor
    def _(pe):
        for n in range(8):
            if n == 0:
                pe.wait_ge(ready, count)
            tiles.wait_free(pe, n)
            wait_packet(k, pe, packet + n)
            mm_packet(k, pe, packet + n, k.ps[:, n % 4, 0:SEQ]).then_inc(k.tile_done, 1)

    @block.scalar
    def _(act):
        for n in range(8):
            refill(k, act, packet + n)

    @block.vector
    def _(dve):
        for n in range(8):
            dve.wait_ge(k.tile_done, packet + n + 1)
            xb = k.x[:, n, META:TOK]
            dve.tensor_tensor(xb, k.ps[:, n % 4, 0:SEQ], xb, ALU.add).then_inc(k.dve_emptied, 1)

    all_end(k, block)


def wide_packets(k, pe, n0, banks, free):
    for j in range(4):
        if j == 0:
            free()
        wait_packet(k, pe, n0 + j)
        hi, lo = (p.rearrange("p (c m) -> p c m", c=2) for p in parts_of(k, n0 + j))
        for t in range(2):
            for i in range(2):
                c = 2 * j + i
                last = matmul3(pe, k.ps[:, banks[t], :], k.xs[:, 0, c, t * P:(t + 1) * P],
                               k.xs[:, 1, c, t * P:(t + 1) * P], hi[:, i, :], lo[:, i, :], c == 0, c == DC - 1)
        last.then_inc(k.tile_done, 1)


def gated_linear_attention(k, block, gain):
    x = k.x[:, :, META:TOK]
    sm, ps = k.small, k.ps
    r, e0, cq = k.norms, k.early, k.columns
    k.norms += 1
    k.early += 1
    k.columns += 1
    mark = k.arena.at
    take = k.arena.take
    H, B, C = GLA_H, GLA_B, GLA_C
    qs, ks = take(H, SEQ), take(H, SEQ)
    vt = take(2, D)
    sg = take(DC, SEQ)
    lr = take(SEQ)
    zb_at = k.arena.at
    zb, az, cum = take(H, SEQ), take(H, SEQ), take(H, SEQ)
    la = zb
    up, down_ = take(H, B), take(H, B)
    off = [0]
    for i in range(B):
        off.append(off[-1] + C * (i + 1))
    eq, ek = take(H, SEQ), take(H, off[B])
    st = take(2, 3 * P)
    o = take(H, 2 * SEQ)
    osq = k.arena.t[:, zb_at:zb_at + 2 * H * SEQ].rearrange("p (h t) -> p h t", h=H)
    rms = take(H, SEQ)
    wlr = sm["w_lr"].rearrange("p (c m) -> p c m", c=DC)
    tiles = Tiles(k, ["D"] * 20)
    p0 = AT["gla_in"]

    @block.scalar
    def _(act):
        norm_act(k, act, r, x, gain)
        columns_act(k, act, cq)
        for n in range(3):
            refill(k, act, p0 + n)
        act.wait_ge(k.gla_dve, 1)
        k.act(act.activation(az, az, ACT.Exp, scale=-1.0))
        k.act.settle(act)
        act.activation(az, az, ACT.Ln, bias=k.one_col).then_inc(k.gla_act, 1)
        for n in range(3, 8):
            refill(k, act, p0 + n)
        act.wait_ge(k.gla_dve, 2)
        for h in range(H):
            for i in range(B):
                act.activation(eq[:, h, C * i:C * (i + 1)], cum[:, h, C * i:C * (i + 1)], ACT.Exp,
                               bias=down_[:, h, i:i + 1], scale=1.0 / 16)
                last = act.activation(ek[:, h, off[i]:off[i + 1]], cum[:, h, 0:C * (i + 1)], ACT.Exp,
                                      bias=up[:, h, i:i + 1], scale=-1.0 / 16)
            last.then_inc(k.gla_act, 1)
            refill(k, act, p0 + 8 + 2 * h)
            refill(k, act, p0 + 9 + 2 * h)
        for n in range(8):
            refill(k, act, p0 + 16 + n)
            act.wait_ge(k.dve_emptied, tiles.base[0] + 13 + n)
            act.activation(sg[:, n, :], sg[:, n, :], ACT.Silu).then_inc(k.gla_silu, 1)
        for h in range(H):
            act.wait_ge(k.gla_o, h + 1)
            act.activation(osq[:, h, :], ps[:, 6 + h % 2, :], ACT.Square).then_inc(k.gla_sq, 1)
        for h in range(H):
            act.wait_ge(k.gla_ss, h + 1)
            act.activation(rms[:, h, :], ps[:, h, 0:SEQ], ACT.Sqrt, bias=k.eps, scale=1.0 / GLA_V
                           ).then_inc(k.gla_rms, 1)

    @block.vector
    def _(dve):
        norm_low(k, dve, e0, x, gain)
        for c in range(DC):
            g = sm["gains"][:, gain * DC + c:gain * DC + c + 1]
            last = dve.tensor_scalar(wlr[:, c, :], wlr[:, c, :], g, None, ALU.mult)
        last.then_inc(k.gla_wlr, 1)
        k.dve(dve.memset(st, 0.0))
        norm_rstd(k, dve, r)
        columns_dve(k, dve, cq)
        dve.wait_ge(k.gla_pe, 1)
        dve.tensor_tensor(lr[0:GLA_RANK, :], ps[0:GLA_RANK, 4, 0:SEQ], k.rstd[0:GLA_RANK, 0:SEQ], ALU.mult
                          ).then_inc(k.gla_lr, 1)
        dve.wait_ge(k.gla_pe, 2)
        for h in range(H):
            k.dve(dve.tensor_scalar(zb[:, h, :], ps[:, 4 + h // 2, (h % 2) * SEQ:(h % 2 + 1) * SEQ],
                                    sm["b_gk"][:, h:h + 1], None, ALU.add))
        k.dve.settle(dve)
        dve.scalar_tensor_tensor(out=az, in0=zb, scalar=-1.0, in1=zb, op0=ALU.mult, op1=ALU.max
                                 ).then_inc(k.gla_dve, 1)
        rstd = k.rstd[:, 0:SEQ]
        for n in range(4):
            dve.wait_ge(k.tile_done, p0 + n + 1)
            dve.scalar_tensor_tensor(out=qs[:, n, :], in0=ps[:, n % 4, 0:SEQ], scalar=GLA_K ** -0.5, in1=rstd,
                                     op0=ALU.mult, op1=ALU.mult).then_inc(k.dve_emptied, 1)
        dve.wait_ge(k.gla_act, 1)
        k.dve(dve.scalar_tensor_tensor(out=la, in0=zb, scalar=0.0, in1=az, op0=ALU.min, op1=ALU.subtract))
        k.dve.settle(dve)
        for h in range(H):
            k.dve(dve.tensor_tensor_scan(cum[:, h, :], k.ones_row[:, 0:SEQ], la[:, h, :], 0.0, ALU.mult, ALU.add))
        k.dve.settle(dve)
        mid = cum.rearrange("p h (i c) -> p h i c", c=C)[:, :, :, C // 2 - 1]
        k.dve(dve.tensor_scalar(up, mid, 1.0 / 16, None, ALU.mult))
        k.dve.settle(dve)
        dve.tensor_scalar(down_, mid, -1.0 / 16, None, ALU.mult).then_inc(k.gla_dve, 1)
        for n in range(4, 8):
            dve.wait_ge(k.tile_done, p0 + n + 1)
            dve.tensor_tensor(ks[:, n - 4, :], ps[:, n % 4, 0:SEQ], rstd, ALU.mult).then_inc(k.dve_emptied, 1)
        for half in range(2):
            dve.wait_ge(k.tile_done, p0 + 8 + 4 * (half + 1))
            for t in range(2):
                dve.tensor_scalar(vt[:, t, half * 512:(half + 1) * 512], ps[:, 2 * half + t, :], k.rcol[:, t:t + 1],
                                  None, ALU.mult).then_inc(k.dve_emptied, 1)
        for n in range(8):
            dve.wait_ge(k.tile_done, p0 + 17 + n)
            dve.tensor_tensor(sg[:, n, :], ps[:, n % 4, 0:SEQ], rstd, ALU.mult).then_inc(k.dve_emptied, 1)
        dve.wait_ge(k.dve_emptied, tiles.base[0] + 20)
        k.dve.settle(dve)
        for h in range(H):
            dve.wait_ge(k.gla_act, 2 + h)
            dve.tensor_tensor(eq[:, h, :], eq[:, h, :], qs[:, h, :], ALU.mult).then_inc(k.gla_qk, 1)
            for i in range(B):
                e = ek[:, h, off[i]:off[i + 1]]
                dve.tensor_tensor(e, e, ks[:, h, 0:C * (i + 1)], ALU.mult).then_inc(k.gla_qk, 1)
        for h in range(H):
            b, s = ps[:, 4 + h % 2, :], st[:, h % 2, :]
            dve.wait_ge(k.gla_s, h + 1)
            if h >= 2:
                dve.wait_ge(k.gla_o, h - 1)
            m = k.keep_ge
            dve.tensor_tensor(s[0:C, 0:C], b[0:C, 0:C], m[0:C, 0:C], ALU.mult)
            dve.tensor_tensor(s[:, C:2 * C], b[:, C:2 * C], m[:, C:2 * C], ALU.mult)
            dve.tensor_copy(s[:, 2 * C:4 * C], b[:, 2 * C:4 * C])
            dve.tensor_tensor(s[0:C, 4 * C:5 * C], b[0:C, 4 * C:5 * C], m[0:C, 0:C], ALU.mult)
            dve.tensor_tensor(s[:, 5 * C:6 * C], b[:, 5 * C:6 * C], m[:, C:2 * C], ALU.mult).then_inc(k.gla_st, 1)
            dve.wait_ge(k.gla_sq, h + 1)
            dve.tensor_copy(o[:, h, :], ps[:, 6 + h % 2, :]).then_inc(k.gla_copied, 1)
        dve.wait_ge(k.gla_copied, H)
        dve.wait_ge(k.gla_silu, 8)
        for h in range(H):
            dve.wait_ge(k.gla_rms, h + 1)
            k.dve(dve.reciprocal(rms[:, h, :], rms[:, h, :]))
            k.dve.settle(dve)
            for e in range(2):
                oe = o[:, h, e * SEQ:(e + 1) * SEQ]
                k.dve(dve.scalar_tensor_tensor(out=oe, in0=oe, scalar=sm["o_norm"][:, e:e + 1], in1=rms[:, h, :],
                                               op0=ALU.mult, op1=ALU.mult))
            k.dve.settle(dve)
            g = sg[:, 2 * h:2 * h + 2, :]
            oh = o[:, h, :].rearrange("p (e t) -> p e t", e=2)
            k.dve(dve.tensor_tensor(g, g, oh, ALU.mult))
            k.dve.settle(dve)
            for c in (2 * h, 2 * h + 1):
                split(k, dve, c, sg[:, c, :]).then_inc(k.mix_ready, 1)

    @block.tensor
    def _(pe):
        def tile(n):
            f = n if n < 8 else n - 4
            tiles.wait_free(pe, f)
            wait_packet(k, pe, p0 + n)
            mm_packet(k, pe, p0 + n, ps[:, f % 4, 0:SEQ]).then_inc(k.tile_done, 1)

        pe.wait_ge(k.xl_ready, DC * (e0 + 1))
        tile(0)
        norm_pe(k, pe, r)
        columns_pe(k, pe, cq)
        pe.wait_ge(k.gla_wlr, 1)
        for c in range(DC):
            last = pe.matmul(ps[0:GLA_RANK, 4, 0:SEQ], wlr[:, c, :], x[:, c, :], start=(c == 0), stop=(c == DC - 1))
        last.then_inc(k.gla_pe, 1)
        tile(1)
        pe.wait_ge(k.gla_lr, 1)
        pe.wait_ge(k.col_rms, cq + 1)
        for h in range(H):
            last = pe.matmul(ps[:, 4 + h // 2, (h % 2) * SEQ:(h % 2 + 1) * SEQ],
                             k.w_gk2[:, h * P:(h + 1) * P], lr[0:GLA_RANK, :], start=True, stop=True)
        last.then_inc(k.gla_pe, 1)
        for n in range(2, 8):
            tile(n)
        for half in range(2):
            def free():
                for t in range(2):
                    tiles.wait_free(pe, 8 + 2 * half + t)
            wide_packets(k, pe, p0 + 8 + 4 * half, (2 * half, 2 * half + 1), free)
        for n in range(16, 24):
            tile(n)

        def scores(h):
            b = ps[:, 4 + h % 2, :]
            pe.wait_ge(k.gla_qk, 5 * (h + 1))
            if h >= 2:
                pe.wait_ge(k.gla_st, h - 1)
            q = lambda i: eq[:, h, C * i:C * (i + 1)]
            kk = lambda i, lo, n: ek[:, h, off[i] + lo:off[i] + lo + n]
            pe.matmul(b[0:C, 0:C], kk(0, 0, C), q(0), start=True, stop=True)
            pe.matmul(b[:, C:2 * C], kk(1, 0, P), q(1), start=True, stop=True)
            pe.matmul(b[:, 2 * C:3 * C], kk(2, 0, P), q(2), start=True, stop=True)
            pe.matmul(b[:, 3 * C:4 * C], kk(3, 0, P), q(3), start=True, stop=True)
            pe.matmul(b[0:C, 4 * C:5 * C], kk(2, P, C), q(2), start=True, stop=True)
            pe.matmul(b[:, 5 * C:6 * C], kk(3, P, P), q(3), start=True, stop=True).then_inc(k.gla_s, 1)

        def outputs(h):
            pe.wait_ge(k.gla_st, h + 1)
            if h >= 2:
                pe.wait_ge(k.gla_copied, h - 1)
                pe.wait_ge(k.gla_sq, h - 1)
            s = st[:, h % 2, :]
            for e in range(2):
                b = ps[:, 6 + h % 2, e * SEQ:(e + 1) * SEQ]
                v = lambda t: vt[:, t, h * GLA_V + e * P:h * GLA_V + (e + 1) * P]
                pe.matmul(b, v(0), s[:, 0:SEQ], start=True, stop=False, skip_group_check=True)
                last = pe.matmul(b[:, P:SEQ], v(1), s[:, SEQ:SEQ + P], start=False, stop=True, skip_group_check=True)
            last.then_inc(k.gla_o, 1)

        for h in range(H):
            scores(h)
            outputs(h)
        for h in range(H):
            pe.wait_ge(k.gla_sq, h + 1)
            if h == 0:
                for n in range(16, 20):
                    tiles.wait_emptied(pe, n)
            for e in range(2):
                last = pe.matmul(ps[:, h, 0:SEQ], k.ones, osq[:, h, e * SEQ:(e + 1) * SEQ], start=(e == 0), stop=(e == 1))
            last.then_inc(k.gla_ss, 1)
        pe.wait_ge(k.gla_rms, H)

    k.mixes += DC
    add_projection(k, block, AT["gla_out"], k.mix_ready, k.mixes)
    k.arena.at = mark


def stick_breaking(k, block, gain):
    x = k.x[:, :, META:TOK]
    ps = k.ps
    r, e0, cq = k.norms, k.early, k.columns
    k.norms += 1
    k.early += 1
    k.columns += 1
    mark = k.arena.at
    take = k.arena.take
    qs, ks = take(DC, SEQ), take(DC, SEQ)
    vt = take(2, D)
    ab, spl, w = take(2, 3 * P), take(2, 3 * P), take(2, 3 * P)
    tiles = Tiles(k, ["D"] * 20)
    p0 = AT["sb_in"]
    N3 = 3 * P
    diag = lambda a: a.rearrange("p (j t) -> p j t", j=3)[:, 0:3:2, :]
    mask = bcast(k.keep_gt, 2)

    @block.scalar
    def _(act):
        norm_act(k, act, r, x, gain)
        columns_act(k, act, cq)
        for n in range(24):
            refill(k, act, p0 + n)
        for h in range(SB_H + 1):
            if h < SB_H:
                b = ps[:, 4 + h % 2, 0:N3]
                a = ab[:, h % 2, :]
                act.wait_ge(k.sb_z, h + 1)
                if h >= 2:
                    act.wait_ge(k.sb_sp, h - 1)
                k.act(act.activation(a, b, ACT.Abs))
                k.act.settle(act)
                k.act(act.activation(a, a, ACT.Exp, scale=-1.0))
                k.act.settle(act)
                act.activation(a, a, ACT.Ln, bias=k.one_col).then_inc(k.sb_ln, 1)
            if h >= 1:
                g = h - 1
                act.wait_ge(k.sb_log, g + 1)
                if g >= 2:
                    act.wait_ge(k.sb_av, g - 1)
                act.activation(w[:, g % 2, :], ps[:, 4 + g % 2, 0:N3], ACT.Exp).then_inc(k.sb_exp, 1)

    @block.vector
    def _(dve):
        norm_low(k, dve, e0, x, gain)
        norm_rstd(k, dve, r)
        columns_dve(k, dve, cq)
        rstd = k.rstd[:, 0:SEQ]
        for n in range(16):
            dve.wait_ge(k.tile_done, p0 + n + 1)
            if n < 8:
                i = dve.scalar_tensor_tensor(out=qs[:, n, :], in0=ps[:, n % 4, 0:SEQ], scalar=SB_D ** -0.5, in1=rstd,
                                             op0=ALU.mult, op1=ALU.mult)
            else:
                i = dve.tensor_tensor(ks[:, n - 8, :], ps[:, n % 4, 0:SEQ], rstd, ALU.mult)
            i.then_inc(k.dve_emptied, 1)
        for half in range(2):
            dve.wait_ge(k.tile_done, p0 + 16 + 4 * (half + 1))
            for t in range(2):
                dve.tensor_scalar(vt[:, t, half * 512:(half + 1) * 512], ps[:, 2 * half + t, :], k.rcol[:, t:t + 1],
                                  None, ALU.mult).then_inc(k.dve_emptied, 1)
        for h in range(SB_H + 2):
            if h < SB_H:
                dve.wait_ge(k.sb_ln, h + 1)
                if h >= 2:
                    dve.wait_ge(k.sb_log, h - 1)
                s = spl[:, h % 2, :]
                k.dve(dve.scalar_tensor_tensor(out=s, in0=ps[:, 4 + h % 2, 0:N3], scalar=0.0, in1=ab[:, h % 2, :],
                                               op0=ALU.max, op1=ALU.add))
                k.dve.settle(dve)
                dve.tensor_tensor(diag(s), diag(s), mask, ALU.mult).then_inc(k.sb_sp, 1)
            if 1 <= h <= SB_H:
                g = h - 1
                dve.wait_ge(k.sb_exp, g + 1)
                s = diag(w[:, g % 2, :])
                dve.scalar_tensor_tensor(out=s, in0=s, scalar=1.0, in1=mask, op0=ALU.min, op1=ALU.mult
                                         ).then_inc(k.sb_w, 1)
            if h >= 2 and (h - 2) % 2 == 1:
                g = h - 2
                dve.wait_ge(k.sb_av, g + 1)
                split(k, dve, g // 2, ps[:, 6 + (g // 2) % 2, 0:SEQ]).then_inc(k.mix_ready, 1)

    @block.tensor
    def _(pe):
        pe.wait_ge(k.xl_ready, DC * (e0 + 1))
        for n in range(16):
            tiles.wait_free(pe, n)
            wait_packet(k, pe, p0 + n)
            mm_packet(k, pe, p0 + n, ps[:, n % 4, 0:SEQ]).then_inc(k.tile_done, 1)
            if n == 0:
                norm_pe(k, pe, r)
                columns_pe(k, pe, cq)
        for half in range(2):
            def free():
                for t in range(2):
                    tiles.wait_free(pe, 16 + 2 * half + t)
            wide_packets(k, pe, p0 + 16 + 4 * half, (2 * half, 2 * half + 1), free)
        tiles.wait_emptied(pe, 19)
        pe.wait_ge(k.col_rms, cq + 1)
        for h in range(SB_H + 2):
            if h < SB_H:
                b = ps[:, 4 + h % 2, :]
                lo = SB_D * (h % 2)
                kt, qt = ks[lo:lo + SB_D, h // 2, :], qs[lo:lo + SB_D, h // 2, :]
                if h >= 2:
                    pe.wait_ge(k.sb_exp, h - 1)
                pe.matmul(b[:, 0:SEQ], kt[:, 0:P], qt, start=True, stop=False, skip_group_check=True)
                pe.matmul(b[:, SEQ:N3], kt[:, P:SEQ], qt[:, P:SEQ], start=False, stop=False, skip_group_check=True
                          ).then_inc(k.sb_z, 1)
            if 1 <= h <= SB_H:
                g = h - 1
                b, s = ps[:, 4 + g % 2, :], spl[:, g % 2, :]
                pe.wait_ge(k.sb_sp, g + 1)
                pe.matmul(b[:, 0:SEQ], k.neg_tri, s[:, 0:SEQ], start=False, stop=False, skip_group_check=True)
                pe.matmul(b[:, P:SEQ], k.neg_ones, s[:, SEQ:N3], start=False, stop=False, skip_group_check=True)
                pe.matmul(b[:, SEQ:N3], k.neg_tri, s[:, SEQ:N3], start=False, stop=True, skip_group_check=True
                          ).then_inc(k.sb_log, 1)
            if h >= 2:
                g = h - 2
                pe.wait_ge(k.sb_w, g + 1)
                if g >= 4 and g % 2 == 0:
                    pe.wait_ge(k.mix_ready, k.mixes + g // 2 - 1)
                lo = SB_D * (g % 2)
                b = ps[lo:lo + SB_D, 6 + (g // 2) % 2, :]
                v = lambda t: vt[:, t, g * SB_D:(g + 1) * SB_D]
                pe.matmul(b[:, 0:SEQ], v(0), w[:, g % 2, 0:SEQ], start=True, stop=False, skip_group_check=True)
                pe.matmul(b[:, P:SEQ], v(1), w[:, g % 2, SEQ:N3], start=False, stop=True, skip_group_check=True
                          ).then_inc(k.sb_av, 1)

    k.mixes += DC
    add_projection(k, block, AT["sb_out"], k.mix_ready, k.mixes)
    k.arena.at = mark


def final_of_first(k, block, gain):
    x = k.x[:, :, META:TOK]
    r = k.norms
    k.norms += 1
    block.scalar(lambda act: norm_act(k, act, r, x, None))
    block.tensor(lambda pe: norm_pe(k, pe, r))

    @block.vector
    def _(dve):
        norm_rstd(k, dve, r)
        for c in range(DC):
            g = k.small["gains"][:, gain * DC + c:gain * DC + c + 1]
            dve.scalar_tensor_tensor(out=x[:, c, :], in0=x[:, c, :], scalar=g, in1=k.rstd[:, 0:SEQ],
                                     op0=ALU.mult, op1=ALU.mult)

    all_end(k, block)


def input_projection(k, block, gain):
    ps = k.ps
    r, e0 = k.norms, k.early
    k.norms += 1
    k.early += 1
    p0 = AT["w_in"]
    tiles = Tiles(k, ["D"] * 36)

    @block.scalar
    def _(act):
        act.wait_ge(k.s5_made, 1)
        norm_act(k, act, r, k.x, gain, TOK)
        for n in range(36):
            refill(k, act, p0 + n)
            if n >= 12:
                act.wait_ge(k.dve_emptied, tiles.base[0] + n + 1)
                s = k.sig[:, n - 12, :]
                act.activation(s, s, ACT.Sigmoid)

    @block.vector
    def _(dve):
        dve.wait_ge(k.s5_made, 1)
        k.dve(dve.memset(k.xm[:, :, 0:3], 0.0))
        norm_low(k, dve, e0, k.x, gain, TOK)
        norm_rstd(k, dve, r, TOK)
        for n in range(36):
            dve.wait_ge(k.tile_done, p0 + n + 1)
            if n < 12:
                dst = k.u[:, n, :] if n < 4 else k.xm[:, n - 4, 3:3 + TOK]
                dve.tensor_tensor(dst, ps[:, n % 4, 0:TOK], k.rstd, ALU.mult).then_inc(k.dve_emptied, 1)
            else:
                dve.tensor_tensor(k.sig[:, n - 12, :], ps[:, n % 4, 0:SEQ], k.rstd[:, META:TOK], ALU.mult
                                  ).then_inc(k.dve_emptied, 1)

    @block.tensor
    def _(pe):
        pe.wait_ge(k.xl_ready, DC * (e0 + 1))
        for n in range(36):
            tiles.wait_free(pe, n)
            wait_packet(k, pe, p0 + n)
            t0, T = (0, TOK) if n < 12 else (META, SEQ)
            mm_packet(k, pe, p0 + n, ps[:, n % 4, 0:T], t0, T).then_inc(k.tile_done, 1)
            if n == 0:
                norm_pe(k, pe, r, TOK)

    all_end(k, block)


def state_space(k, block):
    ps, sm = k.ps, k.small
    mark = k.arena.at
    take = k.arena.take
    v = take(2, TOK)
    hh = take(2, 2, TOK)
    t4 = take(4, TOK)
    y, yg = k.sq[:, 0:4, 0:SEQ], k.sq[:, 4:8, 0:SEQ]
    bre = sm["b_re"].rearrange("p (j m) -> p j m", j=4)
    bim = sm["b_im"].rearrange("p (j m) -> p j m", j=4)
    cre = sm["c_re"].rearrange("p (c m) -> p c m", c=S5_C)
    cim = sm["c_im"].rearrange("p (c m) -> p c m", c=S5_C)
    ec, es = k.s5_ec, k.s5_es
    pg, po = AT["s5_glu"], AT["s5_out"]

    @block.scalar
    def _(act):
        for j in range(4):
            act.wait_ge(k.s5_y, j + 1)
            act.activation(y[:, j, :], y[:, j, :], ACT.Gelu_apprx_tanh).then_inc(k.s5_gelu, 1)
        for j in range(4):
            act.wait_ge(k.tile_done, pg + j // 2 + 1)
            if j % 2 == 0:
                refill(k, act, pg + j // 2)
            act.activation(yg[:, j, :], ps[:, j, 0:SEQ], ACT.Sigmoid, bias=sm["b_glu"][:, j:j + 1]
                           ).then_inc(k.s5_sig, 1)
        for n in range(4):
            refill(k, act, po + n)

    @block.vector
    def _(dve):
        for c in range(S5_C):
            b = c % 2
            br, bi = ps[:, 2 * b, 0:TOK], ps[:, 2 * b + 1, 0:TOK]
            dve.wait_ge(k.s5_bu, c + 1)
            if c:
                dve.wait_ge(k.s5_h, c)
            k.dve(dve.tensor_tensor(t4[:, 0, :], br, ec[:, c, :], ALU.mult))
            k.dve(dve.tensor_tensor(t4[:, 1, :], bi, es[:, c, :], ALU.mult))
            k.dve(dve.tensor_tensor(t4[:, 2, :], bi, ec[:, c, :], ALU.mult))
            dve.tensor_tensor(t4[:, 3, :], br, es[:, c, :], ALU.mult).then_inc(k.s5_bu_used, 1)
            k.dve.settle(dve)
            dve.wait_ge(k.s5_bu_used, c + 1)
            k.dve(dve.tensor_tensor(v[:, 0, :], t4[:, 0, :], t4[:, 1, :], ALU.add))
            k.dve(dve.tensor_tensor(v[:, 1, :], t4[:, 2, :], t4[:, 3, :], ALU.subtract))
            k.dve.settle(dve)
            rr = k.s5_r[:, c:c + 1].to_broadcast([P, TOK])
            for i in range(2):
                k.dve(dve.tensor_tensor_scan(v[:, i, :], rr, v[:, i, :], 0.0, ALU.mult, ALU.add))
            k.dve.settle(dve)
            k.dve(dve.tensor_tensor(t4[:, 0, :], v[:, 0, :], ec[:, c, :], ALU.mult))
            k.dve(dve.tensor_tensor(t4[:, 1, :], v[:, 1, :], es[:, c, :], ALU.mult))
            k.dve(dve.tensor_tensor(t4[:, 2, :], v[:, 0, :], es[:, c, :], ALU.mult))
            k.dve(dve.tensor_tensor(t4[:, 3, :], v[:, 1, :], ec[:, c, :], ALU.mult))
            k.dve.settle(dve)
            if c >= 2:
                dve.wait_ge(k.s5_cu, c - 1)
            k.dve(dve.tensor_tensor(hh[:, b, 0, :], t4[:, 0, :], t4[:, 1, :], ALU.subtract))
            k.dve.settle(dve)
            dve.scalar_tensor_tensor(out=hh[:, b, 1, :], in0=t4[:, 2, :], scalar=-1.0, in1=t4[:, 3, :],
                                     op0=ALU.mult, op1=ALU.subtract).then_inc(k.s5_h, 1)
            if c % 4 == 3:
                j = c // 4
                dve.wait_ge(k.s5_cu, c + 1)
                dve.scalar_tensor_tensor(out=y[:, j, :], in0=k.u[:, j, META:TOK], scalar=sm["s5_d"][:, j:j + 1],
                                         in1=ps[:, 4 + j, 0:SEQ], op0=ALU.mult, op1=ALU.add).then_inc(k.s5_y, 1)
        for j in range(4):
            dve.wait_ge(k.s5_gelu, j + 1)
            split(k, dve, j, y[:, j, :]).then_inc(k.s5_ys, 1)
        dve.wait_ge(k.tile_done, pg + 2)
        for j in range(4):
            dve.wait_ge(k.s5_sig, j + 1)
            k.dve(dve.tensor_tensor(yg[:, j, :], yg[:, j, :], y[:, j, :], ALU.mult))
            k.dve.settle(dve)
            split(k, dve, j, yg[:, j, :]).then_inc(k.s5_yg, 1)
        for n in range(8):
            dve.wait_ge(k.tile_done, po + n // 2 + 1)
            s = k.sig[:, 8 + n, :]
            dve.tensor_tensor(s, s, ps[:, n, 0:SEQ], ALU.mult)

    @block.tensor
    def _(pe):
        def bu(c):
            b, j, lo = c % 2, c // 4, 32 * (c % 4)
            if c >= 2:
                pe.wait_ge(k.s5_bu_used, c - 1)
            pe.matmul(ps[:, 2 * b, 0:TOK], bre[lo:lo + 32, j, :], k.u[lo:lo + 32, j, :], start=True, stop=True,
                      tile_position=(lo, 0))
            pe.matmul(ps[:, 2 * b + 1, 0:TOK], bim[lo:lo + 32, j, :], k.u[lo:lo + 32, j, :], start=True, stop=True,
                      tile_position=(lo, 0)).then_inc(k.s5_bu, 1)

        bu(0)
        for c in range(S5_C):
            if c + 1 < S5_C:
                bu(c + 1)
            j, lo = c // 4, 32 * (c % 4)
            pe.wait_ge(k.s5_h, c + 1)
            for i, w in enumerate((cre, cim)):
                last = pe.matmul(ps[lo:lo + 32, 4 + j, 0:SEQ], w[:, c, :], hh[:, c % 2, i, META:TOK],
                                 start=(i == 0), stop=(i == 1), tile_position=(0, lo))
            last.then_inc(k.s5_cu, 1)
        pe.wait_ge(k.s5_ys, 4)
        pe.wait_ge(k.s5_bu_used, S5_C)
        for n in range(2):
            wait_packet(k, pe, pg + n)
            for i in range(2):
                last = mm_packet(k, pe, pg + n, ps[:, 2 * n + i, 0:SEQ], kc=4, col=P * i)
            last.then_inc(k.tile_done, 1)
        pe.wait_ge(k.s5_yg, 4)
        pe.wait_ge(k.s5_sig, 4)
        pe.wait_ge(k.s5_y, 4)
        for n in range(4):
            wait_packet(k, pe, po + n)
            for i in range(2):
                last = mm_packet(k, pe, po + n, ps[:, 2 * n + i, 0:SEQ], kc=4, col=P * i)
            last.then_inc(k.tile_done, 1)

    all_end(k, block)
    k.arena.at = mark


def mlstm(k, block):
    ps, sm = k.ps, k.small
    mark = k.arena.at
    take = k.arena.take
    xc = take(DC, TOK)
    qkv = take(3, DC, TOK)
    bd = take(3, DC, P)
    vt = take(3, D)
    gi, gf = take(TOK), take(TOK)
    az, cs, mx, bb = take(TOK), take(TOK), take(TOK), take(TOK)
    ccol = take(3, ML_H)
    over = bd.rearrange("p m c j -> p (m c j)")
    dm = over[:, 0:6 * SEQ].rearrange("p (b s t) -> p b s t", b=2, s=3)
    hz = over[:, 6 * SEQ:10 * SEQ].rearrange("p (b t) -> p b t", b=2)
    den = over[:, 10 * SEQ:12 * SEQ].rearrange("p (b t) -> p b t", b=2)
    old = k.small_all[:, SMALL["c_re"][0]:SMALL["b_im"][0] + SMALL["b_im"][1]]
    hsq = old[:, 0:4 * SEQ].rearrange("p (b t) -> p b t", b=2)
    em = old[:, 4 * SEQ:6 * SEQ].rearrange("p (b t) -> p b t", b=2)
    rms = old[:, 6 * SEQ:8 * SEQ].rearrange("p (b t) -> p b t", b=2)
    sT = dm
    w_if = sm["w_if"].rearrange("p (c m) -> p c m", c=24)
    cw = sm["conv_w"].rearrange("p (c m) -> p c m", c=DC)
    spans = ((0, META), (META, P), (META + P, P))
    R = slice(0, ML_H)

    @block.scalar
    def _(act):
        for c in range(DC):
            act.wait_ge(k.ml_conv, c + 1)
            act.activation(xc[:, c, :], xc[:, c, :], ACT.Silu).then_inc(k.ml_xc, 1)
        for n in range(2 * DC):
            act.wait_ge(k.ml_qkv, n + 1)
            act.activation(qkv[:, n // DC, n % DC, :], ps[:, n % 4, 0:TOK], ACT.Copy).then_inc(k.act_emptied, 1)
        act.wait_ge(k.ml_gate, 1)
        act.activation(gi[R, :], ps[R, 4, 0:TOK], ACT.Identity, bias=k.b_if[:, 0:1]).then_inc(k.ml_act, 1)
        act.activation(gf[R, :], ps[R, 5, 0:TOK], ACT.Identity, bias=k.b_if[:, 1:2]).then_inc(k.ml_act, 1)
        act.wait_ge(k.ml_dve, 1)
        k.act(act.activation(az[R, :], az[R, :], ACT.Exp, scale=-1.0))
        k.act.settle(act)
        act.activation(az[R, :], az[R, :], ACT.Ln, bias=k.one_col[R, :]).then_inc(k.ml_act, 1)

        def decays(h):
            b = h % 2
            act.wait_ge(k.ml_mb, h + 1)
            if h >= 2:
                act.wait_ge(k.ml_den, h - 1)
            for s, (lo, n) in enumerate(spans):
                act.activation(dm[0:n, b, s, :], ps[0:n, b, 0:SEQ], ACT.Exp, bias=ccol[0:n, s, h:h + 1], scale=-1.0)
            act.activation(em[:, b, :], ps[:, b, SEQ:2 * SEQ], ACT.Exp, scale=-1.0).then_inc(k.ml_exp, 1)

        decays(0)
        decays(1)
        for h in range(ML_H):
            act.wait_ge(k.ml_hz, h + 1)
            if h >= 2:
                act.wait_ge(k.ml_ss, h - 1)
            act.activation(hsq[:, h % 2, :], hz[:, h % 2, :], ACT.Square).then_inc(k.ml_sq, 1)
            act.wait_ge(k.ml_ss, h + 1)
            act.activation(rms[:, h % 2, :], ps[:, 7, 0:SEQ], ACT.Sqrt, bias=k.eps, scale=1.0 / ML_D
                           ).then_inc(k.ml_rms, 1)
            if h + 2 < ML_H:
                decays(h + 2)

    @block.vector
    def _(dve):
        for c in range(DC):
            k.dve(dve.tensor_scalar(xc[:, c, :], k.xm[:, c, 0:TOK], cw[:, c, 0:1], sm["conv_b"][:, c:c + 1],
                                    ALU.mult, ALU.add))
            for j in range(1, 4):
                k.dve.settle(dve)
                i = dve.scalar_tensor_tensor(out=xc[:, c, :], in0=k.xm[:, c, j:j + TOK], scalar=cw[:, c, j:j + 1],
                                             in1=xc[:, c, :], op0=ALU.mult, op1=ALU.add)
                if j < 3:
                    k.dve(i)
            i.then_inc(k.ml_conv, 1)
        for m, name in enumerate(("wq", "wk", "wv")):
            for c in range(DC):
                w4 = sm[name][:, 4 * c:4 * c + 4]
                last = dve.tensor_tensor(bd[:, m, c, :].rearrange("p (n j) -> p n j", j=4), bcast(w4, 32),
                                         spread(k.block4, 4), ALU.mult)
            last.then_inc(k.ml_bd, 1)
        for c in range(DC):
            dve.wait_ge(k.ml_qkv, 2 * DC + c + 1)
            dve.tensor_copy(qkv[:, 2, c, :], ps[:, c % 4, 0:TOK]).then_inc(k.ml_vcopied, 1)
        for s, (lo, n) in enumerate(spans):
            for half in range(2):
                dve.wait_ge(k.ml_vt, 2 * s + half + 1)
                dve.tensor_copy(vt[0:n, s, half * 512:(half + 1) * 512], ps[0:n, 6 + half, :]).then_inc(k.ml_vtc, 1)
        dve.wait_ge(k.ml_act, 2)
        dve.scalar_tensor_tensor(out=az[R, :], in0=gf[R, :], scalar=-1.0, in1=gf[R, :], op0=ALU.mult, op1=ALU.max
                                 ).then_inc(k.ml_dve, 1)
        dve.wait_ge(k.ml_act, 3)
        k.dve(dve.scalar_tensor_tensor(out=gf[R, :], in0=gf[R, :], scalar=0.0, in1=az[R, :],
                                       op0=ALU.min, op1=ALU.subtract))
        k.dve.settle(dve)
        k.dve(dve.tensor_tensor_scan(bb[R, :], k.ones_row[R, 0:TOK], gf[R, :], 0.0, ALU.mult, ALU.add))
        k.dve.settle(dve)
        k.dve(dve.tensor_tensor(cs[R, :], gi[R, :], bb[R, :], ALU.subtract))
        k.dve.settle(dve)
        k.dve(dve.tensor_tensor_scan(mx[R, :], k.ones_row[R, 0:TOK], cs[R, :], 0.0, ALU.mult, ALU.max))
        k.dve.settle(dve)
        dve.tensor_tensor(bb[R, :], bb[R, :], mx[R, :], ALU.add).then_inc(k.ml_dve, 1)
        dve.wait_ge(k.ml_cc, 1)
        for s, (lo, n) in enumerate(spans):
            last = dve.tensor_copy(ccol[0:n, s, :], ps[0:n, 6, 16 * s:16 * s + ML_H])
        last.then_inc(k.ml_dve, 1)
        for h in range(ML_H):
            b = h % 2
            dve.wait_ge(k.ml_exp, h + 1)
            k.dve(dve.tensor_scalar(dm[0:META, b, 0, :], dm[0:META, b, 0, :], 1.0, None, ALU.min))
            dd = dm[:, b, 1, 0:P]
            k.dve(dve.scalar_tensor_tensor(out=dd, in0=dd, scalar=1.0, in1=k.keep_ge, op0=ALU.min, op1=ALU.mult))
            dd = dm[:, b, 1, P:SEQ]
            k.dve(dve.tensor_scalar(dd, dd, 1.0, None, ALU.min))
            dd = dm[:, b, 2, P:SEQ]
            k.dve(dve.scalar_tensor_tensor(out=dd, in0=dd, scalar=1.0, in1=k.keep_ge, op0=ALU.min, op1=ALU.mult))
            dve.wait_ge(k.ml_s, h + 1)
            if h >= 2:
                dve.wait_ge(k.ml_num, h - 1)
            k.dve.settle(dve)
            sc = ML_D ** -0.5
            dve.scalar_tensor_tensor(out=sT[0:META, b, 0, :], in0=ps[0:META, 2, SEQ:2 * SEQ], scalar=sc,
                                     in1=dm[0:META, b, 0, :], op0=ALU.mult, op1=ALU.mult)
            dve.scalar_tensor_tensor(out=sT[:, b, 1, :], in0=ps[:, 2, 0:SEQ], scalar=sc,
                                     in1=dm[:, b, 1, :], op0=ALU.mult, op1=ALU.mult)
            dve.scalar_tensor_tensor(out=sT[:, b, 2, P:SEQ], in0=ps[:, 3, 0:P], scalar=sc,
                                     in1=dm[:, b, 2, P:SEQ], op0=ALU.mult, op1=ALU.mult).then_inc(k.ml_sT, 1)
            dve.wait_ge(k.ml_num, h + 1)
            k.dve(dve.scalar_tensor_tensor(out=den[:, b, :], in0=ps[:, 6, 0:SEQ], scalar=-1.0, in1=em[:, b, :],
                                           op0=ALU.mult, op1=ALU.max))
            k.dve.settle(dve)
            dve.tensor_tensor(den[:, b, :], ps[:, 6, 0:SEQ], den[:, b, :], ALU.max).then_inc(k.ml_den, 1)
            dve.wait_ge(k.ml_den, h + 1)
            k.dve(dve.reciprocal(den[:, b, :], den[:, b, :]))
            k.dve.settle(dve)
            hv = hz[:, b, :].rearrange("p (e t) -> p e t", e=2)
            k.dve(dve.tensor_tensor(hv, k.sig[:, 2 * h:2 * h + 2, :], bcast(den[:, b, :], 2), ALU.mult))
            k.dve.settle(dve)
            dve.tensor_tensor(hz[:, b, :], ps[:, 4 + b, :], hz[:, b, :], ALU.mult).then_inc(k.ml_hz, 1)
            dve.wait_ge(k.ml_hz, h + 1)
            dve.wait_ge(k.ml_rms, h + 1)
            k.dve(dve.reciprocal(rms[:, b, :], rms[:, b, :]))
            k.dve.settle(dve)
            for e in range(2):
                c = 2 * h + e
                he = hz[:, b, e * SEQ:(e + 1) * SEQ]
                k.dve(dve.scalar_tensor_tensor(out=he, in0=he, scalar=sm["ml_g"][:, c:c + 1], in1=rms[:, b, :],
                                               op0=ALU.mult, op1=ALU.mult))
                k.dve.settle(dve)
                k.dve(dve.scalar_tensor_tensor(out=k.sig[:, c, :], in0=xc[:, c, META:TOK],
                                               scalar=sm["ml_skip"][:, c:c + 1], in1=he,
                                               op0=ALU.mult, op1=ALU.add))
                k.dve.settle(dve)
                split(k, dve, c, k.sig[:, c, :]).then_inc(k.mix_ready, 1)

    @block.tensor
    def _(pe):
        for n in range(3 * DC):
            m, c = n // DC, n % DC
            if c == 0:
                pe.wait_ge(k.ml_bd, m + 1)
            if m < 2:
                pe.wait_ge(k.ml_xc, c + 1)
            if 4 <= n < 2 * DC + 4:
                pe.wait_ge(k.act_emptied, k.act_tiles + n - 3)
            elif n >= 4:
                pe.wait_ge(k.ml_vcopied, n - 3 - 2 * DC)
            src = xc[:, c, :] if m < 2 else k.xm[:, c, 3:3 + TOK]
            pe.matmul(ps[:, n % 4, 0:TOK], bd[:, m, c, :], src, start=True, stop=True).then_inc(k.ml_qkv, 1)
        for s, (lo, n) in enumerate(spans):
            for half in range(2):
                if s:
                    pe.wait_ge(k.ml_vtc, 2 * s + half - 1)
                for c in range(4 * half, 4 * half + 4):
                    last = pe.matmul(ps[0:n, 6 + half, (c % 4) * P:(c % 4 + 1) * P], k.xm[:, c, 3 + lo:3 + lo + n],
                                     bd[:, 2, c, :], start=True, stop=True)
                last.then_inc(k.ml_vt, 1)
        pe.wait_ge(k.ml_vcopied, DC)
        pe.wait_ge(k.act_emptied, k.act_tiles + 2 * DC)
        for g in range(2):
            for c in range(24):
                last = pe.matmul(ps[R, 4 + g, 0:TOK], w_if[:, c, 4 * g:4 * g + 4], qkv[:, c // DC, c % DC, :],
                                 start=(c == 0), stop=(c == 23))
        last.then_inc(k.ml_gate, 1)
        pe.wait_ge(k.ml_dve, 2)
        pe.wait_ge(k.ml_vtc, 6)
        for s, (lo, n) in enumerate(spans):
            last = pe.matmul(ps[0:n, 6, 16 * s:16 * s + ML_H], cs[R, lo:lo + n], k.ident[R, R], start=True, stop=True)
        last.then_inc(k.ml_cc, 1)
        pe.wait_ge(k.ml_dve, 3)
        pe.wait_ge(k.ml_act, 3)

        def stab(h):
            if h >= 2:
                pe.wait_ge(k.ml_exp, h - 1)
            hr = k.head_row[R, h, :]
            pe.matmul(ps[:, h % 2, 0:SEQ], hr, mx[R, META:TOK], start=True, stop=True)
            pe.matmul(ps[:, h % 2, SEQ:2 * SEQ], hr, bb[R, META:TOK], start=True, stop=True).then_inc(k.ml_mb, 1)

        stab(0)
        stab(1)
        for h in range(ML_H):
            b = h % 2
            q = lambda e, lo, hi: qkv[:, 0, 2 * h + e, lo:hi]
            kk = lambda e, s: qkv[:, 1, 2 * h + e, spans[s][0]:spans[s][0] + spans[s][1]]
            if h >= 1:
                pe.wait_ge(k.ml_sT, h)
            for e in range(2):
                pe.matmul(ps[:, 2, 0:SEQ], kk(e, 1), q(e, META, TOK), start=(e == 0), stop=(e == 1))
            for e in range(2):
                pe.matmul(ps[0:META, 2, SEQ:2 * SEQ], kk(e, 0), q(e, META, TOK), start=(e == 0), stop=(e == 1))
            for e in range(2):
                last = pe.matmul(ps[:, 3, 0:P], kk(e, 2), q(e, META + P, TOK), start=(e == 0), stop=(e == 1))
            last.then_inc(k.ml_s, 1)
            pe.wait_ge(k.ml_sT, h + 1)
            if h >= 1:
                pe.wait_ge(k.ml_hz, h)
            for e in range(2):
                o = ps[:, 4 + b, e * SEQ:(e + 1) * SEQ]
                v = lambda s: vt[0:spans[s][1], s, h * ML_D + e * P:h * ML_D + (e + 1) * P]
                pe.matmul(o, v(1), sT[:, b, 1, :], start=True, stop=False, skip_group_check=True)
                pe.matmul(o, v(0), sT[0:META, b, 0, :], start=False, stop=False, skip_group_check=True)
                pe.matmul(o[:, P:SEQ], v(2), sT[:, b, 2, P:SEQ], start=False, stop=True, skip_group_check=True)
            o = ps[:, 6, 0:SEQ]
            pe.matmul(o, k.ones, sT[:, b, 1, :], start=True, stop=False, skip_group_check=True)
            pe.matmul(o, k.ones[0:META, :], sT[0:META, b, 0, :], start=False, stop=False, skip_group_check=True)
            pe.matmul(o[:, P:SEQ], k.ones, sT[:, b, 2, P:SEQ], start=False, stop=True, skip_group_check=True
                      ).then_inc(k.ml_num, 1)
            if h + 2 < ML_H:
                stab(h + 2)
            pe.wait_ge(k.ml_sq, h + 1)
            if h >= 1:
                pe.wait_ge(k.ml_rms, h)
            for e in range(2):
                last = pe.matmul(ps[:, 7, 0:SEQ], k.ones, hsq[:, b, e * SEQ:(e + 1) * SEQ], start=(e == 0), stop=(e == 1))
            last.then_inc(k.ml_ss, 1)

    k.act_tiles += 2 * DC
    k.mixes += 2 * ML_H
    all_end(k, block)
    k.arena.at = mark


def mix_out(k, block):
    tiles = Tiles(k, ["D"] * 8)
    packet = AT["ml_out"]
    ps = k.ps

    @block.tensor
    def _(pe):
        for n in range(8):
            tiles.wait_free(pe, n)
            wait_packet(k, pe, packet + n)
            mm_packet(k, pe, packet + n, ps[:, n % 4, 0:SEQ]).then_inc(k.tile_done, 1)

    @block.scalar
    def _(act):
        for n in range(8):
            refill(k, act, packet + n)

    @block.vector
    def _(dve):
        for n in range(8):
            dve.wait_ge(k.tile_done, packet + n + 1)
            g, s = k.sig[:, 16 + n, :], k.sig[:, 8 + n, :]
            dve.tensor_tensor(g, g, ps[:, n % 4, 0:SEQ], ALU.mult).then_inc(k.dve_emptied, 1)
        dve.wait_ge(k.dve_emptied, tiles.base[0] + 8)
        k.dve(dve.tensor_tensor(k.sig[:, 8:16, :], k.sig[:, 8:16, :], k.sig[:, 16:24, :], ALU.add))
        k.dve.settle(dve)
        for c in range(DC):
            split(k, dve, c, k.sig[:, 8 + c, :]).then_inc(k.mix_ready, 1)

    k.mixes += DC
    add_projection(k, block, AT["w_out"], k.mix_ready, k.mixes)


def peer_route(k, block, gain, rows):
    ps, sm = k.ps, k.small
    x = k.x[:, :, META:TOK]
    r, e0, cq = k.norms, k.early, k.columns
    k.norms += 1
    k.early += 1
    k.columns += 1
    mark = k.arena.at
    take = k.arena.take
    qT = take(16, SEQ)
    sc = take(2, 16, P)
    wk = take(256)
    val = take(16, PE_K)
    idx = take(16, PE_K).bitcast(U32)
    idf = take(16, PE_K)
    cand = take(PE_H, 256)
    cv = take(PE_H, PE_K)
    ci = take(PE_H, PE_K).bitcast(U32)
    ab = take(2, HK).bitcast(U32)
    abf = take(2, HK)
    one = take(HK, PE_K)
    gain_rows = one.rearrange("p a b -> p (a b)")[0:1, :]
    sel = take(2, HK)
    nm = take(PE_H)
    p0, pk = AT["peer_q"], AT["peer_keys"]
    tiles = Tiles(k, ["D"] * 16)

    @block.scalar
    def _(act):
        act.dma_start(gain_rows, rows).then_inc(k.rows_in, 16)
        norm_act(k, act, r, x, gain)
        columns_act(k, act, cq)
        for n in range(16):
            refill(k, act, p0 + n)
        for n in range(8):
            act.wait_ge(k.pr_s, n + 1)
            act.activation(sc[:, n % 2, 4 * (n // 2):4 * (n // 2) + 4, :], ps[:, n % 4, :].rearrange("p (a b) -> p a b", a=4),
                           ACT.Copy).then_inc(k.pr_sc, 1)
        for n in range(4):
            act.wait_ge(k.pr_t, n + 1)
            act.activation(k.xt[:, n // 2, (n % 2) * 512:(n % 2 + 1) * 512], ps[:, 4 + n, :], ACT.Copy
                           ).then_inc(k.pr_tc, 1)
        for i in range(2):
            act.wait_ge(k.pr_gl, i + 1)
            act.activation(k.gain_all[:, i, :].rearrange("p (a b) -> p a b", a=2), ps[:, 2 * i:2 * i + 2, :], ACT.Copy
                           ).then_inc(k.pr_ga, 1)
        for n in range(2):
            act.wait_ge(k.pr_g, n + 1)
            act.activation(k.gate[:, n, :], k.gate[:, n, :], ACT.Exp).then_inc(k.pr_e, 1)

    @block.vector
    def _(dve):
        norm_low(k, dve, e0, x, gain)
        norm_rstd(k, dve, r)
        columns_dve(k, dve, cq)
        for n in range(16):
            dve.wait_ge(k.tile_done, p0 + n + 1)
            dve.tensor_tensor(qT[:, n, :], ps[:, n % 4, 0:SEQ], k.rstd[:, 0:SEQ], ALU.mult).then_inc(k.dve_emptied, 1)
        k.dve(dve.memset(k.expert[:, 4 * HK:], 0))
        dve.wait_ge(k.pr_sc, 8)

        def run(i):
            k.dve(i)
            k.dve.settle(dve)

        def top16(values, scratch, v, ix):
            run(dve.max(v[:, 0:8], values))
            run(dve.max_index(ix[:, 0:8], v[:, 0:8], values))
            run(dve.match_replace(scratch, v[:, 0:8], values, -3e38))
            run(dve.max(v[:, 8:16], scratch))
            run(dve.max_index(ix[:, 8:16], v[:, 8:16], scratch))

        for t in range(2):
            for n in range(16):
                top16(sc[:, t, n, :], wk[:, 0:P], val[:, n, :], idx[:, n, :])
            run(dve.tensor_copy(idf, idx))
            v2 = val.rearrange("p (h i) k -> p h i k", i=2)
            for h in range(PE_H):
                k.dve(dve.tensor_tensor(cand[:, h, :].rearrange("p (a b) -> p a b", a=16), spread(v2[:, h, 0, :], 16),
                                        bcast(v2[:, h, 1, :], 16), ALU.add))
            k.dve.settle(dve)
            for h in range(PE_H):
                top16(cand[:, h, :], wk, cv[:, h, :], ci[:, h, :])
            cif = ci.rearrange("p h k -> p (h k)")
            run(dve.tensor_scalar(ab[:, 0, :], cif, 4, None, ALU.logical_shift_right))
            run(dve.tensor_scalar(ab[:, 1, :], cif, 15, None, ALU.bitwise_and))
            run(dve.tensor_copy(abf, ab))
            dve.wait_ge(k.pr_ga, 2)
            f2 = idf.rearrange("p (h i) k -> p h i k", i=2)
            for i in range(2):
                for h in range(PE_H):
                    o = one[:, h * 16:(h + 1) * 16, :]
                    k.dve(dve.tensor_tensor(o, spread(abf[:, i, h * 16:(h + 1) * 16], 16), k.iota16, ALU.is_equal))
                    k.dve.settle(dve)
                    k.dve(dve.tensor_tensor(o, o, bcast(f2[:, h, i, :], 16), ALU.mult))
                k.dve.settle(dve)
                run(dve.tensor_reduce(sel[:, i, :], one, AX_X, ALU.add))
            run(dve.scalar_tensor_tensor(out=sel[:, 0, :], in0=sel[:, 0, :], scalar=float(PE_N), in1=sel[:, 1, :],
                                         op0=ALU.mult, op1=ALU.add))
            for ph in (t, t + 2):
                k.dve(dve.tensor_copy(k.expert[:, ph * HK:(ph + 1) * HK], sel[:, 0, :]))
            g = k.gate[:, t, :].rearrange("p (h k) -> p h k", h=PE_H)
            dve.tensor_tensor(g, cv, cv[:, :, 0:1].to_broadcast([P, PE_H, PE_K]), ALU.subtract).then_inc(k.pr_g, 1)
            dve.wait_ge(k.pr_e, t + 1)
            run(dve.tensor_reduce(nm, g, AX_X, ALU.add))
            run(dve.reciprocal(nm, nm))
            run(dve.tensor_tensor(g, g, spread(nm, PE_K), ALU.mult))
            dve.wait_ge(k.pr_tc, 4)
            run(dve.scalar_tensor_tensor(out=k.ht[:, t, :], in0=k.xt[:, t, :], scalar=k.rcol[:, t:t + 1],
                                         in1=k.gain_all[:, 0, :], op0=ALU.mult, op1=ALU.mult))

    @block.tensor
    def _(pe):
        pe.wait_ge(k.xl_ready, DC * (e0 + 1))
        for n in range(16):
            tiles.wait_free(pe, n)
            wait_packet(k, pe, p0 + n)
            mm_packet(k, pe, p0 + n, ps[:, n % 4, 0:SEQ]).then_inc(k.tile_done, 1)
            if n == 0:
                norm_pe(k, pe, r)
                columns_pe(k, pe, cq)
        tiles.wait_emptied(pe, 15)
        for n in range(8):
            j, t = n // 2, n % 2
            if n >= 4:
                pe.wait_ge(k.pr_sc, n - 3)
            if j % 2 == 0 and t == 0:
                m = pk + j // 2
                pe.wait_ge(k.landed[m % RAW], 16 * (m // RAW + 1))
            for i in range(4):
                hi = 4 * j + i
                last = pe.matmul(ps[:, n % 4, i * P:(i + 1) * P], qT[:, hi, t * P:(t + 1) * P],
                                 raw_slot(k, pk + j // 2)[:, (hi % 8) * P:(hi % 8 + 1) * P], start=True, stop=True)
            last.then_inc(k.pr_s, 1)
        pe.wait_ge(k.rms_ready, r + 1)
        pe.wait_ge(k.col_rms, cq + 1)
        for n in range(4):
            t, half = n // 2, n % 2
            for i in range(4):
                last = pe.transpose(ps[:, 4 + n, i * P:(i + 1) * P], x[:, 4 * half + i, t * P:(t + 1) * P], k.ident)
            last.then_inc(k.pr_t, 1)
        pe.wait_ge(k.pr_sc, 8)
        pe.wait_ge(k.rows_in, 16)
        for g in range(2):
            for i in range(2):
                last = pe.matmul(ps[:, 2 * g + i, :], k.ones[0:1, :],
                                 gain_rows[:, g * D + i * 512:g * D + (i + 1) * 512], start=True, stop=True)
            last.then_inc(k.pr_gl, 1)

    all_end(k, block)
    k.arena.at = mark


def peer_experts(k, block, u_tab, v_tab, out):
    mark = k.arena.at
    take = k.arena.take
    NS = PE_SLOTS
    rows = take(NS, D)
    ids = take(2, NS).bitcast(U32)
    dots, w8 = take(2, NS), take(NS)
    acts = take(2, HK)
    acc = take(2, D)
    ssq, rms = take(2), take(2)
    turns = HK // NS

    @block.gpsimd
    def _(pool):
        for ph in range(4):
            tab = (u_tab, v_tab)[ph // 2]
            with pool.Fori(0, turns // 2) as i:
                for half in range(2):
                    pool.wait_ge(k.px_ids, i * 2 + (turns * ph + half + 1))
                    for s in range(NS):
                        pool.wait_ge(k.px_free, i * (2 * NS) + (NS * (turns * ph + half) + s + 1))
                        pool.sem_inc(k.px_go, 1)
                        pool.indirect_dma_start(rows[:, s, :], None, tab,
                                                bass.IndirectOffsetOnAxis(ap=ids[:, half, s:s + 1], axis=0)
                                                ).then_inc(k.px_in[s], 16)

    @block.vector
    def _(dve):
        for s in range(NS):
            dve.memset(dots[:, 0, s:s + 1], 0.0).then_inc(k.px_free, 1)
        dve.tensor_copy(ids[:, 0, :], k.expert[:, 0:NS]).then_inc(k.px_ids, 1)
        for ph in range(4):
            t = ph % 2
            for_v = ph >= 2
            if for_v:
                dve.wait_ge(k.px_gelu, t + 1)
                k.dve(dve.tensor_tensor(acts[:, t, :], acts[:, t, :], k.gate[:, t, :], ALU.mult))
                k.dve(dve.memset(acc[:, t, :], 0.0))
                k.dve.settle(dve)
            with dve.Fori(0, turns // 2) as i:
                for half in range(2):
                    used = lambda n: i * (2 * NS) + (NS * (turns * ph + half + 1) + n)
                    dve.tensor_copy(ids[:, 1 - half, :],
                                    k.expert[:, bass.ds(i * (2 * NS) + (ph * HK + (half + 1) * NS), NS)]
                                    ).then_inc(k.px_ids, 1)
                    if for_v:
                        dve.tensor_copy(w8, acts[:, t, bass.ds(i * (2 * NS) + half * NS, NS)]).then_inc(k.px_w, 1)
                        dve.wait_ge(k.px_w, i * 2 + ((ph - 2) * turns + half + 1))
                    for s in range(NS):
                        dve.wait_ge(k.px_in[s], i * 32 + 16 * (ph * turns + half + 1))
                        if for_v:
                            if s:
                                dve.wait_ge(k.px_free, used(s))
                            dve.scalar_tensor_tensor(out=acc[:, t, :], in0=rows[:, s, :], scalar=w8[:, s:s + 1],
                                                     in1=acc[:, t, :], op0=ALU.mult, op1=ALU.add
                                                     ).then_inc(k.px_free, 1)
                        else:
                            dve.tensor_tensor_reduce(rows[:, s, :], rows[:, s, :], k.ht[:, t, :], 1.0, 0.0, ALU.mult, ALU.add,
                                                     dots[:, half, s:s + 1]).then_inc(k.px_free, 1)
                    dve.wait_ge(k.px_free, used(NS))
                    if not for_v:
                        dve.tensor_copy(acts[:, t, bass.ds(i * (2 * NS) + half * NS, NS)], dots[:, half, :]).then_inc(k.px_dots, 1)
        dve.tensor_tensor(acc, acc, k.xt, ALU.add).then_inc(k.px_acc, 1)
        dve.wait_ge(k.px_rms, 2)
        k.dve(dve.reciprocal(rms, rms))
        k.dve.settle(dve)
        for t in range(2):
            dve.scalar_tensor_tensor(out=acc[:, t, :], in0=acc[:, t, :], scalar=rms[:, t:t + 1],
                                     in1=k.gain_all[:, 1, :], op0=ALU.mult, op1=ALU.mult
                                     ).then_inc(k.px_out, 1)

    @block.scalar
    def _(act):
        for t in range(2):
            act.wait_ge(k.px_dots, turns * (t + 1))
            act.activation(acts[:, t, :], acts[:, t, :], ACT.Gelu_apprx_tanh).then_inc(k.px_gelu, 1)
        act.wait_ge(k.px_acc, 1)
        for t in range(2):
            k.act(act.activation(rows[:, t, :], acc[:, t, :], ACT.Square, accum_out=ssq[:, t:t + 1]))
        k.act.settle(act)
        for t in range(2):
            act.activation(rms[:, t:t + 1], ssq[:, t:t + 1], ACT.Sqrt, bias=k.eps, scale=1.0 / D).then_inc(k.px_rms, 1)
        for t in range(2):
            act.wait_ge(k.px_out, t + 1)
            act.dma_start(out[t * P:(t + 1) * P, :], acc[:, t, :]).then_inc(k.stored, 16)
        act.wait_ge(k.stored, 32)

    k.arena.at = mark


class Shared:
    pass


def name_semaphores(k, sem):
    (k.lo_done, k.tile_done, k.hi_done, k.xh_ready, k.sq_ready, k.ss_ready, k.rms_ready,
     k.xl_ready, k.col_ss, k.col_rms, k.dve_emptied, k.act_emptied, k.small_in, k.consts_made,
     k.gate_ready, k.silu_ready, k.h_made, k.h_high, k.h_ready, k.mix_ready, k.rows_in,
     k.stored) = (
        sem(n) for n in """lo_done tile_done hi_done xh_ready sq_ready ss_ready rms_ready xl_ready col_ss
        col_rms dve_emptied act_emptied small_in consts_made gate_ready silu_ready
        h_made h_high h_ready mix_ready rows_in stored""".split())
    (k.gla_dve, k.gla_act, k.gla_s, k.gla_silu, k.gla_o, k.gla_sq, k.gla_ss, k.gla_rms,
     k.gla_wlr, k.gla_pe, k.gla_lr, k.gla_qk, k.gla_st, k.gla_copied) = (
        sem(n) for n in """gla_dve gla_act gla_s gla_silu gla_o gla_sq gla_ss gla_rms gla_wlr gla_pe gla_lr
        gla_qk gla_st gla_copied""".split())
    (k.sb_z, k.sb_sp, k.sb_ln, k.sb_log, k.sb_av, k.sb_exp, k.sb_w) = (
        sem(n) for n in """sb_z sb_sp sb_ln sb_log sb_av sb_exp sb_w""".split())
    (k.s5_act, k.s5_er, k.s5_th, k.s5_h, k.s5_coef, k.s5_made, k.s5_y, k.s5_gelu, k.s5_sig,
     k.s5_bu, k.s5_bu_used, k.s5_cu, k.s5_ys, k.s5_yg) = (
        sem(n) for n in """s5_act s5_er s5_th s5_h s5_coef s5_made s5_y s5_gelu s5_sig s5_bu s5_bu_used s5_cu
        s5_ys s5_yg""".split())
    (k.ml_conv, k.ml_xc, k.ml_qkv, k.ml_gate, k.ml_act, k.ml_dve, k.ml_mb, k.ml_den, k.ml_exp,
     k.ml_hz, k.ml_s, k.ml_ss, k.ml_sq, k.ml_rms, k.ml_bd, k.ml_vcopied, k.ml_vt, k.ml_vtc,
     k.ml_cc, k.ml_num, k.ml_sT) = (
        sem(n) for n in """ml_conv ml_xc ml_qkv ml_gate ml_act ml_dve ml_mb ml_den ml_exp ml_hz ml_s ml_ss
        ml_sq ml_rms ml_bd ml_vcopied ml_vt ml_vtc ml_cc ml_num ml_sT""".split())
    (k.pr_s, k.pr_sc, k.pr_t, k.pr_tc, k.pr_g, k.pr_gl, k.pr_ga, k.pr_e) = (
        sem(n) for n in """pr_s pr_sc pr_t pr_tc pr_g pr_gl pr_ga pr_e""".split())
    (k.px_ids, k.px_free, k.px_go, k.px_gelu, k.px_w, k.px_dots, k.px_acc, k.px_rms, k.px_out) = (
        sem(n) for n in """px_ids px_free px_go px_gelu px_w px_dots px_acc px_rms px_out""".split())


def build_program(nc, ins, out, upto=99, probe=None):
    with ExitStack() as ctx:
        k = Shared()
        name_semaphores(k, lambda n: ctx.enter_context(nc.semaphore(n)))
        width = 32700
        k.arena = Arena(ctx.enter_context(nc.sbuf_tensor("arena", [P, width], F32)), width)
        k.raw = ctx.enter_context(nc.sbuf_tensor("raw", [P, RAW, D], F32))
        k.split = ctx.enter_context(nc.sbuf_tensor("split", [P, SPLIT, 2, D], F32R))
        k.xs = ctx.enter_context(nc.sbuf_tensor("xs", [P, 2, DC, TOK], F32R))
        k.h = ctx.enter_context(nc.sbuf_tensor("h", [P, 2, 2, SEQ], F32R))
        k.ps = ctx.enter_context(nc.psum_tensor("ps", [P, 8, 512], F32))
        k.zero_bf = ctx.enter_context(nc.sbuf_tensor("zero_bf", [P, 512], BF16))[:, :]
        k.w_gk2 = ctx.enter_context(nc.sbuf_tensor("w_gk2_sb", [GLA_RANK, GLA_H * P], F32))
        k.b_if = ctx.enter_context(nc.sbuf_tensor("b_if_sb", [ML_H, 2], F32))
        k.landed = [ctx.enter_context(nc.semaphore(f"landed{s}")) for s in range(RAW)]
        k.px_in = [ctx.enter_context(nc.semaphore(f"px_in{s}")) for s in range(PE_SLOTS)]
        k.stage_sem = {e: ctx.enter_context(nc.semaphore(f"stage_{e}")) for e in ("pe", "act", "dve")}
        k.stage = {e: 0 for e in k.stage_sem}
        k.dve = Counted(ctx.enter_context(nc.semaphore("dve_steps")))
        k.act = Counted(ctx.enter_context(nc.semaphore("act_steps")))
        k.pool = Counted(ctx.enter_context(nc.semaphore("pool_steps")))
        k.norms = k.early = k.columns = k.mixes = k.dve_tiles = k.act_tiles = 0

        take = k.arena.take
        k.x = take(DC, TOK)
        k.small_all = take(SMALL_W)
        k.small = {n: k.small_all[:, a:a + w] for n, (a, w) in SMALL.items()}
        k.rms, k.rstd, k.rcol = take(TOK), take(TOK), take(2)
        k.ones, k.neg_ones, k.ident = take(P), take(P), take(P)
        k.keep_ge, k.keep_gt, k.neg_tri = take(P), take(P), take(P)
        k.head_row, k.block4 = take(ML_H, P)[0:ML_H], take(32)
        k.iota16 = take(16, 16)
        k.eps, k.one_col = take(1), take(1)
        k.ones_row = take(TOK)
        k.s5_r, k.s5_sin, k.s5_cos, k.s5_cre, k.s5_cim = (take(S5_C) for _ in range(5))
        k.s5_dt, k.s5_ere, k.s5_theta, k.s5_half = (take(S5_C) for _ in range(4))
        k.s5_tmp = [take(S5_C) for _ in range(6)]
        k.small_loads = [
            (k.x[:, :, META:TOK], ins["xT"]),
            (k.small_all, ins["small"]),
            (k.x[:, :, 0:META], ins["metaT"]),
            (k.w_gk2[:, :], ins["w_gk2"]),
            (k.b_if[:, :], ins["b_if"]),
        ]
        low = k.arena.at
        k.sq = take(DC, TOK)
        k.gate_t, k.gate_s = take(2, SEQ), take(2, SEQ)
        shared = k.arena.at

        block = ctx.enter_context(nc.Block())
        weights_in(k, block, ins["wstream"])
        setup(k, block)
        s5_parameters(k, block)
        low_parts(k, block, 0, min(AT["sb_out"] + SPLIT, SPLIT_PACKETS))
        feed_forward(k, block, 0, GAIN["ffn1_0"], AT["ffn0"])
        if upto >= 2:
            gated_linear_attention(k, block, GAIN["mix_0"])
        if upto >= 3:
            feed_forward(k, block, 1, GAIN["ffn2_0"], AT["ffn1"])
        k.arena.at = shared
        k.s5_ec, k.s5_es = take(S5_C, TOK), take(S5_C, TOK)
        tables = k.arena.at
        k.s5_big = [take(S5_C, P) for _ in range(2)]
        if upto >= 4:
            feed_forward(k, block, 2, GAIN["ffn1_1"], AT["ffn2"])
            stick_breaking(k, block, GAIN["mix_1"])
            s5_tables(k, block)
            low_parts(k, block, AT["sb_out"] + SPLIT, SPLIT_PACKETS)
        if upto >= 5:
            feed_forward(k, block, 3, GAIN["ffn2_1"], AT["ffn3"])
            final_of_first(k, block, GAIN["final"])
        top = width - 4 * TOK - DC * (TOK + 3) - 24 * SEQ
        k.arena.at = top
        if upto >= 6:
            k.u, k.xm = take(4, TOK), take(DC, TOK + 3)
            k.sig = take(24, SEQ)
            input_projection(k, block, GAIN["norm1"])
            k.arena.at, k.arena.width = tables, top
            state_space(k, block)
        if upto >= 7:
            k.arena.at, k.arena.width = low, top + 4 * TOK
            mlstm(k, block)
            k.arena.width = width
        if upto >= 8:
            mix_out(k, block)
        if upto >= 9:
            k.arena.at = low
            k.sq = take(DC, TOK)
            k.xt, k.ht = take(2, D), take(2, D)
            k.expert = take(4 * HK + PE_SLOTS).bitcast(U32)
            k.gate = take(2, HK)
            k.gain_all = take(2, D)
            peer_route(k, block, GAIN["norm2"], ins["rows"])
            peer_experts(k, block, ins["u_tab"], ins["v_tab"], out)
        else:
            probe(k, block)




def lay_out(a):
    a = {n: np.asarray(v) for n, v in a.items()}

    def columns(w, width=P):
        kc = w.shape[0] // P
        w = w.reshape(kc, P, w.shape[1] // width, width).transpose(2, 1, 0, 3)
        return w.reshape(-1, P, kc * width)

    def feed(gate, up, down):
        g, u, d = columns(gate), columns(up), down.reshape(FT, P, D)
        order = [g[0], u[0], g[1], u[1], d[0]]
        for f in range(2, FT):
            order += [g[f], u[f], d[f - 1]]
        return order + [d[FT - 1]]

    def wide(w):
        w = w.reshape(4, 2, P, w.shape[1] // 512, 512).transpose(3, 0, 2, 1, 4)
        return w.reshape(-1, P, D)

    gla_in = a["gla_w_in"][0]
    sb_in = a["sb_w_in"][0]
    ffn = lambda n, i: feed(a[f"{n}_w_gate"][i], a[f"{n}_w_up"][i], a[f"{n}_w_down"][i])
    cols = 2 * GLA_H * GLA_K + 2 * D
    keys = a["peer_sub_keys_2"][0].reshape(16, PE_N, P).transpose(2, 0, 1).reshape(P, 2, D).transpose(1, 0, 2)
    parts = [
        ffn("ffn1", 0), columns(gla_in[:, :D]), wide(gla_in[:, D:2 * D]), columns(gla_in[:, 2 * D:cols]), columns(a["gla_w_out"][0]), ffn("ffn2", 0),
        ffn("ffn1", 1), columns(sb_in[:, :2 * D]), wide(sb_in[:, 2 * D:]), columns(a["sb_w_out"][0]), ffn("ffn2", 1),
        columns(a["w_in_2"][0]), columns(a["ssm_w_glu_2"][0], 256), columns(a["w_ssm_out_2"][0], 256),
        columns(a["w_ml_out_2"][0]), columns(a["w_out_2"][0]), columns(a["peer_w_q_2"][0]), keys,
    ]
    wstream = np.concatenate([np.stack(p) if isinstance(p, list) else p for p in parts])
    assert wstream.shape == (PACKETS, P, D)

    feat = lambda v: v.reshape(-1, P).T
    gains = np.concatenate([feat(v) for v in (
        a["ffn1_norm"][0], a["mix_norm"][0], a["ffn2_norm"][0], a["ffn1_norm"][1], a["mix_norm"][1],
        a["ffn2_norm"][1], a["final_norm"], a["norm1_g_2"][0], a["norm2_g_2"][0], a["final_norm_g_2"])], 1)

    def c_blocks(c):
        o = np.zeros((2, 64, S5_C, 2, 16), c.dtype)
        c = c.reshape(S5_C, 2, 16, 64)
        for g in range(2):
            o[g, :, :, g, :] = c[:, g].transpose(2, 0, 1)
        return o.reshape(P, -1)

    def b_blocks(b):
        o = np.zeros((4, 2, 16, 4, 2, 64), b.dtype)
        b = b.reshape(4, 4, 2, 64, 16)
        for g in range(2):
            o[:, g, :, :, g, :] = b[:, :, g].transpose(1, 3, 0, 2)
        return o.reshape(P, -1)

    chunks = lambda w: w.reshape(-1, P, w.shape[-1]).transpose(1, 0, 2).reshape(P, -1)
    small = {
        "gains": gains, "b_gk": feat(a["gla_b_gk"][0]), "o_norm": feat(a["gla_o_norm"][0]),
        "w_lr": chunks(gla_in[:, cols:]),
        "a_re": feat(a["ssm_a_re_2"][0].ravel()), "a_im": feat(a["ssm_a_im_2"][0].ravel()),
        "log_dt": feat(np.repeat(a["ssm_log_dt_2"][0], 64)), "s5_d": feat(a["ssm_d_2"][0]),
        "b_glu": feat(a["ssm_b_glu_2"][0]),
        "c_re": c_blocks(a["ssm_c_re_2"][0]), "c_im": c_blocks(a["ssm_c_im_2"][0]),
        "b_re": b_blocks(a["ssm_b_re_2"][0]), "b_im": b_blocks(a["ssm_b_im_2"][0]),
        "conv_w": chunks(a["ml_conv_w_2"][0].T), "conv_b": feat(a["ml_conv_b_2"][0]),
        "wq": chunks(a["ml_wq_2"][0].reshape(D, 4)), "wk": chunks(a["ml_wk_2"][0].reshape(D, 4)),
        "wv": chunks(a["ml_wv_2"][0].reshape(D, 4)),
        "w_if": chunks(a["ml_w_if_2"][0]),
        "ml_g": feat(a["ml_norm_g_2"][0]), "ml_skip": feat(a["ml_skip_2"][0]),
    }
    for n, (_, w) in SMALL.items():
        assert small[n].shape == (P, w), (n, small[n].shape, w)
    tokens = lambda v: v.T.reshape(DC, P, -1).transpose(1, 0, 2)
    return {
        "wstream": wstream,
        "small": np.concatenate([small[n] for n in SMALL], 1),
        "xT": tokens(a["x"][0]), "metaT": tokens(a["meta_tokens_2"]),
        "w_gk2": a["gla_w_gk2"][0], "b_if": a["ml_b_if_2"][0].reshape(2, ML_H).T,
        "rows": np.concatenate([a["norm2_g_2"][0], a["final_norm_g_2"]]).reshape(1, 2 * D),
        "u_tab": a["peer_u_2"][0], "v_tab": a["peer_v_2"][0],
    }


def kernel(**inputs):
    import concourse.bacc as bacc
    from concourse.bass_utils import run_bass_kernel_spmd

    arrays = {n: np.ascontiguousarray(v) for n, v in lay_out(inputs).items()}
    nc = bacc.Bacc("TRN2", target_bir_lowering=False, num_devices=1)
    ins = {n: nc.dram_tensor(n, v.shape, mybir.dt.from_np(v.dtype), kind="ExternalInput").ap()
           for n, v in arrays.items()}
    out = nc.dram_tensor("out", (SEQ, D), F32, kind="ExternalOutput").ap()
    build_program(nc, ins, out)
    r = run_bass_kernel_spmd(nc, [arrays], core_ids=[0])
    return r.results[0]["out"].reshape(1, SEQ, D)
```

```python
from contextlib import ExitStack

import numpy as np
import concourse.bass as bass
from concourse import mybir

F32 = mybir.dt.float32
BF16 = mybir.dt.bfloat16
F32R = mybir.dt.float32r
U32 = mybir.dt.uint32
ACT = mybir.ActivationFunctionType
ALU = mybir.AluOpType
AX_X = mybir.AxisListType.X

P = 128
D = 1024
DC = D // P
SEQ = 256
META = 16
TOK = SEQ + META
DFF = 2816
FT = DFF // P
GLA_H, GLA_K, GLA_V, GLA_RANK, GLA_C = 4, 128, 256, 16, 64
GLA_B = SEQ // GLA_C
SB_H, SB_D = 16, 64
S5_C = 16
S5_W = 512
S5_BESIDE = 2200
S5_STEP = 190
S5_ANGLES = 10
ML_H, ML_D = 4, 256
PE_H, PE_K, PE_N = 8, 16, 128
HK = PE_H * PE_K
PE_SLOTS = 8
EPS = 1e-6
EXP_AND_LN = "natural_log_exp_and_others"
TWO_PI = 2 * np.pi
ROUND = 12582912.0

RAW = 6
SPLIT = 4
BODY = 12


def packet_plan():
    at, n = {}, 0
    for name, count in (
        ("ffn0", 3 * FT), ("gla_in", 24), ("gla_out", 8), ("ffn1", 3 * FT),
        ("ffn2", 3 * FT), ("sb_in", 24), ("sb_out", 8), ("ffn3", 3 * FT),
        ("w_in", 36), ("s5_glu", 2), ("s5_out", 4), ("ml_out", 8), ("w_out", 8),
        ("peer_q", 16),
    ):
        at[name] = n
        n += count
    return at, n


AT, PACKETS = packet_plan()


SMALL = {}
_n = 0
for _name, _width in (
    ("gains", 10 * DC), ("b_gk", 4), ("o_norm", 2), ("w_lr", DC * GLA_RANK),
    ("a_re", S5_C), ("a_im", S5_C), ("log_dt", S5_C), ("s5_d", 4), ("b_glu", 4),
    ("c_re", S5_C * 32), ("c_im", S5_C * 32), ("b_re", 4 * P), ("b_im", 4 * P),
    ("conv_w", DC * 4), ("conv_b", DC), ("wq", DC * 4), ("wk", DC * 4), ("wv", DC * 4),
    ("w_if", 24 * 8), ("ml_g", DC), ("ml_skip", DC),
):
    SMALL[_name] = (_n, _width)
    _n += _width
SMALL_W = _n
GAIN = {n: i for i, n in enumerate(
    ("ffn1_0", "mix_0", "ffn2_0", "ffn1_1", "mix_1", "ffn2_1", "final", "norm1", "norm2", "last"))}


class Counted:

    def __init__(self, sem):
        self.sem, self.n = sem, 0

    def __call__(self, ins):
        self.n += 1
        return ins.then_inc(self.sem, 1)

    def settle(self, eng):
        eng.wait_ge(self.sem, self.n)


class Arena:

    def __init__(self, tensor, width):
        self.t, self.at, self.width = tensor, 0, width

    def take(self, *dims):
        n = int(np.prod(dims))
        a = self.t[:, self.at:self.at + n]
        self.at += n
        assert self.at <= self.width, self.at
        if len(dims) == 2:
            a = a.rearrange("p (a b) -> p a b", b=dims[1])
        elif len(dims) == 3:
            a = a.rearrange("p (a b c) -> p a b c", b=dims[1], c=dims[2])
        elif len(dims) == 4:
            a = a.rearrange("p (a b c d) -> p a b c d", b=dims[1], c=dims[2], d=dims[3])
        return a


def spread(ap, n):
    return ap.unsqueeze(2).to_broadcast([ap.shape[0], ap.shape[1], n])


def bcast(ap, n):
    return ap.unsqueeze(1).to_broadcast([ap.shape[0], n, ap.shape[1]])




def raw_slot(k, n):
    return k.raw[:, n % RAW, :]


def parts_of(k, n):
    return k.split[:, n % SPLIT, 0, :], k.split[:, n % SPLIT, 1, :]


def wait_packet(k, pe, n):
    pe.wait_ge(k.lo_done, n + 1)


def matmul3(pe, out, w_hi, w_lo, x_hi, x_lo, start, stop, **kw):
    pe.matmul(out, w_hi, x_hi, start=start, stop=False, **kw)
    pe.matmul(out, w_hi, x_lo, start=False, stop=False, **kw)
    return pe.matmul(out, w_lo, x_hi, start=False, stop=stop, **kw)


def mm_packet(k, pe, n, out, t0=0, T=SEQ, kc=DC, col=0, width=128):
    hi, lo = (p.rearrange("p (c m) -> p c m", c=kc) for p in parts_of(k, n))
    for c in range(kc):
        last = matmul3(pe, out, hi[:, c, col:col + 128], lo[:, c, col:col + 128],
                       k.xs[:, 0, c, t0:t0 + T], k.xs[:, 1, c, t0:t0 + T], c == 0, c == kc - 1)
    return last


def refill(k, act, n, i=None):
    m = n + SPLIT
    if i is None:
        if m >= PACKETS:
            return
        act.wait_ge(k.tile_done, n + 1)
        act.wait_ge(k.landed[m % RAW], 16 * (m // RAW + 1))
    else:
        act.wait_ge(k.tile_done, i * BODY + (n + 1))
        act.wait_ge(k.landed[m % RAW], i * (16 * BODY // RAW) + 16 * (m // RAW + 1))
    act.activation(parts_of(k, m)[0], raw_slot(k, m), ACT.Copy).then_inc(k.hi_done, 1)


def split(k, dve, c, src, t0=0, T=SEQ):
    k.dve(dve.tensor_copy(k.xs[:, 0, c, t0:t0 + T], src))
    k.dve.settle(dve)
    return dve.tensor_tensor(k.xs[:, 1, c, t0:t0 + T], src, k.xs[:, 0, c, t0:t0 + T].bitcast(F32), ALU.subtract)


def stage_end(k, eng, who):
    k.stage[who] += 1
    eng.drain().then_inc(k.stage_sem[who], 1)
    for other, sem in k.stage_sem.items():
        if other != who:
            eng.wait_ge(sem, k.stage[who])




def norm_act(k, act, r, x, gain, T=SEQ, t0=0, between=lambda: None):
    made, k.x_made = k.x_made, [None] * DC
    for c in range(DC if gain is not None else 0):
        if made[c]:
            act.wait_ge(*made[c])
        g = k.small["gains"][:, gain * DC + c:gain * DC + c + 1]
        act.activation(k.xs[:, 0, c, t0:t0 + T], x[:, c, :], ACT.Copy, scale=g).then_inc(k.xh_ready, 1)
    between()
    for h in range(2):
        act.activation(k.sq[:, 4 * h:4 * h + 4, 0:T], x[:, 4 * h:4 * h + 4, :], ACT.Square).then_inc(k.sq_ready, 1)
    if r is None:
        return
    act.wait_ge(k.ss_ready, r + 1)
    act.activation(k.rms[:, 0:T], k.ps[:, 7, 0:T], ACT.Sqrt, bias=k.eps, scale=1.0 / D).then_inc(k.rms_ready, 1)


def norm_pe(k, pe, r, T=SEQ):
    for c in range(DC):
        if c % 4 == 0:
            pe.wait_ge(k.sq_ready, 2 * r + c // 4 + 1)
        last = pe.matmul(k.ps[:, 7, 0:T], k.ones, k.sq[:, c, 0:T], start=(c == 0), stop=(c == DC - 1))
    last.then_inc(k.ss_ready, 1)


def norm_low(k, dve, q, x, gain, T=SEQ, t0=0):
    for c in range(DC):
        g = k.small["gains"][:, gain * DC + c:gain * DC + c + 1]
        dve.wait_ge(k.xh_ready, DC * q + c + 1)
        dve.scalar_tensor_tensor(out=k.xs[:, 1, c, t0:t0 + T], in0=x[:, c, :], scalar=g,
                                 in1=k.xs[:, 0, c, t0:t0 + T].bitcast(F32), op0=ALU.mult, op1=ALU.subtract
                                 ).then_inc(k.xl_ready, 1)


def norm_rstd(k, dve, r, T=SEQ):
    dve.wait_ge(k.rms_ready, r + 1)
    k.dve(dve.reciprocal(k.rstd[:, 0:T], k.rms[:, 0:T]))
    k.dve.settle(dve)




def columns_pe(k, pe, q):
    for t in range(2):
        for c in range(DC):
            last = pe.matmul(k.ps[:, 5 + t, 0:1], k.sq[:, c, t * P:(t + 1) * P], k.ones[:, 0:1],
                             start=(c == 0), stop=(c == DC - 1))
    last.then_inc(k.col_ss, 1)


def columns_act(k, act, q):
    act.wait_ge(k.col_ss, q + 1)
    act.activation(k.rcol, k.ps[:, 5:7, 0], ACT.Sqrt, bias=k.eps, scale=1.0 / D).then_inc(k.col_rms, 1)


def columns_dve(k, dve, q, ready=None):
    dve.wait_ge(k.col_rms, q + 1)
    if ready is None:
        k.dve(dve.reciprocal(k.rcol, k.rcol))
        k.dve.settle(dve)
    else:
        dve.reciprocal(k.rcol, k.rcol).then_inc(ready, 1)
        dve.wait_ge(ready, 1)


class Tiles:

    def __init__(self, k, engs):
        self.k, self.engs, self.base = k, engs, (k.dve_tiles, k.act_tiles)
        k.dve_tiles += engs.count("D")
        k.act_tiles += engs.count("A")

    def wait_free(self, pe, n):
        if n >= 4:
            self.wait_emptied(pe, n - 4)

    def wait_emptied(self, pe, n):
        if self.engs[n] == "D":
            pe.wait_ge(self.k.dve_emptied, self.base[0] + self.engs[:n + 1].count("D"))
        else:
            pe.wait_ge(self.k.act_emptied, self.base[1] + self.engs[:n + 1].count("A"))




def setup(k, block):

    @block.scalar
    def _(act):
        act.wait_ge(k.x_in, 32)

    @block.vector
    def _(dve):
        k.dve(dve.memset(k.eps, EPS))
        k.dve(dve.memset(k.eps_eps, EPS * EPS))
        k.dve(dve.memset(k.ones, 1.0))
        k.dve(dve.memset(k.one_col, 1.0))
        k.dve(dve.memset(k.neg_ones, -1.0))
        k.dve(dve.memset(k.zero_bf, 0.0))
        k.dve(dve.memset(k.ones_row, 1.0))

    @block.gpsimd
    def _(pool):
        k.pool(pool.memset(k.ident, 1.0))
        k.pool(pool.memset(k.keep_ge, 1.0))
        k.pool(pool.memset(k.keep_gt, 1.0))
        k.pool(pool.memset(k.neg_tri, -1.0))
        k.pool(pool.memset(k.head_row, 1.0))
        k.pool(pool.memset(k.block4, 1.0))
        k.pool(pool.iota(k.iota16, pattern=[[0, 16], [1, 16]], base=0, channel_multiplier=0,
                         allow_small_or_imprecise_dtypes=True))
        k.pool.settle(pool)
        k.pool(pool.affine_select(out=k.ident, in_=k.ident, compare_op=ALU.is_equal, fill=0.0, base=0,
                                  pattern=[[1, P]], channel_multiplier=-1))
        k.pool(pool.affine_select(out=k.keep_ge, in_=k.keep_ge, compare_op=ALU.is_ge, fill=0.0, base=0,
                                  pattern=[[1, P]], channel_multiplier=-1))
        k.pool(pool.affine_select(out=k.keep_gt, in_=k.keep_gt, compare_op=ALU.is_gt, fill=0.0, base=0,
                                  pattern=[[1, P]], channel_multiplier=-1))
        k.pool(pool.affine_select(out=k.neg_tri, in_=k.neg_tri, compare_op=ALU.is_ge, fill=0.0, base=0,
                                  pattern=[[-1, P]], channel_multiplier=1))
        k.pool(pool.affine_select(out=k.head_row, in_=k.head_row, compare_op=ALU.is_equal, fill=0.0, base=0,
                                  pattern=[[1, ML_H], [0, P]], channel_multiplier=-1))
        k.pool(pool.affine_select(out=k.block4, in_=k.block4, compare_op=ALU.is_ge, fill=0.0, base=0,
                                  pattern=[[-4, 32]], channel_multiplier=1))
        k.pool.settle(pool)
        k.pool(pool.affine_select(out=k.block4, in_=k.block4, compare_op=ALU.is_ge, fill=0.0, base=3,
                                  pattern=[[4, 32]], channel_multiplier=-1))


    @block.gpsimd
    def _(pool):
        pool.engine_nop().then_inc(k.consts_made, 1)

    for engine in (block.scalar, block.vector, block.tensor):
        engine(lambda e: e.wait_ge(k.consts_made, 1))
    all_end(k, block)


def all_end(k, block):
    block.scalar(lambda e: stage_end(k, e, "act"))
    block.vector(lambda e: stage_end(k, e, "dve"))
    block.tensor(lambda e: stage_end(k, e, "pe"))


def weights_in(k, block, wstream):

    @block.sync
    def _(sp):
        for dst, src in k.first_loads:
            sp.dma_start(dst, src).then_inc(k.x_in, 16)
        for n in range(RAW):
            sp.dma_start(k.raw[:, n, :], wstream[n]).then_inc(k.landed[n], 16)
        for dst, src in k.small_loads:
            sp.dma_start(dst, src).then_inc(k.small_in, 16)
        full = PACKETS // RAW
        with sp.Fori(1, full) as i:
            for s in range(RAW):
                sp.wait_ge(k.lo_done, (i - 1) * RAW + (s + 1))
                sp.dma_start(k.raw[:, s, :], wstream[bass.ds(i * RAW + s, 1)].rearrange("a p m -> p (a m)")
                             ).then_inc(k.landed[s], 16)
        for n in range(full * RAW, PACKETS):
            sp.wait_ge(k.lo_done, n - RAW + 1)
            sp.dma_start(k.raw[:, n % RAW, :], wstream[n]).then_inc(k.landed[n % RAW], 16)


def low_parts(k, block, first, last):

    @block.gpsimd
    def _(pool):
        def one(n, i=None):
            pool.wait_ge(k.hi_done, n + 1 if i is None else i * BODY + (n + 1))
            hi, lo = parts_of(k, n)
            pool.tensor_tensor(lo, raw_slot(k, n), hi.bitcast(F32), ALU.subtract).then_inc(k.lo_done, 1)

        turns = (last - first) // BODY
        if turns > 1:
            with pool.Fori(0, turns) as i:
                for j in range(BODY):
                    one(first + j, i)
        for n in range(first + BODY * turns if turns > 1 else first, last):
            one(n)


def s5_functions(k, act, part):
    sm = k.small
    if part == 0:
        act.activation(k.s5_dt, sm["log_dt"], ACT.Exp).then_inc(k.s5_act, 1)
    else:
        act.wait_ge(k.s5_er, 1)
        act.activation(k.s5_r, k.s5_ere, ACT.Exp).then_inc(k.s5_act, 1)
        act.wait_ge(k.s5_th, 1)
        act.activation(k.s5_sin, k.s5_theta, ACT.Sin).then_inc(k.s5_act, 1)
        act.activation(k.s5_half, k.s5_theta, ACT.Sin, scale=0.5).then_inc(k.s5_act, 1)


def s5_steps(k, dve):
    sm = k.small
    t = k.s5_tmp
    n16 = S5_C

    def tt(out, a, b, op, n=n16):
        return n, lambda: k.dve(dve.tensor_tensor(out, a, b, op))

    def ts(out, a, s1, s2, op0, op1):
        return n16, lambda: k.dve(dve.tensor_scalar(out, a, s1, s2, op0, op1))

    def first():
        dve.wait_ge(k.s5_act, 1)
        dve.tensor_tensor(k.s5_ere, sm["a_re"], k.s5_dt, ALU.mult).then_inc(k.s5_er, 1)

    def sines():
        dve.wait_ge(k.s5_act, 4)
        k.dve(dve.tensor_tensor(t[0], k.s5_half, k.s5_half, ALU.mult))

    yield n16, first
    yield tt(k.s5_theta, sm["a_im"], k.s5_dt, ALU.mult)
    yield ts(t[0], k.s5_theta, 1.0 / TWO_PI, ROUND, ALU.mult, ALU.add)
    yield ts(t[0], t[0], -ROUND, -6.28125, ALU.add, ALU.mult)
    yield tt(k.s5_theta, k.s5_theta, t[0], ALU.add)
    c2 = round((TWO_PI - 6.28125) * 2 ** 23) / 2 ** 23
    for part in (c2, TWO_PI - 6.28125 - c2):
        yield ts(t[1], t[0], part / 6.28125, None, ALU.mult, ALU.bypass)
        yield tt(k.s5_theta, k.s5_theta, t[1], ALU.add)
    yield n16, lambda: dve.tensor_scalar(k.s5_theta, k.s5_theta, 3.1415925, -3.1415925, ALU.min, ALU.max
                                         ).then_inc(k.s5_th, 1)
    yield n16, sines
    yield ts(k.s5_cos, t[0], -2.0, 1.0, ALU.mult, ALU.add)
    yield tt(t[0], k.s5_r, k.s5_cos, ALU.mult)
    yield ts(t[0], t[0], -1.0, None, ALU.add, ALU.bypass)
    yield tt(t[1], k.s5_r, k.s5_sin, ALU.mult)
    yield tt(t[2], sm["a_re"], sm["a_re"], ALU.mult)
    yield tt(t[3], sm["a_im"], sm["a_im"], ALU.mult)
    yield tt(t[4], t[2], t[3], ALU.add)
    yield n16, lambda: k.dve(dve.reciprocal(t[5], t[4]))
    yield tt(t[2], t[0], sm["a_re"], ALU.mult)
    yield tt(t[3], t[1], sm["a_im"], ALU.mult)
    yield tt(t[2], t[2], t[3], ALU.add)
    yield tt(k.s5_cre, t[2], t[5], ALU.mult)
    yield tt(t[2], t[1], sm["a_re"], ALU.mult)
    yield tt(t[3], t[0], sm["a_im"], ALU.mult)
    yield tt(t[2], t[2], t[3], ALU.subtract)
    yield tt(k.s5_cim, t[2], t[5], ALU.mult)
    cre = sm["c_re"].rearrange("p (c m) -> p c m", c=S5_C)
    cim = sm["c_im"].rearrange("p (c m) -> p c m", c=S5_C)
    ar, ai = spread(k.s5_cre, 32), spread(k.s5_cim, 32)
    w = [k.s5_big[i // 2][:, :, 32 * (i % 2):32 * (i % 2) + 32] for i in range(4)]
    m = S5_C * 32
    yield tt(w[0], cre, ar, ALU.mult, m)
    yield tt(w[1], cim, ai, ALU.mult, m)
    yield tt(w[2], cre, ai, ALU.mult, m)
    yield tt(w[3], cim, ar, ALU.mult, m)
    yield tt(cre, w[0], w[1], ALU.subtract, m)
    yield tt(cim, w[2], w[3], ALU.add, m)
    ec, es = k.s5_ec, k.s5_es
    yield n16, lambda: k.dve(dve.memset(ec[:, :, 0:1], 1.0))
    yield n16, lambda: k.dve(dve.memset(es[:, :, 0:1], 0.0))
    pc, pn = k.s5_cos, k.s5_sin
    n = 1
    while n < TOK:
        m = min(n, TOK - n)
        bc, bs = spread(pc, m), spread(pn, m)
        a, b = k.s5_big[0][:, :, 0:m], k.s5_big[1][:, :, 0:m]
        for x, y, z, op in ((bc, bs, ec, ALU.subtract), (bs, bc, es, ALU.add)):
            yield tt(a, ec[:, :, 0:m], x, ALU.mult, S5_C * m)
            yield tt(b, es[:, :, 0:m], y, ALU.mult, S5_C * m)
            yield tt(z[:, :, n:n + m], a, b, op, S5_C * m)
        yield tt(t[0], pc, pc, ALU.mult)
        yield tt(t[1], pn, pn, ALU.mult)
        yield tt(t[2], pc, pn, ALU.mult)
        yield tt(pc, t[0], t[1], ALU.subtract)
        yield tt(pn, t[2], t[2], ALU.add)
        n *= 2


def feed_forward(k, block, q, gain, packet):
    x = k.x[:, :, META:TOK]
    r, e = k.norms, k.early
    k.norms += 1
    k.early += 1
    gate_ps, up_ps = [k.ps[:, 4 + b, 0:SEQ] for b in range(2)], [k.ps[:, 6 + b, 0:SEQ] for b in range(2)]
    y = k.ps[:, 0:4, :]
    base = FT * q

    @block.scalar
    def _(act):
        def first_parts():
            if packet == 0:
                for n in range(SPLIT):
                    act.wait_ge(k.landed[n], 16)
                    act.activation(parts_of(k, n)[0], raw_slot(k, n), ACT.Copy).then_inc(k.hi_done, 1)

        norm_act(k, act, r, x, gain, between=first_parts)

        def one(b, f):
            act.wait_ge(k.gate_ready, f)
            act.activation(k.gate_s[:, b, :], k.gate_t[:, b, :], ACT.Silu).then_inc(k.silu_ready, 1)

        refill(k, act, packet)
        one(0, base + 1)
        refill(k, act, packet + 1)
        refill(k, act, packet + 2)
        one(1, base + 2)
        refill(k, act, packet + 3)
        refill(k, act, packet + 4)
        with act.Fori(0, (FT - 2) // 4) as i:
            for j in range(4):
                n = packet + 5 + 3 * j
                refill(k, act, n, i)
                one(j % 2, i * 4 + (base + 3 + j))
                refill(k, act, n + 1, i)
                refill(k, act, n + 2, i)
        refill(k, act, packet + 3 * FT - 1)

    @block.vector
    def _(dve):
        norm_low(k, dve, e, x, gain)
        norm_rstd(k, dve, r)

        def one(b, f, n_gate, n_up, first=False):
            dve.wait_ge(k.tile_done, n_gate)
            if not first:
                dve.wait_ge(k.silu_ready, f - 2)
            dve.tensor_tensor(k.gate_t[:, b, :], gate_ps[b], k.rstd[:, 0:SEQ], ALU.mult).then_inc(k.gate_ready, 1)
            dve.wait_ge(k.tile_done, n_up)
            dve.wait_ge(k.silu_ready, f)
            h, hh, hl = k.gate_s[:, b, :], k.h[:, b, 0, :], k.h[:, b, 1, :]
            dve.tensor_tensor(h, h, up_ps[b], ALU.mult).then_inc(k.h_made, 1)
            dve.wait_ge(k.h_made, f)
            dve.tensor_copy(hh, h).then_inc(k.h_high, 1)
            dve.wait_ge(k.h_high, f)
            dve.tensor_tensor(hl, h, hh.bitcast(F32), ALU.subtract).then_inc(k.h_ready, 1)

        one(0, base + 1, packet + 1, packet + 2, first=True)
        one(1, base + 2, packet + 3, packet + 4, first=True)
        with dve.Fori(0, (FT - 2) // 4) as i:
            for j in range(4):
                n = packet + 5 + 3 * j
                one(j % 2, i * 4 + (base + 3 + j), i * BODY + (n + 1), i * BODY + (n + 2))
        dve.wait_ge(k.h_ready, base + FT)
        k.dve(dve.tensor_scalar(k.rstd[:, 0:SEQ], k.rstd[:, 0:SEQ], 0.5, None, ALU.mult))
        k.dve.settle(dve)
        dve.wait_ge(k.tile_done, packet + 3 * FT)
        for b in range(5):
            if b:
                k.dve.settle(dve)
            if b < 4:
                k.dve(dve.tensor_tensor(k.sq[:, 2 * b:2 * b + 2, 0:SEQ], y[:, b, :].rearrange("p (a t) -> p a t", a=2),
                                        bcast(k.rstd[:, 0:SEQ], 2), ALU.mult))
            if b:
                xb = x[:, 2 * b - 2:2 * b, :]
                dve.tensor_tensor(xb, xb, k.sq[:, 2 * b - 2:2 * b, 0:SEQ], ALU.add).then_inc(k.x_added, 1)

    @block.tensor
    def _(pe):
        def half(w, b, n, wait, first=False):
            pe.wait_ge(k.lo_done, wait)
            hi, lo = (p.rearrange("p (c m) -> p c m", c=DC) for p in parts_of(k, n))
            for c in range(DC):
                if first:
                    pe.wait_ge(k.xl_ready, DC * e + c + 1)
                last = matmul3(pe, (gate_ps, up_ps)[w][b], hi[:, c, :], lo[:, c, :],
                               k.xs[:, 0, c, 0:SEQ], k.xs[:, 1, c, 0:SEQ], c == 0, c == DC - 1)
            last.then_inc(k.tile_done, 1)

        def down(b, n, wait, f, stop=False):
            pe.wait_ge(k.h_ready, f)
            pe.wait_ge(k.lo_done, wait)
            hi, lo = parts_of(k, n)
            for c in range(DC):
                last = matmul3(pe, y[:, c // 2, (c % 2) * SEQ:(c % 2 + 1) * SEQ], hi[:, c * P:(c + 1) * P],
                               lo[:, c * P:(c + 1) * P], k.h[:, b, 0, :], k.h[:, b, 1, :], False, stop,
                               skip_group_check=True)
            last.then_inc(k.tile_done, 1)

        half(0, 0, packet, packet + 1, first=True)
        for b in range(4):
            pe.matmul(y[:, b, :], k.zero_bf[:, 0:P], k.zero_bf, start=True, stop=False, skip_group_check=True)
        norm_pe(k, pe, r)
        half(1, 0, packet + 1, packet + 2)
        half(0, 1, packet + 2, packet + 3)
        pe.wait_ge(k.rms_ready, r + 1)
        half(1, 1, packet + 3, packet + 4)
        down(0, packet + 4, packet + 5, base + 1)
        with pe.Fori(0, (FT - 2) // 4) as i:
            for j in range(4):
                n = packet + 5 + 3 * j
                pe.wait_ge(k.h_ready, i * 4 + (base + 1 + j))
                half(0, j % 2, n, i * BODY + (n + 1))
                half(1, j % 2, n + 1, i * BODY + (n + 2))
                down((1 + j) % 2, n + 2, i * BODY + (n + 3), i * 4 + (base + 2 + j))
        n = packet + 3 * FT - 1
        down((FT - 1) % 2, n, n + 1, base + FT, stop=True)

    k.x_made = [(k.x_added, 4 * q + c // 2 + 1) for c in range(DC)]


def add_projection(k, block, packet, ready, count):
    tiles = Tiles(k, ["D"] * 8)

    @block.tensor
    def _(pe):
        for n in range(8):
            if n == 0:
                pe.wait_ge(ready, count)
            tiles.wait_free(pe, n)
            wait_packet(k, pe, packet + n)
            mm_packet(k, pe, packet + n, k.ps[:, n % 4, 0:SEQ]).then_inc(k.tile_done, 1)

    @block.scalar
    def _(act):
        for n in range(8):
            refill(k, act, packet + n)

    @block.vector
    def _(dve):
        for n in range(8):
            dve.wait_ge(k.tile_done, packet + n + 1)
            xb = k.x[:, n, META:TOK]
            dve.tensor_tensor(xb, k.ps[:, n % 4, 0:SEQ], xb, ALU.add).then_inc(k.dve_emptied, 1)

    k.x_made = [(k.tile_done, packet + 8)] * 4 + [(k.dve_emptied, tiles.base[0] + n + 1) for n in range(4, DC)]


def wide_packets(k, pe, n0, banks, free):
    for j in range(4):
        if j == 0:
            free()
        wait_packet(k, pe, n0 + j)
        hi, lo = (p.rearrange("p (c m) -> p c m", c=2) for p in parts_of(k, n0 + j))
        for t in range(2):
            for i in range(2):
                c = 2 * j + i
                last = matmul3(pe, k.ps[:, banks[t], :], k.xs[:, 0, c, t * P:(t + 1) * P],
                               k.xs[:, 1, c, t * P:(t + 1) * P], hi[:, i, :], lo[:, i, :], c == 0, c == DC - 1)
        last.then_inc(k.tile_done, 1)


def gated_linear_attention(k, block, gain):
    x = k.x[:, :, META:TOK]
    sm, ps = k.small, k.ps
    r, e0, cq = k.norms, k.early, k.columns
    k.norms += 1
    k.early += 1
    k.columns += 1
    mark = k.arena.at
    take = k.arena.take
    H, B, C = GLA_H, GLA_B, GLA_C
    qs, ks = take(H, SEQ), take(H, SEQ)
    vt = take(2, D)
    sg = take(DC, SEQ)
    lr = take(SEQ)
    zb_at = k.arena.at
    zb, az, cum = take(H, SEQ), take(H, SEQ), take(H, SEQ)
    la = zb
    up, down_ = take(H, B), take(H, B)
    off = [0]
    for i in range(B):
        off.append(off[-1] + C * (i + 1))
    eq, ek = take(H, SEQ), take(H, off[B])
    st = take(2, 3 * P)
    o = take(H, 2 * SEQ)
    osq = k.arena.t[:, zb_at:zb_at + 2 * H * SEQ].rearrange("p (h t) -> p h t", h=H)
    rms = take(H, SEQ)
    wlr = sm["w_lr"].rearrange("p (c m) -> p c m", c=DC)
    tiles = Tiles(k, ["D"] * 20)
    p0 = AT["gla_in"]

    for engine in (block.scalar, block.vector, block.tensor):
        engine(lambda e: e.wait_ge(k.small_in, 16 * len(k.small_loads)))

    @block.scalar
    def _(act):
        norm_act(k, act, r, x, gain)
        columns_act(k, act, cq)
        for n in range(3):
            refill(k, act, p0 + n)
        act.preload_act_table_set(EXP_AND_LN)
        act.wait_ge(k.gla_dve, 1)
        k.act(act.activation(az, az, ACT.Exp, scale=-1.0))
        k.act.settle(act)
        act.activation(az, az, ACT.Ln, bias=k.one_col).then_inc(k.gla_act, 1)
        for n in range(3, 8):
            refill(k, act, p0 + n)
        act.wait_ge(k.gla_dve, 2)
        for h in range(H):
            for i in range(B):
                act.activation(eq[:, h, C * i:C * (i + 1)], cum[:, h, C * i:C * (i + 1)], ACT.Exp,
                               bias=down_[:, h, i:i + 1], scale=1.0 / 16)
                last = act.activation(ek[:, h, off[i]:off[i + 1]], cum[:, h, 0:C * (i + 1)], ACT.Exp,
                                      bias=up[:, h, i:i + 1], scale=-1.0 / 16)
            last.then_inc(k.gla_act, 1)
            refill(k, act, p0 + 8 + 2 * h)
            refill(k, act, p0 + 9 + 2 * h)

        def square(h):
            act.wait_ge(k.gla_o, h + 1)
            act.activation(osq[:, h, :], ps[:, 6 + h % 2, :], ACT.Square).then_inc(k.gla_sq, 1)

        def root(i):
            act.wait_ge(k.gla_ss, i + 1)
            act.activation(rms[:, 2 * i:2 * i + 2, :], ps[:, 4 + i, :].rearrange("p (a t) -> p a t", a=2), ACT.Sqrt,
                           bias=k.eps, scale=1.0 / GLA_V).then_inc(k.gla_rms, 1)

        for n in range(8):
            refill(k, act, p0 + 16 + n)
            act.wait_ge(k.dve_emptied, tiles.base[0] + 13 + n)
            act.activation(sg[:, n, :], sg[:, n, :], ACT.Silu).then_inc(k.gla_silu, 1)
            if n in (3, 5, 7):
                square((n - 3) // 2)
        root(0)
        square(3)
        root(1)

    @block.vector
    def _(dve):
        norm_low(k, dve, e0, x, gain)
        for c in range(DC):
            g = sm["gains"][:, gain * DC + c:gain * DC + c + 1]
            last = dve.tensor_scalar(wlr[:, c, :], wlr[:, c, :], g, None, ALU.mult)
        last.then_inc(k.gla_wlr, 1)
        k.dve(dve.memset(st, 0.0))
        norm_rstd(k, dve, r)
        columns_dve(k, dve, cq)
        dve.wait_ge(k.gla_pe, 1)
        dve.tensor_tensor(lr[0:GLA_RANK, :], ps[0:GLA_RANK, 4, 0:SEQ], k.rstd[0:GLA_RANK, 0:SEQ], ALU.mult
                          ).then_inc(k.gla_lr, 1)
        dve.wait_ge(k.gla_pe, 2)
        for h in range(H):
            k.dve(dve.tensor_scalar(zb[:, h, :], ps[:, 4 + h // 2, (h % 2) * SEQ:(h % 2 + 1) * SEQ],
                                    sm["b_gk"][:, h:h + 1], None, ALU.add))
        k.dve.settle(dve)
        dve.scalar_tensor_tensor(out=az, in0=zb, scalar=-1.0, in1=zb, op0=ALU.mult, op1=ALU.max
                                 ).then_inc(k.gla_dve, 1)
        rstd = k.rstd[:, 0:SEQ]
        for n in range(4):
            dve.wait_ge(k.tile_done, p0 + n + 1)
            dve.scalar_tensor_tensor(out=qs[:, n, :], in0=ps[:, n % 4, 0:SEQ], scalar=GLA_K ** -0.5, in1=rstd,
                                     op0=ALU.mult, op1=ALU.mult).then_inc(k.dve_emptied, 1)
        dve.wait_ge(k.gla_act, 1)
        k.dve(dve.scalar_tensor_tensor(out=la, in0=zb, scalar=0.0, in1=az, op0=ALU.min, op1=ALU.subtract))
        k.dve.settle(dve)
        for h in range(H):
            k.dve(dve.tensor_tensor_scan(cum[:, h, :], k.ones_row[:, 0:SEQ], la[:, h, :], 0.0, ALU.mult, ALU.add))
        k.dve.settle(dve)
        mid = cum.rearrange("p h (i c) -> p h i c", c=C)[:, :, :, C // 2 - 1]
        k.dve(dve.tensor_scalar(up, mid, 1.0 / 16, None, ALU.mult))
        k.dve.settle(dve)
        dve.tensor_scalar(down_, mid, -1.0 / 16, None, ALU.mult).then_inc(k.gla_dve, 1)
        for n in range(4, 8):
            dve.wait_ge(k.tile_done, p0 + n + 1)
            dve.tensor_tensor(ks[:, n - 4, :], ps[:, n % 4, 0:SEQ], rstd, ALU.mult).then_inc(k.dve_emptied, 1)
        for half in range(2):
            dve.wait_ge(k.tile_done, p0 + 8 + 4 * (half + 1))
            for t in range(2):
                dve.tensor_scalar(vt[:, t, half * 512:(half + 1) * 512], ps[:, 2 * half + t, :], k.rcol[:, t:t + 1],
                                  None, ALU.mult).then_inc(k.dve_emptied, 1)
        dve.wait_ge(k.dve_emptied, tiles.base[0] + 12)

        def empty(n):
            dve.wait_ge(k.tile_done, p0 + 17 + n)
            dve.tensor_tensor(sg[:, n, :], ps[:, n % 4, 0:SEQ], rstd, ALU.mult).then_inc(k.dve_emptied, 1)

        def decayed(h):
            dve.wait_ge(k.gla_act, 2 + h)
            dve.tensor_tensor(eq[:, h, :], eq[:, h, :], qs[:, h, :], ALU.mult).then_inc(k.gla_qk, 1)
            for i in range(B):
                e = ek[:, h, off[i]:off[i + 1]]
                dve.tensor_tensor(e, e, ks[:, h, 0:C * (i + 1)], ALU.mult).then_inc(k.gla_qk, 1)

        def masked(h):
            b, s = ps[:, 4 + h % 2, :], st[:, h % 2, :]
            dve.wait_ge(k.gla_s, h + 1)
            if h >= 2:
                dve.wait_ge(k.gla_o, h - 1)
            m = k.keep_ge
            dve.tensor_tensor(s[0:C, 0:C], b[0:C, 0:C], m[0:C, 0:C], ALU.mult)
            dve.tensor_tensor(s[:, C:2 * C], b[:, C:2 * C], m[:, C:2 * C], ALU.mult)
            dve.tensor_copy(s[:, 2 * C:4 * C], b[:, 2 * C:4 * C])
            dve.tensor_tensor(s[0:C, 4 * C:5 * C], b[0:C, 4 * C:5 * C], m[0:C, 0:C], ALU.mult)
            dve.tensor_tensor(s[:, 5 * C:6 * C], b[:, 5 * C:6 * C], m[:, C:2 * C], ALU.mult).then_inc(k.gla_st, 1)

        def copied(h):
            dve.wait_ge(k.gla_sq, h + 1)
            dve.tensor_copy(o[:, h, :], ps[:, 6 + h % 2, :]).then_inc(k.gla_copied, 1)

        def normed(h):
            dve.wait_ge(k.gla_copied, h + 1)
            dve.wait_ge(k.gla_rms, h // 2 + 1)
            k.dve(dve.reciprocal(rms[:, h, :], rms[:, h, :]))
            k.dve.settle(dve)
            for e in range(2):
                oe = o[:, h, e * SEQ:(e + 1) * SEQ]
                k.dve(dve.scalar_tensor_tensor(out=oe, in0=oe, scalar=sm["o_norm"][:, e:e + 1], in1=rms[:, h, :],
                                               op0=ALU.mult, op1=ALU.mult))
            k.dve.settle(dve)
            g = sg[:, 2 * h:2 * h + 2, :]
            oh = o[:, h, :].rearrange("p (e t) -> p e t", e=2)
            k.dve(dve.tensor_tensor(g, g, oh, ALU.mult))
            k.dve.settle(dve)
            for c in (2 * h, 2 * h + 1):
                k.dve(dve.tensor_copy(k.xs[:, 0, c, 0:SEQ], sg[:, c, :]))
            k.dve.settle(dve)
            for c in (2 * h, 2 * h + 1):
                dve.tensor_tensor(k.xs[:, 1, c, 0:SEQ], sg[:, c, :], k.xs[:, 0, c, 0:SEQ].bitcast(F32), ALU.subtract
                                  ).then_inc(k.mix_ready, 1)

        for n in range(8):
            if n % 2 == 0:
                h = n // 2
                decayed(h)
                if h >= 2:
                    copied(h - 2)
                if h >= 1:
                    masked(h - 1)
            empty(n)
        copied(2)
        masked(3)
        dve.wait_ge(k.gla_silu, 8)
        dve.wait_ge(k.tile_done, p0 + 24)
        normed(0)
        normed(1)
        copied(3)
        normed(2)
        normed(3)

    @block.tensor
    def _(pe):
        def tile(n):
            f = n if n < 8 else n - 4
            tiles.wait_free(pe, f)
            wait_packet(k, pe, p0 + n)
            mm_packet(k, pe, p0 + n, ps[:, f % 4, 0:SEQ]).then_inc(k.tile_done, 1)

        pe.wait_ge(k.xl_ready, DC * (e0 + 1))
        tile(0)
        norm_pe(k, pe, r)
        columns_pe(k, pe, cq)
        pe.wait_ge(k.gla_wlr, 1)
        for c in range(DC):
            last = pe.matmul(ps[0:GLA_RANK, 4, 0:SEQ], wlr[:, c, :], x[:, c, :], start=(c == 0), stop=(c == DC - 1))
        last.then_inc(k.gla_pe, 1)
        tile(1)
        pe.wait_ge(k.gla_lr, 1)
        pe.wait_ge(k.col_rms, cq + 1)
        for h in range(H):
            last = pe.matmul(ps[:, 4 + h // 2, (h % 2) * SEQ:(h % 2 + 1) * SEQ],
                             k.w_gk2[:, h * P:(h + 1) * P], lr[0:GLA_RANK, :], start=True, stop=True)
        last.then_inc(k.gla_pe, 1)
        for n in range(2, 8):
            tile(n)
        for half in range(2):
            def free():
                for t in range(2):
                    tiles.wait_free(pe, 8 + 2 * half + t)
            wide_packets(k, pe, p0 + 8 + 4 * half, (2 * half, 2 * half + 1), free)
        def scores(h):
            b = ps[:, 4 + h % 2, :]
            pe.wait_ge(k.gla_qk, 5 * (h + 1))
            if h >= 2:
                pe.wait_ge(k.gla_st, h - 1)
            q = lambda i: eq[:, h, C * i:C * (i + 1)]
            kk = lambda i, lo, n: ek[:, h, off[i] + lo:off[i] + lo + n]
            pe.matmul(b[0:C, 0:C], kk(0, 0, C), q(0), start=True, stop=True)
            pe.matmul(b[:, C:2 * C], kk(1, 0, P), q(1), start=True, stop=True)
            pe.matmul(b[:, 2 * C:3 * C], kk(2, 0, P), q(2), start=True, stop=True)
            pe.matmul(b[:, 3 * C:4 * C], kk(3, 0, P), q(3), start=True, stop=True)
            pe.matmul(b[0:C, 4 * C:5 * C], kk(2, P, C), q(2), start=True, stop=True)
            pe.matmul(b[:, 5 * C:6 * C], kk(3, P, P), q(3), start=True, stop=True).then_inc(k.gla_s, 1)

        def outputs(h):
            pe.wait_ge(k.gla_st, h + 1)
            if h >= 2:
                pe.wait_ge(k.gla_copied, h - 1)
                pe.wait_ge(k.gla_sq, h - 1)
            s = st[:, h % 2, :]
            for e in range(2):
                b = ps[:, 6 + h % 2, e * SEQ:(e + 1) * SEQ]
                v = lambda t: vt[:, t, h * GLA_V + e * P:h * GLA_V + (e + 1) * P]
                pe.matmul(b, v(0), s[:, 0:SEQ], start=True, stop=False, skip_group_check=True)
                last = pe.matmul(b[:, P:SEQ], v(1), s[:, SEQ:SEQ + P], start=False, stop=True, skip_group_check=True)
            last.then_inc(k.gla_o, 1)

        def squares(i):
            pe.wait_ge(k.gla_sq, 2 * i + 2)
            pe.wait_ge(k.gla_st, 3 + i)
            for h in (2 * i, 2 * i + 1):
                for e in range(2):
                    last = pe.matmul(ps[:, 4 + i, (h % 2) * SEQ:(h % 2 + 1) * SEQ], k.ones, osq[:, h, e * SEQ:(e + 1) * SEQ],
                                     start=(e == 0), stop=(e == 1))
            last.then_inc(k.gla_ss, 1)

        for h in range(H):
            tile(16 + 2 * h)
            tile(17 + 2 * h)
            scores(h)
            if h >= 1:
                outputs(h - 1)
        squares(0)
        outputs(3)
        squares(1)

    k.mixes += DC
    add_projection(k, block, AT["gla_out"], k.mix_ready, k.mixes)
    k.arena.at = mark


def stick_breaking(k, block, gain):
    x = k.x[:, :, META:TOK]
    ps = k.ps
    r, e0, cq = k.norms, k.early, k.columns
    k.norms += 1
    k.early += 1
    k.columns += 1
    mark = k.arena.at
    take = k.arena.take
    qs, ks = take(DC, SEQ), take(DC, SEQ)
    vt = take(2, D)
    ab, spl, w = take(2, 3 * P), take(2, 3 * P), take(2, 3 * P)
    tiles = Tiles(k, ["D"] * 20)
    p0 = AT["sb_in"]
    N3 = 3 * P
    diag = lambda a: a.rearrange("p (j t) -> p j t", j=3)[:, 0:3:2, :]
    mask = bcast(k.keep_gt, 2)

    @block.scalar
    def _(act):
        s5_functions(k, act, 0)
        norm_act(k, act, r, x, gain)
        columns_act(k, act, cq)
        for n in range(24):
            refill(k, act, p0 + n)
            if n == 1:
                s5_functions(k, act, 1)
        act.preload_act_table_set(EXP_AND_LN)
        for h in range(SB_H + 1):
            if h < SB_H:
                b = ps[:, 4 + h % 2, 0:N3]
                a = ab[:, h % 2, :]
                act.wait_ge(k.sb_z, h + 1)
                if h >= 2:
                    act.wait_ge(k.sb_sp, h - 1)
                k.act(act.activation(a, b, ACT.Abs))
                k.act.settle(act)
                k.act(act.activation(a, a, ACT.Exp, scale=-1.0))
                k.act.settle(act)
                act.activation(a, a, ACT.Ln, bias=k.one_col).then_inc(k.sb_ln, 1)
            if h >= 1:
                g = h - 1
                act.wait_ge(k.sb_log, g + 1)
                if g >= 2:
                    act.wait_ge(k.sb_av, g - 1)
                act.activation(w[:, g % 2, :], ps[:, 4 + g % 2, 0:N3], ACT.Exp).then_inc(k.sb_exp, 1)

    @block.vector
    def _(dve):
        steps = list(s5_steps(k, dve))

        def beside(most):
            elements = 0
            while steps and elements < most:
                cost, step = steps.pop(0)
                step()
                k.dve.settle(dve)
                elements += cost + S5_STEP

        beside(S5_ANGLES * (S5_C + S5_STEP))
        norm_low(k, dve, e0, x, gain)
        norm_rstd(k, dve, r)
        columns_dve(k, dve, cq)
        rstd = k.rstd[:, 0:SEQ]
        for n in range(16):
            dve.wait_ge(k.tile_done, p0 + n + 1)
            if n < 8:
                i = dve.scalar_tensor_tensor(out=qs[:, n, :], in0=ps[:, n % 4, 0:SEQ], scalar=SB_D ** -0.5, in1=rstd,
                                             op0=ALU.mult, op1=ALU.mult)
            else:
                i = dve.tensor_tensor(ks[:, n - 8, :], ps[:, n % 4, 0:SEQ], rstd, ALU.mult)
            i.then_inc(k.dve_emptied, 1)
            beside(S5_BESIDE)
        for half in range(2):
            dve.wait_ge(k.tile_done, p0 + 16 + 4 * (half + 1))
            for t in range(2):
                dve.tensor_scalar(vt[:, t, half * 512:(half + 1) * 512], ps[:, 2 * half + t, :], k.rcol[:, t:t + 1],
                                  None, ALU.mult).then_inc(k.dve_emptied, 1)
            beside(3 * S5_BESIDE)
        beside(10 ** 9)
        gains = k.small["gains"]
        dve.tensor_tensor(k.both_gains, gains[:, GAIN["final"] * DC:(GAIN["final"] + 1) * DC],
                          gains[:, GAIN["norm1"] * DC:(GAIN["norm1"] + 1) * DC], ALU.mult).then_inc(k.gains_made, 1)
        for h in range(SB_H + 2):
            if h < SB_H:
                dve.wait_ge(k.sb_ln, h + 1)
                if h >= 2:
                    dve.wait_ge(k.sb_log, h - 1)
                s = spl[:, h % 2, :]
                k.dve(dve.scalar_tensor_tensor(out=s, in0=ps[:, 4 + h % 2, 0:N3], scalar=0.0, in1=ab[:, h % 2, :],
                                               op0=ALU.max, op1=ALU.add))
                k.dve.settle(dve)
                dve.tensor_tensor(diag(s), diag(s), mask, ALU.mult).then_inc(k.sb_sp, 1)
            if 1 <= h <= SB_H:
                g = h - 1
                dve.wait_ge(k.sb_exp, g + 1)
                s = diag(w[:, g % 2, :])
                dve.scalar_tensor_tensor(out=s, in0=s, scalar=1.0, in1=mask, op0=ALU.min, op1=ALU.mult
                                         ).then_inc(k.sb_w, 1)
            if h >= 2 and (h - 2) % 2 == 1:
                g = h - 2
                dve.wait_ge(k.sb_av, g + 1)
                split(k, dve, g // 2, ps[:, 6 + (g // 2) % 2, 0:SEQ]).then_inc(k.mix_ready, 1)

    @block.tensor
    def _(pe):
        pe.wait_ge(k.xl_ready, DC * (e0 + 1))
        for n in range(16):
            tiles.wait_free(pe, n)
            wait_packet(k, pe, p0 + n)
            mm_packet(k, pe, p0 + n, ps[:, n % 4, 0:SEQ]).then_inc(k.tile_done, 1)
            if n == 0:
                norm_pe(k, pe, r)
                columns_pe(k, pe, cq)
        for half in range(2):
            def free():
                for t in range(2):
                    tiles.wait_free(pe, 16 + 2 * half + t)
            wide_packets(k, pe, p0 + 16 + 4 * half, (2 * half, 2 * half + 1), free)
        tiles.wait_emptied(pe, 19)
        pe.wait_ge(k.col_rms, cq + 1)
        for h in range(SB_H + 2):
            if h < SB_H:
                b = ps[:, 4 + h % 2, :]
                lo = SB_D * (h % 2)
                kt, qt = ks[lo:lo + SB_D, h // 2, :], qs[lo:lo + SB_D, h // 2, :]
                if h >= 2:
                    pe.wait_ge(k.sb_exp, h - 1)
                pe.matmul(b[:, 0:SEQ], kt[:, 0:P], qt, start=True, stop=False, skip_group_check=True)
                pe.matmul(b[:, SEQ:N3], kt[:, P:SEQ], qt[:, P:SEQ], start=False, stop=False, skip_group_check=True
                          ).then_inc(k.sb_z, 1)
            if 1 <= h <= SB_H:
                g = h - 1
                b, s = ps[:, 4 + g % 2, :], spl[:, g % 2, :]
                pe.wait_ge(k.sb_sp, g + 1)
                pe.matmul(b[:, 0:SEQ], k.neg_tri, s[:, 0:SEQ], start=False, stop=False, skip_group_check=True)
                pe.matmul(b[:, P:SEQ], k.neg_ones, s[:, SEQ:N3], start=False, stop=False, skip_group_check=True)
                pe.matmul(b[:, SEQ:N3], k.neg_tri, s[:, SEQ:N3], start=False, stop=True, skip_group_check=True
                          ).then_inc(k.sb_log, 1)
            if h >= 2:
                g = h - 2
                pe.wait_ge(k.sb_w, g + 1)
                if g >= 4 and g % 2 == 0:
                    pe.wait_ge(k.mix_ready, k.mixes + g // 2 - 1)
                lo = SB_D * (g % 2)
                b = ps[lo:lo + SB_D, 6 + (g // 2) % 2, :]
                v = lambda t: vt[:, t, g * SB_D:(g + 1) * SB_D]
                pe.matmul(b[:, 0:SEQ], v(0), w[:, g % 2, 0:SEQ], start=True, stop=False, skip_group_check=True)
                pe.matmul(b[:, P:SEQ], v(1), w[:, g % 2, SEQ:N3], start=False, stop=True, skip_group_check=True
                          ).then_inc(k.sb_av, 1)

    k.mixes += DC
    add_projection(k, block, AT["sb_out"], k.mix_ready, k.mixes)
    k.arena.at = mark




def between_act(k, act, r1, final, gain):
    r2 = r1 + 1
    gains = k.small["gains"]
    made, k.x_made = k.x_made, [None] * DC
    seq, meta = k.x[:, :, META:TOK], k.x[:, :, 0:META]
    act.wait_ge(k.gains_made, 1)
    for c in range(DC):
        act.wait_ge(*made[c])
        act.activation(k.xs[:, 0, c, META:TOK], seq[:, c, :], ACT.Copy, scale=k.both_gains[:, c:c + 1])
        act.activation(k.xs[:, 0, c, 0:META], meta[:, c, :], ACT.Copy, scale=gains[:, gain * DC + c:gain * DC + c + 1]
                       ).then_inc(k.xh_ready, 1)
    for h in range(2):
        act.activation(k.sq[:, 4 * h:4 * h + 4, 0:SEQ], seq[:, 4 * h:4 * h + 4, :], ACT.Square).then_inc(k.sq_ready, 1)
    act.activation(k.sq_gf[:, :, 0:META], meta, ACT.Square)
    for c in range(DC):
        i = act.activation(k.sq_gf[:, c, META:TOK], seq[:, c, :], ACT.Square, scale=gains[:, final * DC + c:final * DC + c + 1])
        if c % 4 == 3:
            i.then_inc(k.sq_ready, 1)
    act.wait_ge(k.ss_ready, r1 + 1)
    act.activation(k.rms[:, META:TOK], k.ps[:, 6, 0:SEQ], ACT.Identity, bias=k.eps_eps, scale=EPS / D).then_inc(k.eps_part, 1)
    act.activation(k.rms_first, k.ps[:, 6, 0:SEQ], ACT.Sqrt, bias=k.eps, scale=1.0 / D).then_inc(k.rms_ready, 1)
    act.wait_ge(k.var_made, 1)
    act.activation(k.rms, k.rstd, ACT.Sqrt).then_inc(k.rms_ready, 1)


def between_pe(k, pe, r1):
    for n, (sq, T, b) in enumerate(((k.sq, SEQ, 6), (k.sq_gf, TOK, 7))):
        for c in range(DC):
            if c % 4 == 0:
                pe.wait_ge(k.sq_ready, 2 * (r1 + n) + c // 4 + 1)
            last = pe.matmul(k.ps[:, b, 0:T], k.ones, sq[:, c, 0:T], start=(c == 0), stop=(c == DC - 1))
        last.then_inc(k.ss_ready, 1)


def between_low(k, dve, q, gain):
    k.dve(dve.memset(k.rms[:, 0:META], EPS))
    for c in range(DC):
        g = k.small["gains"][:, gain * DC + c:gain * DC + c + 1]
        dve.wait_ge(k.xh_ready, DC * q + c + 1)
        dve.scalar_tensor_tensor(out=k.xs[:, 1, c, META:TOK], in0=k.x[:, c, META:TOK], scalar=k.both_gains[:, c:c + 1],
                                 in1=k.xs[:, 0, c, META:TOK].bitcast(F32), op0=ALU.mult, op1=ALU.subtract)
        dve.scalar_tensor_tensor(out=k.xs[:, 1, c, 0:META], in0=k.x[:, c, 0:META], scalar=g,
                                 in1=k.xs[:, 0, c, 0:META].bitcast(F32), op0=ALU.mult, op1=ALU.subtract
                                 ).then_inc(k.xl_ready, 1)


def between_rstd(k, dve, r1):
    dve.wait_ge(k.ss_ready, r1 + 2)
    dve.wait_ge(k.eps_part, 1)
    k.dve.settle(dve)
    dve.scalar_tensor_tensor(out=k.rstd, in0=k.ps[:, 7, 0:TOK], scalar=1.0 / D, in1=k.rms, op0=ALU.mult, op1=ALU.add
                             ).then_inc(k.var_made, 1)
    dve.wait_ge(k.rms_ready, r1 + 2)
    k.dve(dve.reciprocal(k.rstd, k.rms))
    k.dve.settle(dve)


def input_and_states(k, block, final, gain):
    ps, sm = k.ps, k.small
    r, e0 = k.norms, k.early
    k.norms += 2
    k.early += 1
    mark = k.arena.at
    take = k.arena.take
    k.sq_gf = take(DC, TOK)
    k.arena.at = mark
    v, hh, t4 = take(2, TOK), take(2, 2, TOK), take(4, TOK)
    y, yg = k.sq[:, 0:4, 0:SEQ], k.sq[:, 4:8, 0:SEQ]
    bre = sm["b_re"].rearrange("p (j m) -> p j m", j=4)
    bim = sm["b_im"].rearrange("p (j m) -> p j m", j=4)
    cre = sm["c_re"].rearrange("p (c m) -> p c m", c=S5_C)
    cim = sm["c_im"].rearrange("p (c m) -> p c m", c=S5_C)
    ec, es = k.s5_ec, k.s5_es
    p0, pg, po = AT["w_in"], AT["s5_glu"], AT["s5_out"]
    tiles = Tiles(k, ["D"] * 36)
    bank = (0, 1, 2, 7)
    y_ps = [ps[:, 5 + j // 2, (j % 2) * SEQ:(j % 2 + 1) * SEQ] for j in range(4)]

    @block.scalar
    def _(act):
        between_act(k, act, r, final, gain)
        for n in range(36):
            refill(k, act, p0 + n)
            if n >= 13:
                act.wait_ge(k.dve_emptied, tiles.base[0] + n)
                s = k.sig[:, n - 13, :]
                act.activation(s, s, ACT.Sigmoid)
        act.wait_ge(k.dve_emptied, tiles.base[0] + 36)
        s = k.sig[:, 23, :]
        act.activation(s, s, ACT.Sigmoid).then_inc(k.sig_made, 1)
        for j in range(4):
            act.wait_ge(k.s5_y, j + 1)
            act.activation(y[:, j, :], y[:, j, :], ACT.Gelu_apprx_tanh).then_inc(k.s5_gelu, 1)
        act.preload_act_table(ACT.Sigmoid)
        for j in range(4):
            act.wait_ge(k.tile_done, pg + j // 2 + 1)
            if j % 2 == 0:
                refill(k, act, pg + j // 2)
            act.activation(yg[:, j, :], ps[:, j, 0:SEQ], ACT.Sigmoid, bias=sm["b_glu"][:, j:j + 1]
                           ).then_inc(k.s5_sig, 1)
        for n in range(4):
            refill(k, act, po + n)
        silu_conv(k, act)

    @block.vector
    def _(dve):
        k.dve(dve.memset(k.xm[:, :, 0:3], 0.0))
        between_low(k, dve, e0, gain)
        between_rstd(k, dve, r)

        def empty(n):
            dve.wait_ge(k.tile_done, p0 + n + 1)
            b = ps[:, bank[n % 4], :]
            if n < 12:
                dst = k.u[:, n, :] if n < 4 else k.xm[:, n - 4, 3:3 + TOK]
                dve.tensor_tensor(dst, b[:, 0:TOK], k.rstd, ALU.mult).then_inc(k.dve_emptied, 1)
            else:
                dve.tensor_tensor(k.sig[:, n - 12, :], b[:, 0:SEQ], k.rstd[:, META:TOK], ALU.mult
                                  ).then_inc(k.dve_emptied, 1)

        for n in range(4):
            empty(n)
        for c in range(S5_C):
            b = c % 2
            br, bi = ps[:, 3, 0:TOK], ps[:, 4, 0:TOK]
            dve.wait_ge(k.s5_bu, c + 1)
            if c:
                dve.wait_ge(k.s5_h, c)
            k.dve(dve.tensor_tensor(t4[:, 0, :], br, ec[:, c, :], ALU.mult))
            k.dve(dve.tensor_tensor(t4[:, 1, :], bi, es[:, c, :], ALU.mult))
            k.dve(dve.tensor_tensor(t4[:, 2, :], bi, ec[:, c, :], ALU.mult))
            dve.tensor_tensor(t4[:, 3, :], br, es[:, c, :], ALU.mult).then_inc(k.s5_bu_used, 1)
            k.dve.settle(dve)
            dve.wait_ge(k.s5_bu_used, c + 1)
            k.dve(dve.tensor_tensor(v[:, 0, :], t4[:, 0, :], t4[:, 1, :], ALU.add))
            k.dve(dve.tensor_tensor(v[:, 1, :], t4[:, 2, :], t4[:, 3, :], ALU.subtract))
            empty(4 + 2 * c)
            k.dve.settle(dve)
            rr = k.s5_r[:, c:c + 1].to_broadcast([P, TOK])
            for i in range(2):
                k.dve(dve.tensor_tensor_scan(v[:, i, :], rr, v[:, i, :], 0.0, ALU.mult, ALU.add))
            k.dve.settle(dve)
            k.dve(dve.tensor_tensor(t4[:, 0, :], v[:, 0, :], ec[:, c, :], ALU.mult))
            k.dve(dve.tensor_tensor(t4[:, 1, :], v[:, 1, :], es[:, c, :], ALU.mult))
            k.dve(dve.tensor_tensor(t4[:, 2, :], v[:, 0, :], es[:, c, :], ALU.mult))
            k.dve(dve.tensor_tensor(t4[:, 3, :], v[:, 1, :], ec[:, c, :], ALU.mult))
            empty(5 + 2 * c)
            k.dve.settle(dve)
            if c >= 2:
                dve.wait_ge(k.s5_cu, c - 1)
            k.dve(dve.tensor_tensor(hh[:, b, 0, :], t4[:, 0, :], t4[:, 1, :], ALU.subtract))
            k.dve.settle(dve)
            dve.scalar_tensor_tensor(out=hh[:, b, 1, :], in0=t4[:, 2, :], scalar=-1.0, in1=t4[:, 3, :],
                                     op0=ALU.mult, op1=ALU.subtract).then_inc(k.s5_h, 1)
            if c == 0:
                k.dve(dve.reciprocal(k.rms_first, k.rms_first))
            if 1 <= c <= DC:
                g = sm["gains"][:, final * DC + c - 1:final * DC + c]
                xc = k.x[:, c - 1, META:TOK]
                dve.scalar_tensor_tensor(out=xc, in0=xc, scalar=g, in1=k.rms_first, op0=ALU.mult, op1=ALU.mult)
            if c % 4 == 3:
                j = c // 4
                dve.wait_ge(k.s5_cu, c + 1)
                dve.scalar_tensor_tensor(out=y[:, j, :], in0=k.u[:, j, META:TOK], scalar=sm["s5_d"][:, j:j + 1],
                                         in1=y_ps[j], op0=ALU.mult, op1=ALU.add).then_inc(k.s5_y, 1)
        dve.wait_ge(k.s5_h, S5_C)
        convolve(k, dve, 0)
        for j in range(4):
            dve.wait_ge(k.s5_gelu, j + 1)
            split(k, dve, j, y[:, j, :]).then_inc(k.s5_ys, 1)
        for c in range(1, 4):
            convolve(k, dve, c)
        dve.wait_ge(k.tile_done, pg + 2)
        for j in range(4):
            dve.wait_ge(k.s5_sig, j + 1)
            k.dve(dve.tensor_tensor(yg[:, j, :], yg[:, j, :], y[:, j, :], ALU.mult))
            k.dve.settle(dve)
            split(k, dve, j, yg[:, j, :]).then_inc(k.s5_yg, 1)
        dve.wait_ge(k.sig_made, 1)
        for n in range(8):
            if n % 2 == 0:
                convolve(k, dve, 4 + n // 2)
            dve.wait_ge(k.tile_done, po + n // 2 + 1)
            s = k.sig[:, 8 + n, :]
            dve.tensor_tensor(s, s, ps[:, n, 0:SEQ], ALU.mult)

    @block.tensor
    def _(pe):
        def tile(n):
            if n == 3:
                pe.wait_ge(k.var_made, 1)
                pe.wait_ge(k.rms_ready, r + 1)
            tiles.wait_free(pe, n)
            wait_packet(k, pe, p0 + n)
            t0, T = (0, TOK) if n < 12 else (META, SEQ)
            mm_packet(k, pe, p0 + n, ps[:, bank[n % 4], 0:T], t0, T).then_inc(k.tile_done, 1)

        def bu(c):
            j, lo = c // 4, 32 * (c % 4)
            if c:
                pe.wait_ge(k.s5_bu_used, c)
            pe.matmul(ps[:, 3, 0:TOK], bre[lo:lo + 32, j, :], k.u[lo:lo + 32, j, :], start=True, stop=True,
                      tile_position=(lo, 0))
            pe.matmul(ps[:, 4, 0:TOK], bim[lo:lo + 32, j, :], k.u[lo:lo + 32, j, :], start=True, stop=True,
                      tile_position=(lo, 0)).then_inc(k.s5_bu, 1)

        def cu(c):
            j, lo = c // 4, 32 * (c % 4)
            pe.wait_ge(k.s5_h, c + 1)
            for i, w in enumerate((cre, cim)):
                last = pe.matmul(y_ps[j][lo:lo + 32], w[:, c, :], hh[:, c % 2, i, META:TOK],
                                 start=(i == 0), stop=(i == 1), tile_position=(0, lo))
            last.then_inc(k.s5_cu, 1)

        pe.wait_ge(k.xl_ready, DC * (e0 + 1))
        tile(0)
        between_pe(k, pe, r)
        for n in range(1, 5):
            tile(n)
        tiles.wait_emptied(pe, 3)
        bu(0)
        for c in range(S5_C):
            tile(5 + 2 * c)
            if c:
                cu(c - 1)
            if 6 + 2 * c < 36:
                tile(6 + 2 * c)
            if c + 1 < S5_C:
                bu(c + 1)
        cu(S5_C - 1)
        pe.wait_ge(k.s5_ys, 4)
        pe.wait_ge(k.s5_bu_used, S5_C)
        tiles.wait_emptied(pe, 35)
        for n in range(2):
            wait_packet(k, pe, pg + n)
            for i in range(2):
                last = mm_packet(k, pe, pg + n, ps[:, 2 * n + i, 0:SEQ], kc=4, col=P * i)
            last.then_inc(k.tile_done, 1)
        pe.wait_ge(k.s5_yg, 4)
        pe.wait_ge(k.s5_sig, 4)
        pe.wait_ge(k.s5_y, 4)
        for n in range(4):
            wait_packet(k, pe, po + n)
            for i in range(2):
                last = mm_packet(k, pe, po + n, ps[:, 2 * n + i, 0:SEQ], kc=4, col=P * i)
            last.then_inc(k.tile_done, 1)

    all_end(k, block)
    k.arena.at = mark


def convolve(k, dve, c):
    cw = k.small["conv_w"].rearrange("p (c m) -> p c m", c=DC)
    xc = k.xc[:, c, :]
    k.dve(dve.tensor_scalar(xc, k.xm[:, c, 0:TOK], cw[:, c, 0:1], k.small["conv_b"][:, c:c + 1], ALU.mult, ALU.add))
    for j in range(1, 4):
        k.dve.settle(dve)
        i = dve.scalar_tensor_tensor(out=xc, in0=k.xm[:, c, j:j + TOK], scalar=cw[:, c, j:j + 1], in1=xc,
                                     op0=ALU.mult, op1=ALU.add)
        if j < 3:
            k.dve(i)
    i.then_inc(k.ml_conv, 1)


def silu_conv(k, act):
    act.preload_act_table(ACT.Silu)
    for c in range(DC):
        act.wait_ge(k.ml_conv, c + 1)
        act.activation(k.xc[:, c, :], k.xc[:, c, :], ACT.Silu).then_inc(k.ml_xc, 1)


def mlstm(k, block):
    ps, sm = k.ps, k.small
    mark = k.arena.at
    take = k.arena.take
    bd = take(3, DC, P)
    k.arena.at = k.xc_end
    xc = k.xc
    qkv = take(3, DC, TOK)
    vt = take(3, D)
    g8, gf = take(TOK), take(TOK)
    gi = g8
    az, cs, mx, bb = take(TOK), take(TOK), take(TOK), take(TOK)
    ccol = take(3, ML_H)
    over = bd.rearrange("p m c j -> p (m c j)")
    dm = over[:, 0:6 * SEQ].rearrange("p (b s t) -> p b s t", b=2, s=3)
    hz = over[:, 6 * SEQ:10 * SEQ].rearrange("p (b t) -> p b t", b=2)
    den = over[:, 10 * SEQ:12 * SEQ].rearrange("p (b t) -> p b t", b=2)
    old = k.small_all[:, SMALL["c_re"][0]:SMALL["b_im"][0] + SMALL["b_im"][1]]
    hsq = old[:, 0:4 * SEQ].rearrange("p (b t) -> p b t", b=2)
    em = old[:, 4 * SEQ:6 * SEQ].rearrange("p (b t) -> p b t", b=2)
    rms = old[:, 6 * SEQ:8 * SEQ].rearrange("p (b t) -> p b t", b=2)
    sT = dm
    w_if = sm["w_if"].rearrange("p (c m) -> p c m", c=24)
    spans = ((0, META), (META, P), (META + P, P))
    R = slice(0, ML_H)

    @block.scalar
    def _(act):
        for n in range(2 * DC):
            act.wait_ge(k.ml_qkv, n + 1)
            act.activation(qkv[:, n // DC, n % DC, :], ps[:, n % 4, 0:TOK], ACT.Copy).then_inc(k.act_emptied, 1)
        act.wait_ge(k.ml_gate, 1)
        act.activation(g8[0:2 * ML_H, :], ps[0:2 * ML_H, 4, 0:TOK], ACT.Identity, bias=k.b_if[:, :]).then_inc(k.ml_act, 1)
        act.wait_ge(k.ml_gf, 1)
        act.activation(gf[R, :], ps[R, 5, 0:TOK], ACT.Copy).then_inc(k.ml_act, 1)
        act.preload_act_table_set(EXP_AND_LN)
        act.wait_ge(k.ml_dve, 1)
        k.act(act.activation(az[R, :], az[R, :], ACT.Exp, scale=-1.0))
        k.act.settle(act)
        act.activation(az[R, :], az[R, :], ACT.Ln, bias=k.one_col[R, :]).then_inc(k.ml_act, 1)

        def decays(h):
            b = h % 2
            act.wait_ge(k.ml_mb, h + 1)
            if h >= 2:
                act.wait_ge(k.ml_den, h - 1)
            for s, (lo, n) in enumerate(spans):
                act.activation(dm[0:n, b, s, :], ps[0:n, b, 0:SEQ], ACT.Exp, bias=ccol[0:n, s, h:h + 1], scale=-1.0)
            act.activation(em[:, b, :], ps[:, b, SEQ:2 * SEQ], ACT.Exp, scale=-1.0).then_inc(k.ml_exp, 1)

        decays(0)
        decays(1)
        for h in range(ML_H):
            act.wait_ge(k.ml_hz, h + 1)
            if h >= 2:
                act.wait_ge(k.ml_ss, h - 1)
            act.activation(hsq[:, h % 2, :], hz[:, h % 2, :], ACT.Square).then_inc(k.ml_sq, 1)
            if h + 2 < ML_H:
                decays(h + 2)
            act.wait_ge(k.ml_ss, h + 1)
            act.activation(rms[:, h % 2, :], ps[:, 7, 0:SEQ], ACT.Sqrt, bias=k.eps, scale=1.0 / ML_D
                           ).then_inc(k.ml_rms, 1)

    @block.vector
    def _(dve):
        for m, name in enumerate(("wq", "wk", "wv")):
            for c in range(DC):
                w4 = sm[name][:, 4 * c:4 * c + 4]
                last = dve.tensor_tensor(bd[:, m, c, :].rearrange("p (n j) -> p n j", j=4), bcast(w4, 32),
                                         spread(k.block4, 4), ALU.mult)
            last.then_inc(k.ml_bd, 1)
        for c in range(DC):
            dve.wait_ge(k.ml_qkv, 2 * DC + c + 1)
            dve.tensor_copy(qkv[:, 2, c, :], ps[:, c % 4, 0:TOK]).then_inc(k.ml_vcopied, 1)
        for s, (lo, n) in enumerate(spans):
            for half in range(2):
                dve.wait_ge(k.ml_vt, 2 * s + half + 1)
                dve.tensor_copy(vt[0:n, s, half * 512:(half + 1) * 512], ps[0:n, 6 + half, :]).then_inc(k.ml_vtc, 1)
        dve.wait_ge(k.ml_act, 2)
        dve.scalar_tensor_tensor(out=az[R, :], in0=gf[R, :], scalar=-1.0, in1=gf[R, :], op0=ALU.mult, op1=ALU.max
                                 ).then_inc(k.ml_dve, 1)
        dve.wait_ge(k.ml_act, 3)
        k.dve(dve.scalar_tensor_tensor(out=gf[R, :], in0=gf[R, :], scalar=0.0, in1=az[R, :],
                                       op0=ALU.min, op1=ALU.subtract))
        k.dve.settle(dve)
        k.dve(dve.tensor_tensor_scan(bb[R, :], k.ones_row[R, 0:TOK], gf[R, :], 0.0, ALU.mult, ALU.add))
        k.dve.settle(dve)
        k.dve(dve.tensor_tensor(cs[R, :], gi[R, :], bb[R, :], ALU.subtract))
        k.dve.settle(dve)
        k.dve(dve.tensor_tensor_scan(mx[R, :], k.ones_row[R, 0:TOK], cs[R, :], 0.0, ALU.mult, ALU.max))
        k.dve.settle(dve)
        dve.tensor_tensor(bb[R, :], bb[R, :], mx[R, :], ALU.add).then_inc(k.ml_dve, 1)
        dve.wait_ge(k.ml_cc, 1)
        for s, (lo, n) in enumerate(spans):
            last = dve.tensor_copy(ccol[0:n, s, :], ps[0:n, 6, 16 * s:16 * s + ML_H])
        last.then_inc(k.ml_dve, 1)
        def weighted(h):
            b = h % 2
            dve.wait_ge(k.ml_exp, h + 1)
            k.dve(dve.tensor_scalar(dm[0:META, b, 0, :], dm[0:META, b, 0, :], 1.0, None, ALU.min))
            dd = dm[:, b, 1, 0:P]
            k.dve(dve.scalar_tensor_tensor(out=dd, in0=dd, scalar=1.0, in1=k.keep_ge, op0=ALU.min, op1=ALU.mult))
            dd = dm[:, b, 1, P:SEQ]
            k.dve(dve.tensor_scalar(dd, dd, 1.0, None, ALU.min))
            dd = dm[:, b, 2, P:SEQ]
            k.dve(dve.scalar_tensor_tensor(out=dd, in0=dd, scalar=1.0, in1=k.keep_ge, op0=ALU.min, op1=ALU.mult))
            dve.wait_ge(k.ml_s, h + 1)
            if h >= 2:
                dve.wait_ge(k.ml_num, h - 1)
            k.dve.settle(dve)
            sc = ML_D ** -0.5
            dve.scalar_tensor_tensor(out=sT[0:META, b, 0, :], in0=ps[0:META, 2, SEQ:2 * SEQ], scalar=sc,
                                     in1=dm[0:META, b, 0, :], op0=ALU.mult, op1=ALU.mult)
            dve.scalar_tensor_tensor(out=sT[:, b, 1, :], in0=ps[:, 2, 0:SEQ], scalar=sc,
                                     in1=dm[:, b, 1, :], op0=ALU.mult, op1=ALU.mult)
            dve.scalar_tensor_tensor(out=sT[:, b, 2, P:SEQ], in0=ps[:, 3, 0:P], scalar=sc,
                                     in1=dm[:, b, 2, P:SEQ], op0=ALU.mult, op1=ALU.mult).then_inc(k.ml_sT, 1)

        def divided(h):
            b = h % 2
            dve.wait_ge(k.ml_num, h + 1)
            k.dve(dve.scalar_tensor_tensor(out=den[:, b, :], in0=ps[:, 6, 0:SEQ], scalar=-1.0, in1=em[:, b, :],
                                           op0=ALU.mult, op1=ALU.max))
            k.dve.settle(dve)
            dve.tensor_tensor(den[:, b, :], ps[:, 6, 0:SEQ], den[:, b, :], ALU.max).then_inc(k.ml_den, 1)
            dve.wait_ge(k.ml_den, h + 1)
            k.dve(dve.reciprocal(den[:, b, :], den[:, b, :]))
            k.dve.settle(dve)
            hv = hz[:, b, :].rearrange("p (e t) -> p e t", e=2)
            k.dve(dve.tensor_tensor(hv, k.sig[:, 2 * h:2 * h + 2, :], bcast(den[:, b, :], 2), ALU.mult))
            k.dve.settle(dve)
            dve.tensor_tensor(hz[:, b, :], ps[:, 4 + b, :], hz[:, b, :], ALU.mult).then_inc(k.ml_hz, 1)

        def normed(h):
            b = h % 2
            dve.wait_ge(k.ml_hz, h + 1)
            dve.wait_ge(k.ml_rms, h + 1)
            k.dve(dve.reciprocal(rms[:, b, :], rms[:, b, :]))
            k.dve.settle(dve)
            for e in range(2):
                c = 2 * h + e
                he = hz[:, b, e * SEQ:(e + 1) * SEQ]
                k.dve(dve.scalar_tensor_tensor(out=he, in0=he, scalar=sm["ml_g"][:, c:c + 1], in1=rms[:, b, :],
                                               op0=ALU.mult, op1=ALU.mult))
                k.dve.settle(dve)
                k.dve(dve.scalar_tensor_tensor(out=k.sig[:, c, :], in0=xc[:, c, META:TOK],
                                               scalar=sm["ml_skip"][:, c:c + 1], in1=he,
                                               op0=ALU.mult, op1=ALU.add))
                k.dve.settle(dve)
                split(k, dve, c, k.sig[:, c, :]).then_inc(k.mix_ready, 1)

        weighted(0)
        for h in range(ML_H):
            if h + 1 < ML_H:
                weighted(h + 1)
            divided(h)
            if h:
                normed(h - 1)
        normed(ML_H - 1)

    @block.tensor
    def _(pe):
        for n in range(3 * DC):
            m, c = n // DC, n % DC
            if c == 0:
                pe.wait_ge(k.ml_bd, m + 1)
            if m < 2:
                pe.wait_ge(k.ml_xc, c + 1)
            if 4 <= n < 2 * DC + 4:
                pe.wait_ge(k.act_emptied, k.act_tiles + n - 3)
            elif n >= 4:
                pe.wait_ge(k.ml_vcopied, n - 3 - 2 * DC)
            src = xc[:, c, :] if m < 2 else k.xm[:, c, 3:3 + TOK]
            pe.matmul(ps[:, n % 4, 0:TOK], bd[:, m, c, :], src, start=True, stop=True).then_inc(k.ml_qkv, 1)
        for s, (lo, n) in enumerate(spans):
            for half in range(2):
                if s:
                    pe.wait_ge(k.ml_vtc, 2 * s + half - 1)
                for c in range(4 * half, 4 * half + 4):
                    last = pe.matmul(ps[0:n, 6 + half, (c % 4) * P:(c % 4 + 1) * P], k.xm[:, c, 3 + lo:3 + lo + n],
                                     bd[:, 2, c, :], start=True, stop=True)
                last.then_inc(k.ml_vt, 1)
        pe.wait_ge(k.ml_vcopied, DC)
        pe.wait_ge(k.act_emptied, k.act_tiles + 2 * DC)
        for c in range(24):
            last = pe.matmul(ps[0:2 * ML_H, 4, 0:TOK], w_if[:, c, :], qkv[:, c // DC, c % DC, :],
                             start=(c == 0), stop=(c == 23))
        last.then_inc(k.ml_gate, 1)
        pe.wait_ge(k.ml_act, 1)
        pe.matmul(ps[R, 5, 0:TOK], k.ident[0:2 * ML_H, ML_H:2 * ML_H], g8[0:2 * ML_H, :], start=True, stop=True
                  ).then_inc(k.ml_gf, 1)
        pe.wait_ge(k.ml_dve, 2)
        pe.wait_ge(k.ml_vtc, 6)
        for s, (lo, n) in enumerate(spans):
            last = pe.matmul(ps[0:n, 6, 16 * s:16 * s + ML_H], cs[R, lo:lo + n], k.ident[R, R], start=True, stop=True)
        last.then_inc(k.ml_cc, 1)
        pe.wait_ge(k.ml_dve, 3)
        pe.wait_ge(k.ml_act, 3)

        def stab(h):
            if h >= 2:
                pe.wait_ge(k.ml_exp, h - 1)
            hr = k.head_row[R, h, :]
            pe.matmul(ps[:, h % 2, 0:SEQ], hr, mx[R, META:TOK], start=True, stop=True)
            pe.matmul(ps[:, h % 2, SEQ:2 * SEQ], hr, bb[R, META:TOK], start=True, stop=True).then_inc(k.ml_mb, 1)

        def scores(h):
            q = lambda e, lo, hi: qkv[:, 0, 2 * h + e, lo:hi]
            kk = lambda e, s: qkv[:, 1, 2 * h + e, spans[s][0]:spans[s][0] + spans[s][1]]
            if h >= 1:
                pe.wait_ge(k.ml_sT, h)
            for e in range(2):
                pe.matmul(ps[:, 2, 0:SEQ], kk(e, 1), q(e, META, TOK), start=(e == 0), stop=(e == 1))
            for e in range(2):
                pe.matmul(ps[0:META, 2, SEQ:2 * SEQ], kk(e, 0), q(e, META, TOK), start=(e == 0), stop=(e == 1))
            for e in range(2):
                last = pe.matmul(ps[:, 3, 0:P], kk(e, 2), q(e, META + P, TOK), start=(e == 0), stop=(e == 1))
            last.then_inc(k.ml_s, 1)

        def outputs(h):
            b = h % 2
            pe.wait_ge(k.ml_sT, h + 1)
            if h >= 1:
                pe.wait_ge(k.ml_hz, h)
            for e in range(2):
                o = ps[:, 4 + b, e * SEQ:(e + 1) * SEQ]
                v = lambda s: vt[0:spans[s][1], s, h * ML_D + e * P:h * ML_D + (e + 1) * P]
                pe.matmul(o, v(1), sT[:, b, 1, :], start=True, stop=False, skip_group_check=True)
                pe.matmul(o, v(0), sT[0:META, b, 0, :], start=False, stop=False, skip_group_check=True)
                pe.matmul(o[:, P:SEQ], v(2), sT[:, b, 2, P:SEQ], start=False, stop=True, skip_group_check=True)
            o = ps[:, 6, 0:SEQ]
            pe.matmul(o, k.ones, sT[:, b, 1, :], start=True, stop=False, skip_group_check=True)
            pe.matmul(o, k.ones[0:META, :], sT[0:META, b, 0, :], start=False, stop=False, skip_group_check=True)
            pe.matmul(o[:, P:SEQ], k.ones, sT[:, b, 2, P:SEQ], start=False, stop=True, skip_group_check=True
                      ).then_inc(k.ml_num, 1)

        def squares(h):
            pe.wait_ge(k.ml_sq, h + 1)
            if h >= 1:
                pe.wait_ge(k.ml_rms, h)
            for e in range(2):
                last = pe.matmul(ps[:, 7, 0:SEQ], k.ones, hsq[:, h % 2, e * SEQ:(e + 1) * SEQ], start=(e == 0), stop=(e == 1))
            last.then_inc(k.ml_ss, 1)

        stab(0)
        stab(1)
        scores(0)
        for h in range(ML_H):
            if h + 1 < ML_H:
                scores(h + 1)
            outputs(h)
            if h + 2 < ML_H:
                stab(h + 2)
            squares(h)

    k.act_tiles += 2 * DC
    k.mixes += 2 * ML_H
    all_end(k, block)
    k.arena.at = mark


def mix_out(k, block):
    tiles = Tiles(k, ["D"] * 8)
    packet = AT["ml_out"]
    ps = k.ps

    @block.tensor
    def _(pe):
        for n in range(8):
            tiles.wait_free(pe, n)
            wait_packet(k, pe, packet + n)
            mm_packet(k, pe, packet + n, ps[:, n % 4, 0:SEQ]).then_inc(k.tile_done, 1)

    @block.scalar
    def _(act):
        for n in range(8):
            refill(k, act, packet + n)

    @block.vector
    def _(dve):
        for n in range(8):
            dve.wait_ge(k.tile_done, packet + n + 1)
            g, s = k.sig[:, 16 + n, :], k.sig[:, 8 + n, :]
            dve.tensor_tensor(g, g, ps[:, n % 4, 0:SEQ], ALU.mult).then_inc(k.dve_emptied, 1)
        dve.wait_ge(k.dve_emptied, tiles.base[0] + 8)
        k.dve(dve.tensor_tensor(k.sig[:, 8:16, :], k.sig[:, 8:16, :], k.sig[:, 16:24, :], ALU.add))
        k.dve.settle(dve)
        for c in range(DC):
            split(k, dve, c, k.sig[:, 8 + c, :]).then_inc(k.mix_ready, 1)

    k.mixes += DC
    add_projection(k, block, AT["w_out"], k.mix_ready, k.mixes)


def peer(k, block, gain, ins, out):
    ps, sm = k.ps, k.small
    x = k.x[:, :, META:TOK]
    r, e0, cq = k.norms, k.early, k.columns
    k.norms += 1
    k.early += 1
    k.columns += 1
    take = k.arena.take
    NS = PE_SLOTS
    turns = HK // NS
    rows_at = k.arena.at
    k.sq = take(DC, TOK)
    qT, keys = take(16, SEQ), take(16, PE_N)
    rows = k.arena.t[:, rows_at:rows_at + NS * D].rearrange("p (s m) -> p s m", s=NS)
    k.arena.at = max(k.arena.at, rows_at + NS * D)
    sc1, sc0 = take(16, P), take(16, P)
    sc = (sc0, sc1)
    acc = sc0.rearrange("p a b -> p (a b)").rearrange("p (t m) -> p t m", t=2)
    xt, ht, gain_all = k.raw[:, 0:2, :], k.raw[:, 2:4, :], k.raw[:, 4:6, :]
    wk, cand = take(4, 256), take(4, 256)
    val, idx, idf = take(16, PE_K), take(16, PE_K).bitcast(U32), take(16, PE_K)
    cv, ci = take(PE_H, PE_K), take(PE_H, PE_K).bitcast(U32)
    v16, i16 = take(2, PE_K), take(2, PE_K).bitcast(U32)
    ab, abf, sel = take(2, HK).bitcast(U32), take(2, HK), take(2, HK)
    one = take(HK, PE_K)
    gain_rows = one.rearrange("p a b -> p (a b)")[0:1, :]
    nm = take(PE_H)
    expert = take(4 * HK + NS).bitcast(U32)
    gate, acts = take(2, HK), take(2, HK)
    ids = take(2, NS).bitcast(U32)
    dots, w8 = take(2, NS), take(NS)
    ssq, rms = take(2), take(2)
    p0 = AT["peer_q"]
    tiles = Tiles(k, ["A"] * 16)
    hp = lambda a: a.rearrange("p h k -> p (h k)")

    @block.scalar
    def _(act):
        act.dma_start(gain_rows, ins["rows"]).then_inc(k.rows_in, 16)
        act.dma_start(keys, ins["keys"]).then_inc(k.keys_in, 16)
        norm_act(k, act, None, x, gain)
        columns_act(k, act, cq)

        def scores(n):
            act.wait_ge(k.pr_s, n + 1)
            act.activation(sc[n % 2][:, 4 * (n // 2):4 * (n // 2) + 4, :], ps[:, 4 + n % 4, :].rearrange("p (a b) -> p a b", a=4),
                           ACT.Copy, scale=k.rcol[:, n % 2:n % 2 + 1]).then_inc(k.pr_sc, 1)

        for n in range(16):
            refill(k, act, p0 + n)
            act.wait_ge(k.tile_done, p0 + n + 1)
            act.activation(qT[:, n, :], ps[:, n % 4, 0:SEQ], ACT.Copy).then_inc(k.act_emptied, 1)
            if n == 0:
                act.wait_ge(k.pr_rcol, 1)
            if n >= 5 and n % 4 == 1:
                scores((n - 5) // 2)
                scores((n - 5) // 2 + 1)
        scores(6)
        scores(7)
        act.wait_ge(k.lo_done, PACKETS)
        for n in range(4):
            act.wait_ge(k.pr_t, n + 1)
            act.activation(xt[:, n // 2, (n % 2) * 512:(n % 2 + 1) * 512], ps[:, n, :], ACT.Copy).then_inc(k.pr_tc, 1)
        for i in range(2):
            act.wait_ge(k.pr_gl, i + 1)
            act.activation(gain_all[:, i, :].rearrange("p (a b) -> p a b", a=2), ps[:, 2 * i:2 * i + 2, :], ACT.Copy
                           ).then_inc(k.pr_ga, 1)

        def exponentials(t):
            act.wait_ge(k.pr_g, t + 1)
            act.activation(gate[:, t, :], gate[:, t, :], ACT.Exp).then_inc(k.pr_e, 1)

        def gelu(t):
            act.preload_act_table(ACT.Gelu_apprx_tanh)
            act.wait_ge(k.px_dots, turns * (t + 1))
            act.activation(acts[:, t, :], acts[:, t, :], ACT.Gelu_apprx_tanh).then_inc(k.px_gelu, 1)

        def finish(t):
            act.wait_ge(k.px_acc, t + 1)
            k.act(act.activation(ht[:, t, :], acc[:, t, :], ACT.Square, accum_out=ssq[:, t:t + 1]))
            k.act.settle(act)
            act.activation(rms[:, t:t + 1], ssq[:, t:t + 1], ACT.Sqrt, bias=k.eps, scale=1.0 / D).then_inc(k.px_rms, 1)
            act.wait_ge(k.px_out, t + 1)
            act.dma_start(out[t * P:(t + 1) * P, :], acc[:, t, :]).then_inc(k.stored, 16)

        exponentials(0)
        gelu(0)
        exponentials(1)
        finish(0)
        gelu(1)
        finish(1)
        act.wait_ge(k.stored, 32)

    @block.tensor
    def _(pe):
        def scores(j):
            for t in range(2):
                n = 2 * j + t
                if n >= 4:
                    pe.wait_ge(k.pr_sc, n - 3)
                for i in range(4):
                    hi = 4 * j + i
                    last = pe.matmul(ps[:, 4 + n % 4, i * P:(i + 1) * P], qT[:, hi, t * P:(t + 1) * P], keys[:, hi, :],
                                     start=True, stop=True)
                last.then_inc(k.pr_s, 1)

        pe.wait_ge(k.xl_ready, DC * (e0 + 1))
        for n in range(16):
            tiles.wait_free(pe, n)
            wait_packet(k, pe, p0 + n)
            mm_packet(k, pe, p0 + n, ps[:, n % 4, 0:SEQ]).then_inc(k.tile_done, 1)
            if n == 0:
                pe.wait_ge(k.sq_ready, 2 * r + 2)
                columns_pe(k, pe, cq)
            if n >= 4 and n % 4 == 0:
                if n == 4:
                    pe.wait_ge(k.col_rms, cq + 1)
                    pe.wait_ge(k.keys_in, 16)
                tiles.wait_emptied(pe, n - 1)
                scores(n // 4 - 1)
        tiles.wait_emptied(pe, 15)
        scores(3)
        for n in range(4):
            t, half = n // 2, n % 2
            for i in range(4):
                last = pe.transpose(ps[:, n, i * P:(i + 1) * P], x[:, 4 * half + i, t * P:(t + 1) * P], k.ident)
            last.then_inc(k.pr_t, 1)
        pe.wait_ge(k.rows_in, 16)
        for g in range(2):
            pe.wait_ge(k.pr_tc, 2 * g + 2)
            for i in range(2):
                last = pe.matmul(ps[:, 2 * g + i, :], k.ones[0:1, :], gain_rows[:, g * D + i * 512:g * D + (i + 1) * 512],
                                 start=True, stop=True)
            last.then_inc(k.pr_gl, 1)

    @block.gpsimd
    def _(pool):
        for ph in range(4):
            tab = (ins["u_tab"], ins["v_tab"])[ph % 2]
            with pool.Fori(0, turns // 2) as i:
                for half in range(2):
                    pool.wait_ge(k.px_ids, i * 2 + (turns * ph + half + 1))
                    for s in range(NS):
                        pool.wait_ge(k.px_free, i * (2 * NS) + (NS * (turns * ph + half) + s + 1))
                        pool.sem_inc(k.px_go, 1)
                        pool.indirect_dma_start(rows[:, s, :], None, tab,
                                                bass.IndirectOffsetOnAxis(ap=ids[:, half, s:s + 1], axis=0)
                                                ).then_inc(k.px_in[s], 16)

    @block.vector
    def _(dve):
        norm_low(k, dve, e0, x, gain)
        columns_dve(k, dve, cq, k.pr_rcol)
        k.dve(dve.memset(expert[:, 4 * HK:], 0))

        def run(i):
            k.dve(i)
            k.dve.settle(dve)

        def top16_steps(values, scratch, v, ix):
            return (lambda: dve.max(v[:, 0:8], values),
                    lambda: dve.max_index(ix[:, 0:8], v[:, 0:8], values),
                    lambda: dve.match_replace(scratch, v[:, 0:8], values, -3e38),
                    lambda: dve.max(v[:, 8:16], scratch),
                    lambda: dve.max_index(ix[:, 8:16], v[:, 8:16], scratch))

        def candidates(out, first, second):
            return dve.tensor_tensor(out.rearrange("p (a b) -> p a b", a=16), spread(first, 16), bcast(second, 16), ALU.add)

        def together(lists):
            for step in zip(*lists):
                for s in step:
                    k.dve(s())
                k.dve.settle(dve)

        def choose(t):
            g = gate[:, t, :].rearrange("p (h k) -> p h k", h=PE_H)
            f2 = idf.rearrange("p (h i) k -> p h i k", i=2)
            one4 = one.rearrange("p (h a) b -> p h a b", h=PE_H)

            def apart():
                dve.tensor_tensor(g, cv, cv[:, :, 0:1].to_broadcast([P, PE_H, PE_K]), ALU.subtract).then_inc(k.pr_g, 1)

            def picked(i, h):
                return lambda: k.dve(dve.tensor_tensor(one4[:, h:h + 4], one4[:, h:h + 4],
                                                       f2[:, h:h + 4, i, :].unsqueeze(2).to_broadcast([P, 4, 16, 16]), ALU.mult))

            def summed():
                dve.wait_ge(k.pr_e, t + 1)
                k.dve(dve.tensor_reduce(nm, g, AX_X, ALU.add))

            yield apart
            yield lambda: k.dve(dve.tensor_copy(idf, idx))
            yield lambda: k.dve(dve.tensor_scalar(ab[:, 0, :], hp(ci), 4, None, ALU.logical_shift_right))
            yield lambda: k.dve(dve.tensor_scalar(ab[:, 1, :], hp(ci), 15, None, ALU.bitwise_and))
            yield lambda: k.dve(dve.tensor_copy(abf, ab))
            for i in range(2):
                for lo in (0, HK // 2):
                    yield lambda i=i, lo=lo: k.dve(dve.tensor_tensor(
                        one[:, lo:lo + HK // 2, :], spread(abf[:, i, lo:lo + HK // 2], 16),
                        bcast(k.iota16[:, 0, :], HK // 2), ALU.is_equal))
                for h in (0, 4):
                    yield picked(i, h)
                for lo in (0, HK // 2):
                    yield lambda i=i, lo=lo: k.dve(dve.tensor_reduce(
                        sel[:, i, lo:lo + HK // 2], one[:, lo:lo + HK // 2, :], AX_X, ALU.add))
            yield lambda: k.dve(dve.scalar_tensor_tensor(out=sel[:, 0, :], in0=sel[:, 0, :], scalar=float(PE_N),
                                                         in1=sel[:, 1, :], op0=ALU.mult, op1=ALU.add))
            for ph in (2 * t, 2 * t + 1):
                yield lambda ph=ph: k.dve(dve.tensor_copy(expert[:, ph * HK:(ph + 1) * HK], sel[:, 0, :]))
            yield lambda: k.dve(dve.scalar_tensor_tensor(out=ht[:, t, :], in0=xt[:, t, :], scalar=k.rcol[:, t:t + 1],
                                                         in1=gain_all[:, 0, :], op0=ALU.mult, op1=ALU.mult))
            yield summed
            yield lambda: k.dve(dve.reciprocal(nm, nm))
            yield lambda: k.dve(dve.tensor_tensor(g, g, spread(nm, PE_K), ALU.mult))

        for j in range(4):
            dve.wait_ge(k.pr_sc, 2 * j + 1)
            together([top16_steps(sc0[:, n, :], wk[:, n % 4, 0:P], val[:, n, :], idx[:, n, :])
                      for n in range(4 * j, 4 * j + 4)])
            for h in (2 * j, 2 * j + 1):
                k.dve(candidates(cand[:, h % 2, :], val[:, 2 * h, :], val[:, 2 * h + 1, :]))
            k.dve.settle(dve)
            together([top16_steps(cand[:, h % 2, :], wk[:, h % 2, :], cv[:, h, :], ci[:, h, :])
                      for h in (2 * j, 2 * j + 1)])
        dve.wait_ge(k.pr_ga, 2)
        for step in choose(0):
            step()
            k.dve.settle(dve)

        dve.wait_ge(k.pr_sc, 8)
        for s in range(NS):
            dve.memset(dots[:, 0, s:s + 1], 0.0).then_inc(k.px_free, 1)
        dve.tensor_copy(ids[:, 0, :], expert[:, 0:NS]).then_inc(k.px_ids, 1)
        dve.memset(dots[:, 1, 0:1], 0.0).then_inc(k.px_route, 1)
        flat = lambda a: a.rearrange("p a b -> p (a b)")

        def sub_key(n):
            here = cand[:, 0, 0:P]
            return (lambda: dve.tensor_copy(here, flat(sc1)[:, bass.ds(n * PE_N, PE_N)]),
                    *top16_steps(here, wk[:, 0, 0:P], v16[:, 0, :], i16[:, 0, :]),
                    lambda: dve.tensor_copy(flat(val)[:, bass.ds(n * PE_K, PE_K)], v16[:, 0, :]),
                    lambda: dve.tensor_copy(flat(idx)[:, bass.ds(n * PE_K, PE_K)], i16[:, 0, :]))

        def head(h):
            return (lambda: candidates(cand[:, 0, :], flat(val)[:, bass.ds(h * (2 * PE_K), PE_K)],
                                       flat(val)[:, bass.ds(h * (2 * PE_K) + PE_K, PE_K)]),
                    *top16_steps(cand[:, 0, :], wk[:, 0, :], v16[:, 0, :], i16[:, 0, :]),
                    lambda: dve.tensor_copy(flat(cv)[:, bass.ds(h * PE_K, PE_K)], v16[:, 0, :]),
                    lambda: dve.tensor_copy(flat(ci)[:, bass.ds(h * PE_K, PE_K)], i16[:, 0, :]))

        def turn(ph, i, half, beside=None, done=0, plain=()):
            t, for_v = ph // 2, ph % 2
            used = lambda n: i * (2 * NS) + (NS * (turns * ph + half + 1) + n)
            steps = beside(i * 2 + half) if beside else ()
            dve.tensor_copy(ids[:, 1 - half, :], expert[:, bass.ds(i * (2 * NS) + (ph * HK + (half + 1) * NS), NS)]
                            ).then_inc(k.px_ids, 1)
            if for_v:
                dve.tensor_copy(w8, acts[:, t, bass.ds(i * (2 * NS) + half * NS, NS)]).then_inc(k.px_w, 1)
                dve.wait_ge(k.px_w, i * 2 + (t * turns + half + 1))
            for s in range(NS):
                dve.wait_ge(k.px_in[s], i * 32 + 16 * (ph * turns + half + 1))
                if for_v:
                    if s:
                        dve.wait_ge(k.px_free, used(s))
                    dve.scalar_tensor_tensor(out=acc[:, t, :], in0=rows[:, s, :], scalar=w8[:, s:s + 1],
                                             in1=acc[:, t, :], op0=ALU.mult, op1=ALU.add
                                             ).then_inc(k.px_free, 1)
                else:
                    dve.tensor_tensor_reduce(rows[:, s, :], rows[:, s, :], ht[:, t, :], 1.0, 0.0, ALU.mult, ALU.add,
                                             dots[:, half, s:s + 1]).then_inc(k.px_free, 1)
                if steps:
                    dve.wait_ge(k.px_route, i * (2 * NS) + (done + NS * half + s + 1))
                    dve.sem_inc(k.px_step, 1)
                    steps[s]().then_inc(k.px_route, 1)
                for step in plain[s:s + 1]:
                    k.dve.settle(dve)
                    step()
            dve.wait_ge(k.px_free, used(NS))
            if not for_v:
                dve.tensor_copy(acts[:, t, bass.ds(i * (2 * NS) + half * NS, NS)], dots[:, half, :]).then_inc(k.px_dots, 1)

        def phase(ph, first, last, **kw):
            with dve.Fori(first, last) as i:
                for half in range(2):
                    turn(ph, i, half, **kw)

        def weights(t):
            dve.wait_ge(k.px_gelu, t + 1)
            k.dve(dve.tensor_tensor(acts[:, t, :], acts[:, t, :], gate[:, t, :], ALU.mult))
            k.dve(dve.memset(acc[:, t, :], 0.0))
            k.dve.settle(dve)

        def residual(t):
            dve.tensor_tensor(acc[:, t, :], acc[:, t, :], xt[:, t, :], ALU.add).then_inc(k.px_acc, 1)

        def finish(t):
            dve.wait_ge(k.px_rms, t + 1)
            run(dve.reciprocal(rms[:, t:t + 1], rms[:, t:t + 1]))
            dve.scalar_tensor_tensor(out=acc[:, t, :], in0=acc[:, t, :], scalar=rms[:, t:t + 1],
                                     in1=gain_all[:, 1, :], op0=ALU.mult, op1=ALU.mult).then_inc(k.px_out, 1)

        n = turns // 2
        phase(0, 0, n, beside=sub_key)
        weights(0)
        phase(1, 0, PE_H // 2, beside=head, done=NS * 16)
        dve.wait_ge(k.px_route, NS * (16 + PE_H) + 1)
        steps = list(choose(1))
        long = -(-len(steps) // (2 * NS))
        for i in range(PE_H // 2, PE_H // 2 + long):
            for half in range(2):
                at = ((i - PE_H // 2) * 2 + half) * NS
                turn(1, i, half, plain=steps[at:at + NS])
        k.dve.settle(dve)
        phase(1, PE_H // 2 + long, n)
        residual(0)
        for half in range(2):
            turn(2, 0, half)
        finish(0)
        phase(2, 1, n)
        weights(1)
        phase(3, 0, n)
        residual(1)
        finish(1)


class Shared:
    pass


def name_semaphores(k, sem):
    (k.lo_done, k.tile_done, k.hi_done, k.xh_ready, k.sq_ready, k.ss_ready, k.rms_ready,
     k.xl_ready, k.col_ss, k.col_rms, k.dve_emptied, k.act_emptied, k.x_in, k.consts_made,
     k.small_in, k.gate_ready, k.silu_ready, k.h_made, k.h_high, k.h_ready, k.x_added,
     k.mix_ready, k.gains_made, k.eps_part, k.var_made, k.sig_made, k.rows_in, k.keys_in,
     k.stored) = (
        sem(n) for n in """lo_done tile_done hi_done xh_ready sq_ready ss_ready rms_ready xl_ready col_ss
        col_rms dve_emptied act_emptied x_in consts_made small_in gate_ready
        silu_ready h_made h_high h_ready x_added mix_ready gains_made eps_part
        var_made sig_made rows_in keys_in stored""".split())
    (k.gla_dve, k.gla_act, k.gla_o, k.gla_sq, k.gla_s, k.gla_ss, k.gla_rms, k.gla_silu,
     k.gla_wlr, k.gla_pe, k.gla_lr, k.gla_qk, k.gla_st, k.gla_copied) = (
        sem(n) for n in """gla_dve gla_act gla_o gla_sq gla_s gla_ss gla_rms gla_silu gla_wlr gla_pe gla_lr
        gla_qk gla_st gla_copied""".split())
    (k.sb_z, k.sb_sp, k.sb_ln, k.sb_log, k.sb_av, k.sb_exp, k.sb_w) = (
        sem(n) for n in """sb_z sb_sp sb_ln sb_log sb_av sb_exp sb_w""".split())
    (k.s5_act, k.s5_er, k.s5_th, k.s5_h, k.s5_y, k.s5_gelu, k.s5_sig, k.s5_bu, k.s5_bu_used,
     k.s5_cu, k.s5_ys, k.s5_yg) = (
        sem(n) for n in """s5_act s5_er s5_th s5_h s5_y s5_gelu s5_sig s5_bu s5_bu_used s5_cu s5_ys s5_yg""".split())
    (k.ml_conv, k.ml_xc, k.ml_qkv, k.ml_gate, k.ml_act, k.ml_gf, k.ml_dve, k.ml_mb, k.ml_den,
     k.ml_exp, k.ml_hz, k.ml_ss, k.ml_s, k.ml_sq, k.ml_rms, k.ml_bd, k.ml_vcopied, k.ml_vt,
     k.ml_vtc, k.ml_cc, k.ml_num, k.ml_sT) = (
        sem(n) for n in """ml_conv ml_xc ml_qkv ml_gate ml_act ml_gf ml_dve ml_mb ml_den ml_exp ml_hz ml_ss
        ml_s ml_sq ml_rms ml_bd ml_vcopied ml_vt ml_vtc ml_cc ml_num ml_sT""".split())
    (k.pr_s, k.pr_sc, k.pr_rcol, k.pr_t, k.pr_tc, k.pr_gl, k.pr_g, k.pr_ga, k.pr_e) = (
        sem(n) for n in """pr_s pr_sc pr_rcol pr_t pr_tc pr_gl pr_g pr_ga pr_e""".split())
    (k.px_dots, k.px_gelu, k.px_acc, k.px_rms, k.px_out, k.px_ids, k.px_free, k.px_go,
     k.px_route, k.px_w, k.px_step) = (
        sem(n) for n in """px_dots px_gelu px_acc px_rms px_out px_ids px_free px_go px_route px_w px_step""".split())


def build_program(nc, ins, out, upto=99, probe=None):
    with ExitStack() as ctx:
        k = Shared()
        name_semaphores(k, lambda n: ctx.enter_context(nc.semaphore(n)))
        width = 32700
        k.arena = Arena(ctx.enter_context(nc.sbuf_tensor("arena", [P, width], F32)), width)
        k.raw = ctx.enter_context(nc.sbuf_tensor("raw", [P, RAW, D], F32))
        k.split = ctx.enter_context(nc.sbuf_tensor("split", [P, SPLIT, 2, D], F32R))
        k.xs = ctx.enter_context(nc.sbuf_tensor("xs", [P, 2, DC, TOK], F32R))
        k.h = ctx.enter_context(nc.sbuf_tensor("h", [P, 2, 2, SEQ], F32R))
        k.ps = ctx.enter_context(nc.psum_tensor("ps", [P, 8, 512], F32))
        k.zero_bf = ctx.enter_context(nc.sbuf_tensor("zero_bf", [P, 512], BF16))[:, :]
        k.w_gk2 = ctx.enter_context(nc.sbuf_tensor("w_gk2_sb", [GLA_RANK, GLA_H * P], F32))
        k.b_if = ctx.enter_context(nc.sbuf_tensor("b_if_sb", [2 * ML_H, 1], F32))
        k.landed = [ctx.enter_context(nc.semaphore(f"landed{s}")) for s in range(RAW)]
        k.px_in = [ctx.enter_context(nc.semaphore(f"px_in{s}")) for s in range(PE_SLOTS)]
        k.stage_sem = {e: ctx.enter_context(nc.semaphore(f"stage_{e}")) for e in ("pe", "act", "dve")}
        k.stage = {e: 0 for e in k.stage_sem}
        k.dve = Counted(ctx.enter_context(nc.semaphore("dve_steps")))
        k.act = Counted(ctx.enter_context(nc.semaphore("act_steps")))
        k.pool = Counted(ctx.enter_context(nc.semaphore("pool_steps")))
        k.x_made = [None] * DC
        k.norms = k.early = k.columns = k.mixes = k.dve_tiles = k.act_tiles = 0

        take = k.arena.take
        k.x = take(DC, TOK)
        k.small_all = take(SMALL_W)
        k.small = {n: k.small_all[:, a:a + w] for n, (a, w) in SMALL.items()}
        k.rms, k.rstd, k.rcol = take(TOK), take(TOK), take(2)
        k.ones, k.neg_ones, k.ident = take(P), take(P), take(P)
        k.keep_ge, k.keep_gt, k.neg_tri = take(P), take(P), take(P)
        k.head_row, k.block4 = take(ML_H, P)[0:ML_H], take(32)
        k.iota16 = take(16, 16)
        k.eps, k.eps_eps, k.one_col, k.both_gains = take(1), take(1), take(1), take(DC)
        k.ones_row = take(TOK)
        k.s5_r, k.s5_sin, k.s5_cos, k.s5_cre, k.s5_cim = (take(S5_C) for _ in range(5))
        k.s5_dt, k.s5_ere, k.s5_theta, k.s5_half = (take(S5_C) for _ in range(4))
        k.s5_tmp = [take(S5_C) for _ in range(6)]
        g = SMALL["gains"][1]
        k.first_loads = [(k.x[:, :, META:TOK], ins["xT"]), (k.small_all[:, 0:g], ins["small"][:, 0:g])]
        k.small_loads = [
            (k.small_all[:, g:], ins["small"][:, g:]),
            (k.x[:, :, 0:META], ins["metaT"]),
            (k.w_gk2[:, :], ins["w_gk2"]),
            (k.b_if[:, :], ins["b_if"]),
        ]
        low = k.arena.at
        k.sq = take(DC, TOK)
        k.gate_t, k.gate_s = take(2, SEQ), take(2, SEQ)
        shared = k.arena.at

        block = ctx.enter_context(nc.Block())
        weights_in(k, block, ins["wstream"])
        setup(k, block)
        low_parts(k, block, 0, PACKETS)
        feed_forward(k, block, 0, GAIN["ffn1_0"], AT["ffn0"])
        if upto >= 2:
            gated_linear_attention(k, block, GAIN["mix_0"])
        if upto >= 3:
            feed_forward(k, block, 1, GAIN["ffn2_0"], AT["ffn1"])
        k.arena.at = shared
        k.s5_ec, k.s5_es = take(S5_C, TOK), take(S5_C, TOK)
        tables = k.arena.at
        k.rms_first = k.gate_t[:, 0, :]
        k.s5_big = [take(S5_C, P) for _ in range(2)]
        if upto >= 4:
            feed_forward(k, block, 2, GAIN["ffn1_1"], AT["ffn2"])
            stick_breaking(k, block, GAIN["mix_1"])
        if upto >= 5:
            feed_forward(k, block, 3, GAIN["ffn2_1"], AT["ffn3"])
        top = width - 4 * TOK - DC * (TOK + 3) - 24 * SEQ
        k.arena.at = top
        if upto >= 6:
            k.u, k.xm = take(4, TOK), take(DC, TOK + 3)
            k.sig = take(24, SEQ)
            k.arena.at = shared
            k.xc = take(DC, TOK)
            k.xc_end = k.arena.at
            k.arena.at, k.arena.width = tables, top
            input_and_states(k, block, GAIN["final"], GAIN["norm1"])
        if upto >= 7:
            k.arena.at, k.arena.width = low, top + 4 * TOK
            mlstm(k, block)
            k.arena.width = width
        if upto >= 8:
            mix_out(k, block)
        if upto >= 9:
            k.arena.at = low
            peer(k, block, GAIN["norm2"], ins, out)
        else:
            all_end(k, block)
            probe(k, block)




def lay_out(a):
    a = {n: np.asarray(v) for n, v in a.items()}

    def columns(w, width=P):
        kc = w.shape[0] // P
        w = w.reshape(kc, P, w.shape[1] // width, width).transpose(2, 1, 0, 3)
        return w.reshape(-1, P, kc * width)

    def feed(gate, up, down):
        g, u, d = columns(gate), columns(up), down.reshape(FT, P, D)
        order = [g[0], u[0], g[1], u[1], d[0]]
        for f in range(2, FT):
            order += [g[f], u[f], d[f - 1]]
        return order + [d[FT - 1]]

    def wide(w):
        w = w.reshape(4, 2, P, w.shape[1] // 512, 512).transpose(3, 0, 2, 1, 4)
        return w.reshape(-1, P, D)

    gla_in = a["gla_w_in"][0]
    sb_in = a["sb_w_in"][0]
    ffn = lambda n, i: feed(a[f"{n}_w_gate"][i], a[f"{n}_w_up"][i], a[f"{n}_w_down"][i])
    cols = 2 * GLA_H * GLA_K + 2 * D
    keys = a["peer_sub_keys_2"][0].reshape(16, PE_N, P).transpose(2, 0, 1)
    parts = [
        ffn("ffn1", 0), columns(gla_in[:, :D]), wide(gla_in[:, D:2 * D]), columns(gla_in[:, 2 * D:cols]), columns(a["gla_w_out"][0]), ffn("ffn2", 0),
        ffn("ffn1", 1), columns(sb_in[:, :2 * D]), wide(sb_in[:, 2 * D:]), columns(a["sb_w_out"][0]), ffn("ffn2", 1),
        columns(a["w_in_2"][0]), columns(a["ssm_w_glu_2"][0], 256), columns(a["w_ssm_out_2"][0], 256),
        columns(a["w_ml_out_2"][0]), columns(a["w_out_2"][0]), columns(a["peer_w_q_2"][0]),
    ]
    wstream = np.concatenate([np.stack(p) if isinstance(p, list) else p for p in parts])
    assert wstream.shape == (PACKETS, P, D)

    feat = lambda v: v.reshape(-1, P).T
    gains = np.concatenate([feat(v) for v in (
        a["ffn1_norm"][0], a["mix_norm"][0], a["ffn2_norm"][0], a["ffn1_norm"][1], a["mix_norm"][1],
        a["ffn2_norm"][1], a["final_norm"], a["norm1_g_2"][0], a["norm2_g_2"][0], a["final_norm_g_2"])], 1)

    def c_blocks(c):
        o = np.zeros((2, 64, S5_C, 2, 16), c.dtype)
        c = c.reshape(S5_C, 2, 16, 64)
        for g in range(2):
            o[g, :, :, g, :] = c[:, g].transpose(2, 0, 1)
        return o.reshape(P, -1)

    def b_blocks(b):
        o = np.zeros((4, 2, 16, 4, 2, 64), b.dtype)
        b = b.reshape(4, 4, 2, 64, 16)
        for g in range(2):
            o[:, g, :, :, g, :] = b[:, :, g].transpose(1, 3, 0, 2)
        return o.reshape(P, -1)

    chunks = lambda w: w.reshape(-1, P, w.shape[-1]).transpose(1, 0, 2).reshape(P, -1)
    small = {
        "gains": gains, "b_gk": feat(a["gla_b_gk"][0]), "o_norm": feat(a["gla_o_norm"][0]),
        "w_lr": chunks(gla_in[:, cols:]),
        "a_re": feat(a["ssm_a_re_2"][0].ravel()), "a_im": feat(a["ssm_a_im_2"][0].ravel()),
        "log_dt": feat(np.repeat(a["ssm_log_dt_2"][0], 64)), "s5_d": feat(a["ssm_d_2"][0]),
        "b_glu": feat(a["ssm_b_glu_2"][0]),
        "c_re": c_blocks(a["ssm_c_re_2"][0]), "c_im": c_blocks(a["ssm_c_im_2"][0]),
        "b_re": b_blocks(a["ssm_b_re_2"][0]), "b_im": b_blocks(a["ssm_b_im_2"][0]),
        "conv_w": chunks(a["ml_conv_w_2"][0].T), "conv_b": feat(a["ml_conv_b_2"][0]),
        "wq": chunks(a["ml_wq_2"][0].reshape(D, 4)), "wk": chunks(a["ml_wk_2"][0].reshape(D, 4)),
        "wv": chunks(a["ml_wv_2"][0].reshape(D, 4)),
        "w_if": chunks(a["ml_w_if_2"][0]),
        "ml_g": feat(a["ml_norm_g_2"][0]), "ml_skip": feat(a["ml_skip_2"][0]),
    }
    for n, (_, w) in SMALL.items():
        assert small[n].shape == (P, w), (n, small[n].shape, w)
    tokens = lambda v: v.T.reshape(DC, P, -1).transpose(1, 0, 2)
    return {
        "wstream": wstream,
        "small": np.concatenate([small[n] for n in SMALL], 1),
        "xT": tokens(a["x"][0]), "metaT": tokens(a["meta_tokens_2"]),
        "w_gk2": a["gla_w_gk2"][0], "b_if": a["ml_b_if_2"][0].reshape(2 * ML_H, 1),
        "keys": keys, "rows": np.concatenate([a["norm2_g_2"][0], a["final_norm_g_2"]]).reshape(1, 2 * D),
        "u_tab": a["peer_u_2"][0], "v_tab": a["peer_v_2"][0],
    }


def kernel(**inputs):
    import concourse.bacc as bacc
    from concourse.bass_utils import run_bass_kernel_spmd

    arrays = {n: np.ascontiguousarray(v) for n, v in lay_out(inputs).items()}
    nc = bacc.Bacc("TRN2", target_bir_lowering=False, num_devices=1)
    ins = {n: nc.dram_tensor(n, v.shape, mybir.dt.from_np(v.dtype), kind="ExternalInput").ap()
           for n, v in arrays.items()}
    out = nc.dram_tensor("out", (SEQ, D), F32, kind="ExternalOutput").ap()
    build_program(nc, ins, out)
    r = run_bass_kernel_spmd(nc, [arrays], core_ids=[0])
    return r.results[0]["out"].reshape(1, SEQ, D)
```
